# Optimizing a Trainium2 kernel written in Bass

```python
import math
import jax
import jax.numpy as jnp
from jax import lax
import numpy as np

D_MODEL = 1024
BATCH = 1
SEQ = 1024
DEPTH = 1
DEC_BATCH = 8
DEC_SEQ = 1
PAST_LEN = 2048
PAGE_SIZE = 128

GLA_HEADS = 4
GLA_DK = D_MODEL // 2 // GLA_HEADS
GLA_DV = D_MODEL // GLA_HEADS
GLA_RANK = 16
GLA_TAU = 16.0
GLA_CHUNK = 64
ATT_GROUPS = ((128, 1), (512, 4), (2048, 16))
N_GROUPS = 3
ATT_HEADS = 4
ATT_HD = 128
ATT_BLOCK = 128
ROPE_DIM = ATT_HD // 4
ROPE_THETA = 500000.0
PEER_HEADS = 8
PEER_NKEYS = 128
PEER_NEXPERTS = PEER_NKEYS * PEER_NKEYS
PEER_DQ = 128
PEER_TOPK = 16
PEER_BLOCK = 128
NORM_EPS = 1e-6

W_QA = GLA_HEADS * GLA_DK
W_VA = GLA_HEADS * GLA_DV
W_QB = N_GROUPS * ATT_HEADS * ATT_HD
W_OB = ATT_HEADS * ATT_HD
IN_WIDTHS = (W_QA, W_QA, W_VA, W_VA, GLA_RANK, W_QB, W_QB, W_QB, D_MODEL, D_MODEL)
IN_TOTAL = 2 * W_QA + 2 * W_VA + GLA_RANK + 3 * W_QB + 2 * D_MODEL

kernel_name = 'hybrid_gla_dilated_peer_step'

def rms_norm(x, g):
    xf = x.astype(jnp.float32)
    y = xf * lax.rsqrt(jnp.mean(xf * xf, axis=-1, keepdims=True) + NORM_EPS)
    return (y * g.astype(jnp.float32)).astype(x.dtype)

def partial_rope(x, pos):
    half = ROPE_DIM // 2
    inv_freq = ROPE_THETA ** (-jnp.arange(half, dtype=jnp.float32) / half)
    ang = pos.astype(jnp.float32)[:, None] * inv_freq[None, :]
    cos = jnp.cos(ang)[:, None, :]
    sin = jnp.sin(ang)[:, None, :]
    xr = x[..., :ROPE_DIM].astype(jnp.float32)
    x1, x2 = xr[..., :half], xr[..., half:]
    rot = jnp.concatenate([x1 * cos - x2 * sin, x2 * cos + x1 * sin], axis=-1)
    return jnp.concatenate([rot.astype(x.dtype), x[..., ROPE_DIM:]], axis=-1)

def gla_chunked(q, k, v, la, s0):
    n, l, h, dk = q.shape
    dv = v.shape[-1]
    c = min(GLA_CHUNK, l)
    lp = -(-l // c) * c

    def to_chunks(t):
        t = jnp.pad(t.astype(jnp.float32), ((0, 0), (0, lp - l), (0, 0), (0, 0)))
        return t.reshape(n, lp // c, c, h, t.shape[-1]).transpose(1, 0, 3, 2, 4)

    causal = jnp.tril(jnp.ones((c, c), dtype=bool))[:, :, None]

    def step(s, xs):
        qc, kc, vc, lc = xs
        b = jnp.cumsum(lc, axis=2)
        inter = jnp.einsum('nhtk,nhkv->nhtv', qc * jnp.exp(b), s)
        diff = b[:, :, :, None, :] - b[:, :, None, :, :]
        decay = jnp.exp(jnp.where(causal, diff, -jnp.inf))
        att = jnp.einsum('nhtk,nhsk,nhtsk->nhts', qc, kc, decay)
        o = inter + jnp.einsum('nhts,nhsv->nhtv', att, vc)
        b_last = b[:, :, -1:, :]
        s = jnp.exp(b_last[:, :, 0, :])[..., None] * s + jnp.einsum('nhsk,nhsv->nhkv', kc * jnp.exp(b_last - b), vc)
        return s, o

    s_fin, o = lax.scan(step, s0.astype(jnp.float32), (to_chunks(q), to_chunks(k), to_chunks(v), to_chunks(la)))
    o = o.transpose(1, 0, 3, 2, 4).reshape(n, lp, h, dv)[:, :l]
    return o, s_fin

def band_attention(q, k, v, steps):
    n, l, h, d = q.shape
    blk = ATT_BLOCK
    lp = -(-l // blk) * blk
    nb = lp // blk

    def blocks(t):
        return jnp.pad(t, ((0, 0), (0, lp - l), (0, 0), (0, 0))).reshape(n, nb, blk, h, d)

    def two_blocks(t):
        tb = blocks(t)
        prev = jnp.pad(tb, ((0, 0), (1, 0), (0, 0), (0, 0), (0, 0)))[:, :-1]
        return jnp.concatenate([prev, tb], axis=2)

    qb, kb, vb = blocks(q), two_blocks(k), two_blocks(v)
    s = jnp.einsum('nbqhd,nbkhd->nbhqk', qb, kb, preferred_element_type=jnp.float32) * (d ** -0.5)
    qi = jnp.arange(blk)[:, None]
    ki = jnp.arange(2 * blk)[None, :]
    dist = blk + qi - ki
    band = (dist >= 0) & (dist <= steps)
    valid = (jnp.arange(nb)[:, None, None] > 0) | (ki >= blk)[None]
    mask = band[None] & valid
    s = jnp.where(mask[None, :, None], s, -jnp.inf)
    lse = jax.nn.logsumexp(s, axis=-1)
    p = jnp.exp(s - lse[..., None])
    o = jnp.einsum('nbhqk,nbkhd->nbqhd', p, vb.astype(jnp.float32)).reshape(n, lp, h, d)[:, :l]
    lse = lse.transpose(0, 1, 3, 2).reshape(n, lp, h)[:, :l]
    return o, lse

def dilated_prompt(q, k, v, window, dil):
    b, l, h, d = q.shape

    def split(t):
        return t.reshape(b, l // dil, dil, h, d).transpose(0, 2, 1, 3, 4).reshape(b * dil, l // dil, h, d)

    o, lse = band_attention(split(q), split(k), split(v), window // dil)
    o = o.reshape(b, dil, l // dil, h, d).transpose(0, 2, 1, 3, 4).reshape(b, l, h, d)
    lse = lse.reshape(b, dil, l // dil, h).transpose(0, 2, 1, 3).reshape(b, l, h)
    return o, lse

def dilated_step(q, kv_new, buf, window, dil):
    kv = jnp.concatenate([buf, kv_new.astype(buf.dtype)], axis=1)
    wb = buf.shape[1]
    t = q.shape[1]
    idx = wb + jnp.arange(t)[:, None] - dil * jnp.arange(window // dil + 1)[None, :]
    valid = idx >= 0
    g = kv[:, jnp.maximum(idx, 0)]
    s = jnp.einsum('nthd,ntkhd->nthk', q, g[:, :, :, 0], preferred_element_type=jnp.float32) * (q.shape[-1] ** -0.5)
    s = jnp.where(valid[None, :, None, :], s, -jnp.inf)
    lse = jax.nn.logsumexp(s, axis=-1)
    p = jnp.exp(s - lse[..., None])
    o = jnp.einsum('nthk,ntkhd->nthd', p, g[:, :, :, 1].astype(jnp.float32))
    keep = min(window, wb + t)
    return o, lse, kv[:, wb + t - keep:]

def peer_ffn(h, w_q, k1, k2, u, v):
    t, d = h.shape
    q = (h @ w_q).reshape(t, PEER_HEADS, 2, PEER_DQ // 2).astype(jnp.float32)
    s1 = jnp.einsum('thd,nd->thn', q[:, :, 0], k1.astype(jnp.float32))
    s2 = jnp.einsum('thd,nd->thn', q[:, :, 1], k2.astype(jnp.float32))
    v1, i1 = lax.top_k(s1, PEER_TOPK)
    v2, i2 = lax.top_k(s2, PEER_TOPK)
    cand = (v1[..., :, None] + v2[..., None, :]).reshape(t, PEER_HEADS, PEER_TOPK * PEER_TOPK)
    sc, ci = lax.top_k(cand, PEER_TOPK)
    e = (jnp.take_along_axis(i1, ci // PEER_TOPK, axis=-1) * PEER_NKEYS
         + jnp.take_along_axis(i2, ci % PEER_TOPK, axis=-1))
    gate = jax.nn.softmax(sc, axis=-1)
    blk = min(PEER_BLOCK, t)
    tp = -(-t // blk) * blk
    nb = tp // blk
    hp = jnp.pad(h, ((0, tp - t), (0, 0))).reshape(nb, blk, d)
    ep = jnp.pad(e, ((0, tp - t), (0, 0), (0, 0))).reshape(nb, blk, PEER_HEADS, PEER_TOPK)
    gp = jnp.pad(gate, ((0, tp - t), (0, 0), (0, 0))).reshape(nb, blk, PEER_HEADS, PEER_TOPK)

    def one_block(args):
        hb, eb, gb = args
        a = jax.nn.gelu(jnp.einsum('td,thkd->thk', hb, u[eb], preferred_element_type=jnp.float32))
        return jnp.einsum('thk,thkd->td', (gb * a).astype(v.dtype), v[eb])

    out = lax.map(one_block, (hp, ep, gp))
    return out.reshape(tp, d)[:t].astype(h.dtype)

def decoder_layer(x, c, pos, gla_s0, att_bufs, ada_w, ada_b, norm1_g, w_in, gla_a_w2, gla_a_b, gla_gn_g,
                  w_branch_a, w_branch_b, w_out, norm2_g, peer_wq, peer_k1, peer_k2, peer_u, peer_v):
    n, l, d = x.shape
    mod = jax.nn.silu(c) @ ada_w + ada_b
    sh1, sc1, g1, sh2, sc2, g2 = jnp.split(mod[:, None, :], 6, axis=-1)
    h = rms_norm(x, norm1_g) * (1 + sc1) + sh1
    z = h @ w_in
    points = [int(p) for p in np.cumsum(IN_WIDTHS)[:-1]]
    qa, ka, va, ra, alr, qb, kb, vb, gza, gzb = jnp.split(z, points, axis=-1)

    la = jax.nn.log_sigmoid((alr @ gla_a_w2 + gla_a_b).astype(jnp.float32)) / GLA_TAU
    o_a, s_a = gla_chunked(qa.reshape(n, l, GLA_HEADS, GLA_DK) * (GLA_DK ** -0.5),
                           ka.reshape(n, l, GLA_HEADS, GLA_DK),
                           va.reshape(n, l, GLA_HEADS, GLA_DV),
                           la.reshape(n, l, GLA_HEADS, GLA_DK), gla_s0)
    o_a = rms_norm(o_a, gla_gn_g.reshape(GLA_HEADS, GLA_DV)).reshape(n, l, W_VA)
    o_a = o_a.astype(x.dtype) * jax.nn.silu(ra)

    q_all = partial_rope(qb.reshape(n, l, N_GROUPS * ATT_HEADS, ATT_HD), pos)
    k_all = partial_rope(kb.reshape(n, l, N_GROUPS * ATT_HEADS, ATT_HD), pos)
    v_all = vb.reshape(n, l, N_GROUPS * ATT_HEADS, ATT_HD)
    outs, lses, new_bufs = [], [], []
    for gi in range(N_GROUPS):
        window, dil = ATT_GROUPS[gi]
        sl = slice(gi * ATT_HEADS, (gi + 1) * ATT_HEADS)
        q_g, k_g, v_g = q_all[:, :, sl], k_all[:, :, sl], v_all[:, :, sl]
        kv_g = jnp.stack([k_g, v_g], axis=2)
        if att_bufs is None:
            o_g, lse_g = dilated_prompt(q_g, k_g, v_g, window, dil)
            new_bufs.append(kv_g[:, l - min(window, l):])
        else:
            o_g, lse_g, buf_g = dilated_step(q_g, kv_g, att_bufs[gi], window, dil)
            new_bufs.append(buf_g)
        outs.append(o_g)
        lses.append(lse_g)
    wts = jax.nn.softmax(jnp.stack(lses, axis=0), axis=0)
    o_b = jnp.einsum('gnlh,gnlhd->nlhd', wts, jnp.stack(outs, axis=0)).reshape(n, l, W_OB).astype(x.dtype)

    merged = jax.nn.sigmoid(gza) * (o_a @ w_branch_a) + jax.nn.sigmoid(gzb) * (o_b @ w_branch_b)
    x = x + g1 * (merged @ w_out)

    h2 = rms_norm(x, norm2_g) * (1 + sc2) + sh2
    x = x + g2 * peer_ffn(h2.reshape(n * l, d), peer_wq, peer_k1, peer_k2, peer_u, peer_v).reshape(n, l, d)
    return x, s_a.astype(gla_s0.dtype), new_bufs

def setup_inputs(seed: int = 0) -> dict:
    key = jax.random.key(seed)
    ks = jax.random.split(key, 32)

    def nrm(k, shape, scale):
        return jax.random.normal(k, shape, jnp.float32) * scale

    def kv_shape(w):
        return (DEPTH, DEC_BATCH, min(w, PAST_LEN), 2, ATT_HEADS, ATT_HD)

    return {
        'x_prompt': nrm(ks[0], (BATCH, SEQ, D_MODEL), 1.0),
        'x_sample': nrm(ks[1], (DEC_BATCH, DEC_SEQ, D_MODEL), 1.0),
        'c_prompt': nrm(ks[2], (BATCH, D_MODEL), 1.0),
        'c_sample': nrm(ks[3], (DEC_BATCH, D_MODEL), 1.0),
        'state_gla': nrm(ks[4], (DEPTH, DEC_BATCH, GLA_HEADS, GLA_DK, GLA_DV), 0.3),
        'cache_kv_w128': nrm(ks[5], kv_shape(128), 1.0),
        'cache_kv_w512': nrm(ks[6], kv_shape(512), 1.0),
        'cache_kv_w2048': nrm(ks[7], kv_shape(2048), 1.0),
        'ada_w': nrm(ks[8], (DEPTH, D_MODEL, 6 * D_MODEL), 0.5 * D_MODEL ** -0.5),
        'ada_b': nrm(ks[9], (DEPTH, 6 * D_MODEL), 0.01),
        'norm1_g': 1.0 + nrm(ks[10], (DEPTH, D_MODEL), 0.05),
        'w_in': nrm(ks[11], (DEPTH, D_MODEL, IN_TOTAL), D_MODEL ** -0.5),
        'gla_a_w2': nrm(ks[12], (DEPTH, GLA_RANK, W_QA), GLA_RANK ** -0.5),
        'gla_a_b': nrm(ks[13], (DEPTH, W_QA), 0.1),
        'gla_gn_g': 1.0 + nrm(ks[14], (DEPTH, W_VA), 0.05),
        'w_branch_a': nrm(ks[15], (DEPTH, W_VA, D_MODEL), W_VA ** -0.5),
        'w_branch_b': nrm(ks[16], (DEPTH, W_OB, D_MODEL), W_OB ** -0.5),
        'w_out': nrm(ks[17], (DEPTH, D_MODEL, D_MODEL), D_MODEL ** -0.5),
        'norm2_g': 1.0 + nrm(ks[18], (DEPTH, D_MODEL), 0.05),
        'peer_wq': nrm(ks[19], (DEPTH, D_MODEL, PEER_HEADS * PEER_DQ), D_MODEL ** -0.5),
        'peer_k1': nrm(ks[20], (DEPTH, PEER_NKEYS, PEER_DQ // 2), (PEER_DQ // 2) ** -0.5),
        'peer_k2': nrm(ks[21], (DEPTH, PEER_NKEYS, PEER_DQ // 2), (PEER_DQ // 2) ** -0.5),
        'peer_u': nrm(ks[22], (DEPTH, PEER_NEXPERTS, D_MODEL), D_MODEL ** -0.5),
        'peer_v': nrm(ks[23], (DEPTH, PEER_NEXPERTS, D_MODEL), PEER_HEADS ** -0.5),
        'final_g': 1.0 + nrm(ks[24], (D_MODEL,), 0.05),
    }

def reference(x_prompt, x_sample, c_prompt, c_sample, state_gla, cache_kv_w128, cache_kv_w512, cache_kv_w2048,
              ada_w, ada_b, norm1_g, w_in, gla_a_w2, gla_a_b, gla_gn_g, w_branch_a, w_branch_b, w_out,
              norm2_g, peer_wq, peer_k1, peer_k2, peer_u, peer_v, final_g):
    n_p, l_p = x_prompt.shape[0], x_prompt.shape[1]
    l_s = x_sample.shape[1]
    pos_p = jnp.arange(l_p, dtype=jnp.int32)
    pos_s = PAST_LEN + jnp.arange(l_s, dtype=jnp.int32)
    s0_p = jnp.zeros((n_p, GLA_HEADS, GLA_DK, GLA_DV), state_gla.dtype)
    xp, xs = x_prompt, x_sample
    gla_p, gla_s = [], []
    kv_p = ([], [], [])
    kv_s = ([], [], [])
    for i in range(DEPTH):
        lw = (ada_w[i], ada_b[i], norm1_g[i], w_in[i], gla_a_w2[i], gla_a_b[i], gla_gn_g[i],
              w_branch_a[i], w_branch_b[i], w_out[i], norm2_g[i], peer_wq[i], peer_k1[i], peer_k2[i],
              peer_u[i], peer_v[i])
        xp, sp, bp = decoder_layer(xp, c_prompt, pos_p, s0_p, None, *lw)
        xs, ss, bs = decoder_layer(xs, c_sample, pos_s, state_gla[i],
                                   (cache_kv_w128[i], cache_kv_w512[i], cache_kv_w2048[i]), *lw)
        gla_p.append(sp)
        gla_s.append(ss)
        for g in range(N_GROUPS):
            kv_p[g].append(bp[g])
            kv_s[g].append(bs[g])
    y_prompt = rms_norm(xp, final_g)
    y_sample = rms_norm(xs, final_g)
    return (y_prompt, y_sample, jnp.stack(gla_p, 0), jnp.stack(gla_s, 0),
            jnp.stack(kv_p[0], 0), jnp.stack(kv_s[0], 0), jnp.stack(kv_p[1], 0), jnp.stack(kv_s[1], 0),
            jnp.stack(kv_p[2], 0), jnp.stack(kv_s[2], 0))


_drawn_inputs = setup_inputs


def setup_inputs(seed=0):
    import zlib

    import numpy as np

    out = dict(_drawn_inputs(seed))
    spreads = {}
    factors = {'gla_gn_g': 7.807, 'norm2_g': 4.038}
    for name, (base, spread) in spreads.items():
        noise = np.random.default_rng([zlib.crc32(name.encode()), seed]).standard_normal(out[name].shape)
        drawn = base * np.exp(spread * noise) if base else spread * noise
        out[name] = jnp.asarray(drawn.astype(out[name].dtype))
    for name, factor in factors.items():
        out[name] = (out[name] * factor).astype(out[name].dtype)
    return out
```

```python
from contextlib import ExitStack

import numpy as np
import concourse.bass as bass
from concourse import mybir
from concourse.alu_op_type import AluOpType as ALU

F32 = mybir.dt.float32
BF16 = mybir.dt.bfloat16
U32 = mybir.dt.uint32
ACT = mybir.ActivationFunctionType
AX = mybir.AxisListType

P = 128
D = 1024
KD = D // P
SEQ = 1024
TILES = SEQ // P
NS = 8
ROWS = SEQ + NS
PAST = 2048
GH, GK, GV = 4, 128, 256
GC = 64
RANK = 16
TAU = 16.0
GROUPS = ((128, 1), (512, 4), (2048, 16))
AH, HD = 4, 128
NG = len(GROUPS)
QH = NG * AH
ROT = HD // 4 // 2
THETA = 500000.0
PH, NK, DQ, TOPK = 8, 128, 128, 16
EPS = 1e-6
QA, KA = 0, GH * GK
VA = 2 * GH * GK
RA = VA + GH * GV
ALR = RA + GH * GV
QB = ALR + RANK
KB = QB + QH * HD
VB = KB + QH * HD
GZA = VB + QH * HD
GZB = GZA + D
INW = GZB + D
SCALE_A = GK ** -0.5
SCALE_B = HD ** -0.5
MASKED = -1e30


def at_least(eng, sem, value):
    if not isinstance(value, int) or value > 0:
        eng.wait_ge(sem, value)


def early(eng, value):
    if not isinstance(value, int):
        eng.compute_val(value)
    return value


def first_then_loop(eng, n, body):
    body(0)
    with eng.Fori(1, n) as i:
        body(i)


def chained(eng, sem, base=0):
    count = [0]

    def link(ins):
        count[0] += 1
        ins.then_inc(sem, 1)
        eng.wait_ge(sem, base + count[0])
    link.count = count
    return link


def constants():
    half = np.arange(ROT, dtype=np.float32)
    inv = np.power(np.float32(THETA), -half / np.float32(ROT)).astype(np.float32)
    pos = np.concatenate([np.arange(SEQ), np.full(NS, PAST)]).astype(np.float32)
    ang = (pos[:, None] * inv[None, :]).astype(np.float32)
    rope = np.concatenate([np.cos(ang), np.sin(ang)], axis=1).astype(np.float32)
    tq = np.arange(P)[:, None]

    def band(width, dil, ahead, n):
        dist = tq - (np.arange(n)[None, :] - ahead)
        ok = (dist >= 0) & (dist <= width) & (dist % dil == 0)
        return np.where(ok, 0.0, MASKED).astype(np.float32)

    masks = np.concatenate([band(2048, 16, 896, 1920), band(512, 4, 512, 1152), band(128, 1, 128, 384)], axis=1)
    s, t = np.arange(P)[:, None], np.arange(P)[None, :]
    causal = ((s <= t) & (s // GC == t // GC)).astype(np.float32)
    restart = np.ones((P, P), np.float32)
    restart[:, ::GC] = 0.0
    pick = np.zeros((P, P), np.float32)
    pick[:NS, :NS * NS] = (np.arange(NS)[:, None] == (np.arange(NS * NS) // NS)[None, :])
    pick[:, NS * NS:] = np.eye(NS, dtype=np.float32).reshape(1, NS * NS)
    slot = np.tile(np.arange(TOPK, dtype=np.float32)[None, :], (P, 1))
    misc = np.concatenate([np.eye(P, dtype=np.float32), causal, restart, pick, slot], axis=1)
    return {"rope": rope, "masks": masks, "misc": misc}


C_ID, C_CAUSAL, C_RESTART, C_PICK, C_SLOT = 0, 128, 256, 384, 512
C_W = 528


class Ctx:

    def __init__(self, nc, stack, ins, outs, consts):
        self.nc, self.stack = nc, stack
        self.i, self.o, self.c = ins, outs, consts
        self.phase_sems = []
        self.z = nc.dram_tensor("z_scratch", (ROWS, INW), F32).ap()
        self.mod = nc.dram_tensor("mod_scratch", (1 + NS, 6 * D), F32).ap()
        self.mix = nc.dram_tensor("mix_scratch", (ROWS, GH * GV + AH * HD), F32).ap()
        self.x1 = nc.dram_tensor("x1_scratch", (ROWS, D), F32).ap()
        self.h2 = nc.dram_tensor("h2_scratch", (ROWS, D), F32).ap()

    def sem(self, name, kept=False):
        handle = self.nc.alloc_semaphore(name)
        if not kept:
            self.phase_sems.append(handle)
        return handle

    def clear_sems(self):
        self.nc.clear_and_free_semaphores(self.phase_sems)
        self.nc.all_engine_barrier()
        self.phase_sems = []

    def phase(self):
        return Phase(self)


class Phase:

    def __init__(self, k):
        self.k, self.stack = k, ExitStack()

    def __enter__(self):
        return self

    def __exit__(self, *a):
        return self.stack.__exit__(*a)

    def sb(self, name, shape, dt=F32):
        return self.stack.enter_context(self.k.nc.sbuf_tensor(name, shape, dt))

    def ps(self, name, shape, dt=F32):
        return self.stack.enter_context(self.k.nc.psum_tensor(name, shape, dt))


def modulation(k, misc):
    nc = k.nc
    NB, U, W = 12, 3, 512
    M = 1 + NS
    c_in, w_in_ = k.sem("mod_c_loaded"), [k.sem(f"mod_w_loaded{u}") for u in range(U)]
    cachecopy = k.sem("cache_rows_copied", kept=True)
    act_s, silu_s, tps, tsb = k.sem("mod_exp_done"), k.sem("mod_silu_steps"), k.sem("mod_cT_psum"), k.sem("mod_cT_ready")
    prod, summed, stored = k.sem("mod_product"), k.sem("mod_summed"), k.sem("mod_stored")
    k.cachecopy = cachecopy
    with k.phase() as f:
        c9, e9, s9 = f.sb("c9", [M, D]), f.sb("e9", [M, D]), f.sb("s9", [M, D])
        cT = f.sb("cT", [P, KD, M])
        w = [f.sb(f"ada{u}", [P, KD, W]) for u in range(U)]
        bias, mod = f.sb("ada_bias", [M, 6 * D]), f.sb("mod_sb", [M, 6 * D])
        pT = f.ps("cT_ps", [P, KD, 16])
        pm = [f.ps(f"mod_ps{u}", [M, W]) for u in range(U)]
        wv = k.i["ada_w"][0].rearrange("(k p) n -> p k n", p=P)
        with nc.Block() as block:
            @block.sync
            def _(sp):
                sp.dma_start(c9[0:1, :], k.i["c_prompt"]).then_inc(c_in, 16)
                sp.dma_start(c9[1:M, :], k.i["c_sample"]).then_inc(c_in, 16)
                sp.dma_start(misc[:, :], k.c["misc"]).then_inc(c_in, 16)
                sp.dma_start(bias[:, :], k.i["ada_b"].to_broadcast([M, 6 * D])).then_inc(c_in, 16)

                def step(j):
                    for u in range(U):
                        at_least(sp, prod, j * U + u + 1 - U)
                        sp.dma_start(w[u][:, :, :], wv[:, :, bass.ds(j * (U * W) + u * W, W)]).then_inc(w_in_[u], 16)
                first_then_loop(sp, NB // U, step)
                sp.wait_ge(summed, NB)
                sp.dma_start(k.mod, mod[:, :]).then_inc(stored, 16)
                sp.wait_ge(stored, 16)

            @block.scalar
            def _(act):
                act.wait_ge(c_in, 64)
                nc.scalar.activation(e9[:, :], c9[:, :], ACT.Exp, scale=-1.0).then_inc(act_s, 1)

            @block.vector
            def _(dve):
                dve.wait_ge(act_s, 1)
                link = chained(dve, silu_s)
                link(nc.vector.tensor_scalar_add(e9[:, :], e9[:, :], 1.0))
                link(nc.vector.reciprocal(s9[:, :], e9[:, :]))
                link(nc.vector.tensor_tensor(s9[:, :], s9[:, :], c9[:, :], ALU.mult))
                dve.wait_ge(tps, 1)
                nc.vector.tensor_copy(cT[:, :, :], pT[:, :, 0:M]).then_inc(tsb, 1)

                def step(j):
                    for u in range(U):
                        dve.wait_ge(prod, j * U + u + 1)
                        cols = bass.ds(j * (U * W) + u * W, W)
                        nc.vector.tensor_tensor(mod[:, cols], pm[u][:, :], bias[:, cols], ALU.add).then_inc(summed, 1)
                first_then_loop(dve, NB // U, step)

            @block.tensor
            def _(pe):
                pe.wait_ge(silu_s, 3)
                for c in range(KD):
                    last = nc.tensor.transpose(pT[:, c, 0:M], s9[:, c * P:(c + 1) * P], misc[0:M, C_ID:C_ID + M])
                last.then_inc(tps, 1)
                pe.wait_ge(tsb, 1)

                def step(j):
                    for u in range(U):
                        pe.wait_ge(w_in_[u], 16 * j + 16)
                        at_least(pe, summed, j * U + u + 1 - U)
                        for c in range(KD):
                            last = nc.tensor.matmul(pm[u][:, :], cT[:, c, :], w[u][:, c, :], start=(c == 0), stop=(c == KD - 1))
                        last.then_inc(prod, 1)
                first_then_loop(pe, NB // U, step)


def norm_and_project(k, misc):
    nc = k.nc
    W, U = 464, 3
    STEPS = INW // W
    assert STEPS * W == INW and STEPS % U == 0
    x_in, sqs, steps, h_made, hps, hev = (k.sem("n1_" + n) for n in ("loaded", "squares", "steps", "h_made", "hT_psum", "hT_ready"))
    gm_s, root = k.sem("n1_gain_steps"), k.sem("n1_root")
    w_l = [k.sem(f"win_loaded{u}") for u in range(U)]
    prod, evac, used, zout = k.sem("z_product"), k.sem("z_evacuated"), k.sem("win_used"), [k.sem(f"z_stored{u}") for u in range(U)]
    with k.phase() as f:
        hT = f.sb("hT", [P, KD, ROWS])
        w = [f.sb(f"win{u}", [P, KD, W]) for u in range(U)]
        wv = k.i["w_in"][0].rearrange("(k p) n -> p k n", p=P)
        with k.phase() as f1:
            xs = f1.sb("x_rows", [P, TILES + 1, D])
            mods = f1.sb("n1_mod", [P, 2, 2, D])
            g = f1.sb("n1_g", [P, D])
            junk, h = f1.sb("n1_junk", [P, D]), f1.sb("n1_h", [P, D])
            ss, rs = f1.sb("n1_ss", [P, 1]), f1.sb("n1_rs", [P, 2])
            pT = f1.ps("hT_ps", [P, KD, P])
            with nc.Block() as block:
                @block.sync
                def _(sp):
                    sp.dma_start(mods[:, 0, :, :].rearrange("p a d -> p (a d)"), k.mod[0:1, 0:2 * D].to_broadcast([P, 2 * D])).then_inc(x_in, 16)
                    sp.dma_start(mods[0:NS, 1, :, :].rearrange("p a d -> p (a d)"), k.mod[1:1 + NS, 0:2 * D]).then_inc(x_in, 16)
                    sp.dma_start(g[:, :], k.i["norm1_g"].to_broadcast([P, D])).then_inc(x_in, 16)
                    sp.dma_start(xs[:, 0:TILES, :], k.i["x_prompt"][0].rearrange("(t p) d -> p t d", p=P)).then_inc(x_in, 16)
                    sp.dma_start(xs[0:NS, TILES, :], k.i["x_sample"][:, 0, :]).then_inc(x_in, 16)
                    for u in range(U):
                        sp.dma_start(w[u][:, :, :], wv[:, :, u * W:(u + 1) * W]).then_inc(w_l[u], 16)

                def rows_of(i):
                    return NS if isinstance(i, int) and i == TILES else P

                def all_tiles(eng, body):
                    first_then_loop(eng, TILES, body)
                    body(TILES)

                @block.scalar
                def _(act):
                    act.wait_ge(x_in, 80)

                    def tile(i):
                        R = rows_of(i)
                        at_least(act, h_made, i)
                        nc.scalar.activation(junk[0:R, :], xs[0:R, i, :], ACT.Square, accum_out=ss[0:R, :]).then_inc(sqs, 1)
                        act.wait_ge(steps, 3 * i + 2)
                        nc.scalar.activation(rs[0:R, 1:2], rs[0:R, 0:1], ACT.Sqrt).then_inc(root, 1)
                        act.wait_ge(hps, i + 1)
                        for b in range(2):
                            nc.scalar.copy(hT[:, 4 * b:4 * b + 4, bass.ds(i * P, R)], pT[:, 4 * b:4 * b + 4, 0:R]).then_inc(hev, 1)
                    all_tiles(act, tile)

                @block.vector
                def _(dve):
                    dve.wait_ge(x_in, 80)
                    for n, R in ((0, P), (1, NS)):
                        nc.vector.scalar_tensor_tensor(out=mods[0:R, n, 1, :], in0=mods[0:R, n, 1, :], scalar=1.0, in1=g[0:R, :],
                                                       op0=ALU.add, op1=ALU.mult).then_inc(gm_s, 1)
                    dve.wait_ge(gm_s, 2)

                    def tile(i):
                        R = rows_of(i)
                        n = 1 if R == NS else 0
                        dve.wait_ge(sqs, i + 1)
                        at_least(dve, hps, i)
                        link = chained(dve, steps, 3 * i)
                        link(nc.vector.tensor_scalar(rs[0:R, 0:1], ss[0:R, :], 1.0 / D, EPS, ALU.mult, ALU.add))
                        link(nc.vector.reciprocal(rs[0:R, 0:1], rs[0:R, 0:1]))
                        dve.wait_ge(root, i + 1)
                        link(nc.vector.scalar_tensor_tensor(out=h[0:R, :], in0=xs[0:R, i, :], scalar=rs[0:R, 1:2], in1=mods[0:R, n, 1, :],
                                                            op0=ALU.mult, op1=ALU.mult))
                        nc.vector.tensor_tensor(h[0:R, :], h[0:R, :], mods[0:R, n, 0, :], ALU.add).then_inc(h_made, 1)
                    all_tiles(dve, tile)

                @block.tensor
                def _(pe):
                    def tile(i):
                        R = rows_of(i)
                        pe.wait_ge(h_made, i + 1)
                        at_least(pe, hev, 2 * i)
                        for c in range(KD):
                            last = nc.tensor.transpose(pT[:, c, 0:R], h[0:R, c * P:(c + 1) * P], misc[0:R, C_ID:C_ID + R])
                        last.then_inc(hps, 1)
                    all_tiles(pe, tile)

        zst = [f.sb(f"z_stage{u}", [P, TILES + 1, W]) for u in range(U)]
        NBK = 3
        pz = [f.ps(f"z_ps{b}", [P, 512]) for b in range(NBK)]
        T1 = TILES + 1
        zp = k.z[0:SEQ, :].rearrange("(t p) n -> p t n", p=P)
        with nc.Block() as block:
            @block.sync
            def _(sp):
                for name, (width, _) in zip(("w128", "w512", "w2048"), GROUPS):
                    for n in range(NS):
                        src = k.i["cache_kv_" + name][0, n, 1:width].rearrange("w a h d -> (w a h d)")
                        dst = k.o["kv_" + name + "_sample"][0, n, 0:width - 1].rearrange("w a h d -> (w a h d)")
                        sp.dma_start(dst.rearrange("(p f) -> p f", p=16), src.rearrange("(p f) -> p f", p=16)).then_inc(k.cachecopy, 16)
                with sp.Fori(1, STEPS // U) as j:
                    for u in range(U):
                        sp.wait_ge(used, j * U + u + 1 - U)
                        sp.dma_start(w[u][:, :, :], wv[:, :, bass.ds(j * (U * W) + u * W, W)]).then_inc(w_l[u], 16)

            @block.scalar
            def _(act):
                def step(j):
                    for u in range(U):
                        at_least(act, zout[u], 32 * j)
                        for t in range(T1):
                            R = NS if t == TILES else P
                            act.wait_ge(prod, j * (U * T1) + u * T1 + t + 1)
                            nc.scalar.copy(zst[u][0:R, t, :], pz[t % NBK][0:R, 0:W]).then_inc(evac, 1)
                        act.wait_ge(evac, j * (U * T1) + (u + 1) * T1)
                        cols = bass.ds(j * (U * W) + u * W, W)
                        act.dma_start(zp[:, :, cols], zst[u][:, 0:TILES, :]).then_inc(zout[u], 16)
                        act.dma_start(k.z[SEQ:ROWS, cols], zst[u][0:NS, TILES, :]).then_inc(zout[u], 16)
                first_then_loop(act, STEPS // U, step)
                for u in range(U):
                    act.wait_ge(zout[u], 32 * (STEPS // U))

            @block.tensor
            def _(pe):
                def step(j):
                    for u in range(U):
                        pe.wait_ge(w_l[u], 16 * j + 16)
                        for t in range(T1):
                            R = NS if t == TILES else P
                            at_least(pe, evac, j * (U * T1) + u * T1 + t + 1 - NBK)
                            for c in range(KD):
                                last = nc.tensor.matmul(pz[t % NBK][0:R, 0:W], hT[:, c, t * P:t * P + R], w[u][:, c, :],
                                                        start=(c == 0), stop=(c == KD - 1))
                            last.then_inc(prod, 1)
                        nc.tensor.wait_ge(prod, j * (U * T1) + (u + 1) * T1)
                        pe.sem_inc(used, 1)
                first_then_loop(pe, STEPS // U, step)


def prompt_mixers(k, misc):
    nc = k.nc
    GW = GH * GV
    KT = TILES + 5 + 2
    NKEY = KT * P
    M1, M0 = 1920, 1920 + 1152
    s = {n: k.sem("mx_" + n) for n in (
        "const", "cast", "zg", "zq", "v", "init", "tr", "alr", "x", "xb", "ln", "ln_steps", "dec_steps", "exps", "qk", "gact", "gupd", "state",
        "squares", "var", "var_steps", "root", "normed", "silu_e", "silu_steps", "mixa", "rope_steps", "roped", "scores", "max_steps", "negmax", "exp",
        "pv", "rinv", "heads", "kout", "outa", "outb", "vout", "final")}
    full = [k.sem("mx_T_full0"), k.sem("mx_T_full1")]
    free = [k.sem("mx_T_free0"), k.sem("mx_T_free1")]
    USES = 12
    with k.phase() as f:
        masks = f.sb("mx_masks", [P, 3456], BF16)
        identb = f.sb("mx_ident", [P, P], BF16)
        ropes = f.sb("mx_rope", [P, TILES, 2 * ROT])
        w2, ab, gn = f.sb("mx_w2", [RANK, GH * GK]), f.sb("mx_ab", [P, GH]), f.sb("mx_gn", [P, GW])
        zg, zq = f.sb("mx_zg", [P, QB]), f.sb("mx_zq", [P, 2 * QH, HD])
        kT, V = f.sb("mx_kT", [P, QH, SEQ]), f.sb("mx_V", [P, TILES, QH * HD])
        qT = f.sb("mx_qT", [P, QH, P])
        alrT, xb, xa = f.sb("mx_alrT", [RANK, P]), f.sb("mx_xb", [P, GH * P]), f.sb("mx_xa", [P, GH * P])
        B, d1, dl = f.sb("mx_B", [P, GH * P]), f.sb("mx_d1", [P, GH * P]), f.sb("mx_dl", [P, GH * P])
        E = [f.sb("mx_E0", [P, GH * P]), d1, f.sb("mx_E2", [P, GH * P]), dl]
        EL = f.sb("mx_EL", [P, 2 * GH])
        kp, kpp = f.sb("mx_kp", [P, GH * P]), f.sb("mx_kpp", [P, GH * P])
        attm, kTok = f.sb("mx_attm", [P, GH, P]), f.sb("mx_kTok", [P, GH, P])
        S = [f.sb("mx_S0", [P, GH, GV]), f.sb("mx_S1", [P, GH, GV])]
        gst = f.sb("mx_gst", [P, 2, GH])
        er, om = f.sb("mx_er", [P, GW]), f.sb("mx_om", [P, GW])
        Pm = f.sb("mx_P", [P, NKEY])
        PT = [f.sb(f"mx_PT{n}", [P, KT, P]) for n in range(2)]
        rt = PT[1][:, :, :].rearrange("p j t -> p (j t)")[:, 0:4 * 2 * QH * ROT].rearrange("p (n h r) -> p n h r", n=4, h=2 * QH)
        mx, nm, sm, ri = (f.sb("mx_" + n, [P, AH]) for n in ("max", "negm", "sum", "rinv"))
        ob = f.sb("mx_ob", [P, AH * HD])
        big = f.ps("mx_big", [P, 4, 512])
        Tb = [f.ps("mx_T0", [P, 512]), f.ps("mx_T1", [P, 512])]
        OM = [f.ps("mx_O", [P, 512]), f.ps("mx_M", [P, 512])]
        sc_all = big[:, :, :].rearrange("p b n -> p (b n)")
        qps = big[:, 0, :]
        kps = big[:, 1, :]
        v8 = lambda t: t[:, :].rearrange("p (n c) -> p n c", c=GC)
        causal = misc[:, C_CAUSAL:C_CAUSAL + P]
        restart = misc[:, C_RESTART:C_RESTART + P]
        ident = misc[:, C_ID:C_ID + P]
        vg = zg[:, VA:VA + GW]
        ra = zg[:, RA:RA + GW]

        def tiles(eng, body):
            body(0, 0, 0, 0, 0, False)
            with eng.Fori(1, 4) as i:
                body(i, 0, 0 - i, i - 1, -1, False)
            with eng.Fori(4, TILES) as i:
                body(i, i - 4, -4, i - 1, -1, True)

        with nc.Block() as block:
            @block.gpsimd
            def _(pool):
                pool.dma_start(masks[:, :], k.c["masks"]).then_inc(s["cast"], 16)
                pool.dma_start(identb[:, :], k.c["misc"][:, C_ID:C_ID + P]).then_inc(s["cast"], 16)
                nc.gpsimd.memset(kT[:, :, :], 0.0).then_inc(s["init"], 1)
                nc.gpsimd.memset(S[0][:, :, :], 0.0).then_inc(s["init"], 1)

            @block.sync
            def _(sp):
                sp.dma_start(ropes[:, :, :], k.c["rope"][0:SEQ, :].rearrange("(t p) n -> p t n", p=P)).then_inc(s["const"], 16)
                sp.dma_start(w2[:, :], k.i["gla_a_w2"][0]).then_inc(s["const"], 16)
                with nc.allow_non_contiguous_dma(reason="512 single values, once"):
                    sp.dma_start(ab[:, :], k.i["gla_a_b"][0].rearrange("(h p) -> p h", p=P)).then_inc(s["const"], 16)
                sp.dma_start(gn[:, :], k.i["gla_gn_g"].to_broadcast([P, GW])).then_inc(s["const"], 16)

                def load_gla(rows):
                    sp.dma_start(zg[:, :], k.z[bass.ds(rows, P), 0:QB]).then_inc(s["zg"], 16)

                def load_qk(rows):
                    sp.dma_start(zq[:, :, :].rearrange("p h d -> p (h d)"), k.z[bass.ds(rows, P), QB:VB]).then_inc(s["zq"], 16)
                load_gla(0)
                load_qk(0)
                sp.dma_start(V[:, :, :], k.z[0:SEQ, VB:GZA].rearrange("(t p) n -> p t n", p=P)).then_inc(s["v"], 16)
                for g, name in enumerate(("w128", "w512", "w2048")):
                    o = k.o["kv_" + name + "_prompt"][0, 0]
                    W = o.shape[0]
                    sp.dma_start(o[:, 1, :, :].rearrange("t h d -> t (h d)"),
                                 k.z[SEQ - W:SEQ, VB + g * AH * HD:VB + (g + 1) * AH * HD]).then_inc(s["vout"], 16)

                def tile(i, st1, lag1, st0, lag0, late):
                    last = isinstance(i, int) and i == TILES - 1
                    one, rows, upds, turned = (early(sp, x) for x in (i + 1, i * P, 8 * i + 8, USES * i + 4))
                    next_rows, headed, keys_out = (early(sp, x) for x in (i * P + P, 4 * i + 4, 16 * (2 * i - 2) if late else 16 * (i + 1)))
                    old = early(sp, (i - 4) * P) if late else 0
                    sp.wait_ge(s["roped"], one)
                    sp.dma_start(k.o["kv_w2048_prompt"][0, 0, bass.ds(rows, P), 0, :, :], zq[:, QH + 8:QH + 12, :]).then_inc(s["kout"], 16)
                    if late:
                        sp.dma_start(k.o["kv_w512_prompt"][0, 0, bass.ds(old, P), 0, :, :], zq[:, QH + 4:QH + 8, :]).then_inc(s["kout"], 16)
                    sp.wait_ge(s["mixa"], one)
                    sp.dma_start(k.mix[bass.ds(rows, P), 0:GW], om[:, :]).then_inc(s["outa"], 16)
                    if not last:
                        sp.wait_ge(s["gupd"], upds)
                        load_gla(next_rows)
                        sp.wait_ge(full[0], turned)
                        sp.wait_ge(full[1], turned)
                        sp.wait_ge(s["kout"], keys_out)
                        load_qk(next_rows)
                    sp.wait_ge(s["heads"], headed)
                    sp.dma_start(k.mix[bass.ds(rows, P), GW:GW + AH * HD], ob[:, :]).then_inc(s["outb"], 16)
                tile(0, 0, 0, 0, 0, False)
                with sp.Fori(1, 4) as i:
                    tile(i, 0, 0 - i, i - 1, -1, False)
                with sp.Fori(4, TILES - 1) as i:
                    tile(i, i - 4, -4, i - 1, -1, True)
                tile(TILES - 1, 3, -4, 6, -1, True)
                sp.dma_start(k.o["kv_w128_prompt"][0, 0, :, 0, :, :], zq[:, QH:QH + 4, :]).then_inc(s["kout"], 16)
                sp.wait_ge(s["state"], 8 * TILES)
                sp.dma_start(k.o["state_prompt"][0, 0].rearrange("h k v -> k h v"), S[0][:, :, :]).then_inc(s["final"], 16)
                for name, n in (("final", 1), ("vout", 3), ("kout", 8 + 4 + 1), ("outa", TILES), ("outb", TILES)):
                    sp.wait_ge(s[name], 16 * n)

            @block.tensor
            def _(pe):
                pe.wait_ge(s["const"], 64)
                pe.wait_ge(s["cast"], 32)
                pe.wait_ge(s["init"], 2)
                pe.wait_ge(s["v"], 16)

                def tile(i, st1, lag1, st0, lag0, late):
                    pe.wait_ge(s["zg"], 16 * i + 16)
                    at_least(pe, s["exp"], 4 * i)
                    for h in range(GH):
                        nc.tensor.transpose(qps[:, h * P:(h + 1) * P], zg[:, QA + h * GK:QA + (h + 1) * GK], ident)
                        nc.tensor.transpose(kps[:, h * P:(h + 1) * P], zg[:, KA + h * GK:KA + (h + 1) * GK], ident)
                    at_least(pe, s["heads"], 4 * i)
                    nc.tensor.transpose(OM[0][0:RANK, 0:P], zg[:, ALR:ALR + RANK], ident).then_inc(s["tr"], 1)
                    pe.wait_ge(s["alr"], i + 1)
                    for h in range(GH):
                        last = nc.tensor.matmul(OM[1][:, h * P:(h + 1) * P], w2[:, h * GK:(h + 1) * GK], alrT[:, :], start=True, stop=True)
                    last.then_inc(s["x"], 1)
                    pe.wait_ge(s["qk"], 4 * i + 4)
                    at_least(pe, free[0], USES * i)
                    for h in range(GH):
                        last = nc.tensor.matmul(Tb[0][:, h * P:(h + 1) * P], kp[:, h * P:(h + 1) * P], E[0][:, h * P:(h + 1) * P], start=True, stop=True)
                    last.then_inc(full[0], 1)
                    at_least(pe, free[1], USES * i)
                    for h in range(GH):
                        last = nc.tensor.transpose(Tb[1][:, h * P:(h + 1) * P], kpp[:, h * P:(h + 1) * P], ident)
                    last.then_inc(full[1], 1)
                    pe.wait_ge(free[0], USES * i + 1)
                    pe.wait_ge(free[1], USES * i + 1)
                    upd = lambda h: OM[h // 2][:, (h % 2) * GV:(h % 2 + 1) * GV]
                    at_least(pe, s["state"], 8 * i)
                    for h in range(GH):
                        nc.tensor.matmul(big[:, h, 0:GV], attm[:, h, :], vg[:, h * GV:(h + 1) * GV], start=True, stop=False)
                        nc.tensor.matmul(big[0:GC, h, 0:GV], E[2][:, h * P:h * P + GC], S[0][:, h, :], start=False, stop=True)
                        nc.tensor.matmul(upd(h), kTok[0:GC, h, :], vg[0:GC, h * GV:(h + 1) * GV], start=True, stop=True).then_inc(s["gupd"], 1)
                    for h in range(GH):
                        pe.wait_ge(s["state"], 8 * i + (h | 1) + 1)
                        nc.tensor.matmul(big[GC:P, h, 0:GV], E[2][:, h * P + GC:(h + 1) * P], S[1][:, h, :], start=False, stop=True)
                        nc.tensor.matmul(upd(h), kTok[GC:P, h, :], vg[GC:P, h * GV:(h + 1) * GV], start=True, stop=True).then_inc(s["gupd"], 1)
                    pe.wait_ge(s["roped"], i + 1)
                    for b in range(6):
                        at_least(pe, free[b % 2], USES * i + 1 + b // 2)
                        for h in range(4):
                            last = nc.tensor.transpose(Tb[b % 2][:, h * P:(h + 1) * P], zq[:, 4 * b + h, :], ident)
                        last.then_inc(full[b % 2], 1)

                    def scores(h):
                        if h == 0:
                            pe.wait_ge(free[0], USES * i + 4)
                            pe.wait_ge(free[1], USES * i + 4)
                            pe.wait_ge(s["normed"], 4 * i + 4)
                        else:
                            pe.wait_ge(s["exp"], 4 * i + h)
                        for b in range(2):
                            nc.tensor.matmul(big[:, b, :], identb[:, :], masks[:, bass.ds(896 + 512 * b - P * i, 512)], start=True, stop=False)
                            nc.tensor.matmul(big[:, b, :], qT[:, 8 + h, :], kT[:, 8 + h, b * 512:(b + 1) * 512], start=False, stop=True)
                        for c, n in ((0, 512), (512, P)):
                            dst = big[:, 2 + c // 512, 0:n]
                            nc.tensor.matmul(dst, identb[:, :], masks[:, bass.ds(M1 + 512 + c + lag1 * P, n)], start=True, stop=False)
                            nc.tensor.matmul(dst, qT[:, 4 + h, :], kT[:, 4 + h, bass.ds(st1 * P + c, n)], start=False, stop=True)
                        dst = big[:, 3, P:3 * P]
                        nc.tensor.matmul(dst, identb[:, :], masks[:, bass.ds(M0 + P + lag0 * P, 2 * P)], start=True, stop=False)
                        nc.tensor.matmul(dst, qT[:, h, :], kT[:, h, bass.ds(st0 * P, 2 * P)], start=False, stop=True).then_inc(s["scores"], 1)

                    scores(0)
                    for h in range(AH):
                        if h + 1 < AH:
                            scores(h + 1)
                        else:
                            pe.wait_ge(s["exp"], 4 * i + h + 1)
                        for b in range(4):
                            at_least(pe, free[b % 2], USES * i + 4 + 2 * h + b // 2)
                            for j in range(4 * b, min(4 * b + 4, KT)):
                                last = nc.tensor.transpose(Tb[b % 2][:, (j % 4) * P:(j % 4 + 1) * P], Pm[:, j * P:(j + 1) * P], ident)
                            last.then_inc(full[b % 2], 1)
                        pe.wait_ge(free[0], USES * i + 6 + 2 * h)
                        pe.wait_ge(free[1], USES * i + 6 + 2 * h)
                        if h < 2:
                            pe.wait_ge(s["state"], 8 * i + 8)
                        else:
                            pe.wait_ge(s["heads"], 4 * i + h - 1)
                        for j in range(KT):
                            g, t = (2, j) if j < 8 else (1, st1 + j - 8) if j < 13 else (0, st0 + j - 13)
                            c0 = (g * AH + h) * HD
                            vv = V[:, bass.ds(t, 1), c0:c0 + HD].rearrange("p a d -> p (a d)")
                            last = nc.tensor.matmul(OM[h % 2][:, 0:HD], PT[h % 2][:, j, :], vv, start=(j == 0), stop=(j == KT - 1))
                        last.then_inc(s["pv"], 1)
                tiles(pe, tile)

            @block.scalar
            def _(act):
                act.wait_ge(s["const"], 64)

                def tile(i, st1, lag1, st0, lag0, late):
                    act.wait_ge(s["zg"], 16 * i + 16)
                    at_least(act, s["mixa"], i)
                    nc.scalar.activation(er[:, :], ra, ACT.Exp, scale=-1.0).then_inc(s["silu_e"], 1)
                    act.wait_ge(s["tr"], i + 1)
                    nc.scalar.copy(alrT[:, :], OM[0][0:RANK, 0:P]).then_inc(s["alr"], 1)
                    act.wait_ge(s["xb"], 4 * i + 4)
                    link = chained(act, s["ln_steps"], 2 * i)
                    link(nc.scalar.activation(xa[:, :], xb[:, :], ACT.Abs))
                    link(nc.scalar.activation(xa[:, :], xa[:, :], ACT.Exp, scale=-1.0))
                    nc.scalar.activation(xa[:, :], xa[:, :], ACT.Ln, bias=1.0).then_inc(s["ln"], 1)
                    act.wait_ge(s["dec_steps"], 8 * i + 8)
                    nc.scalar.activation(E[0][:, :], d1[:, :], ACT.Exp, scale=1.0 / TAU).then_inc(s["exps"], 1)
                    nc.scalar.activation(E[1][:, :], d1[:, :], ACT.Exp, scale=-1.0 / TAU).then_inc(s["exps"], 1)
                    nc.scalar.activation(E[2][:, :], B[:, :], ACT.Exp, scale=1.0 / TAU).then_inc(s["exps"], 1)
                    nc.scalar.activation(E[3][:, :], dl[:, :], ACT.Exp, scale=1.0 / TAU).then_inc(s["exps"], 1)
                    at_least(act, s["state"], 8 * i)
                    nc.scalar.activation(EL[:, :], v8(B)[:, :, GC - 1:GC].rearrange("p n c -> p (n c)"), ACT.Exp, scale=1.0 / TAU).then_inc(s["exps"], 1)
                    act.wait_ge(full[1], USES * i + 1)
                    nc.scalar.copy(kTok[:, :, :].rearrange("p h d -> p (h d)"), Tb[1][:, :]).then_inc(free[1], 1)
                    act.wait_ge(s["gupd"], 8 * i + 8)
                    for h in range(GH):
                        nc.scalar.activation(xa[:, 0:GV], big[:, h, 0:GV], ACT.Square, accum_out=gst[:, 0, h:h + 1]).then_inc(s["squares"], 1)
                        act.wait_ge(s["squares"], 4 * i + h + 1)
                    act.wait_ge(s["var_steps"], 2 * i + 2)
                    nc.scalar.activation(gst[:, 1, :], gst[:, 0, :], ACT.Sqrt).then_inc(s["root"], 1)
                    for b in (1, 3, 5):
                        act.wait_ge(full[1], USES * i + 2 + b // 2)
                        dst = qT[:, 4 * b:4 * b + 4, :] if b < 3 else kT[:, 4 * b - QH:4 * b - QH + 4, bass.ds(i * P, P)]
                        nc.scalar.copy(dst, Tb[1][:, :].rearrange("p (h t) -> p h t", h=4)).then_inc(free[1], 1)
                    for h in range(AH):
                        act.wait_ge(s["negmax"], 4 * i + h + 1)
                        if h:
                            act.wait_ge(full[0], USES * i + 4 + 2 * h)
                            act.wait_ge(full[1], USES * i + 4 + 2 * h)
                        nc.scalar.activation(Pm[:, :], sc_all[:, 0:NKEY], ACT.Exp, bias=nm[:, h:h + 1], scale=SCALE_B,
                                             accum_out=sm[:, h:h + 1]).then_inc(s["exp"], 1)
                        if h < 2:
                            at_least(act, s["pv"], 4 * i)
                        else:
                            act.wait_ge(s["pv"], 4 * i + h - 1)
                        for b in (1, 3):
                            n = min(4, KT - 4 * b)
                            act.wait_ge(full[1], USES * i + 5 + 2 * h + b // 2)
                            nc.scalar.copy(PT[h % 2][:, 4 * b:4 * b + n, :].rearrange("p j t -> p (j t)"), Tb[1][:, 0:n * P]).then_inc(free[1], 1)
                tiles(act, tile)

            @block.vector
            def _(dve):
                dve.wait_ge(s["const"], 64)

                def tile(i, st1, lag1, st0, lag0, late):
                    dve.wait_ge(s["zq"], 16 * i + 16)
                    cos = ropes[:, bass.ds(i, 1), 0:ROT].to_broadcast([P, 2 * QH, ROT])
                    sin = ropes[:, bass.ds(i, 1), ROT:2 * ROT].to_broadcast([P, 2 * QH, ROT])
                    x1, x2 = zq[:, :, 0:ROT], zq[:, :, ROT:2 * ROT]
                    for n, (a, b) in enumerate(((x1, cos), (x2, sin), (x2, cos), (x1, sin))):
                        nc.vector.tensor_tensor(rt[:, n], a, b, ALU.mult).then_inc(s["rope_steps"], 1)
                    dve.wait_ge(s["rope_steps"], 5 * i + 4)
                    nc.vector.tensor_tensor(x1, rt[:, 0], rt[:, 1], ALU.subtract).then_inc(s["rope_steps"], 1)
                    nc.vector.tensor_tensor(x2, rt[:, 2], rt[:, 3], ALU.add).then_inc(s["roped"], 1)
                    dve.wait_ge(s["rope_steps"], 5 * i + 5)
                    dve.wait_ge(s["roped"], i + 1)
                    dve.wait_ge(s["x"], i + 1)
                    for h in range(GH):
                        nc.vector.tensor_scalar(xb[:, h * P:(h + 1) * P], OM[1][:, h * P:(h + 1) * P], ab[:, h:h + 1], None, ALU.add).then_inc(s["xb"], 1)
                    dve.wait_ge(s["ln"], i + 1)
                    link = chained(dve, s["dec_steps"], 8 * i)
                    link(nc.vector.scalar_tensor_tensor(out=xb[:, :], in0=xb[:, :], scalar=0.0, in1=xa[:, :], op0=ALU.min, op1=ALU.subtract))
                    for h in range(GH):
                        link(nc.vector.tensor_tensor_scan(B[:, h * P:(h + 1) * P], restart, xb[:, h * P:(h + 1) * P], 0.0, ALU.mult, ALU.add))
                    mid = v8(B)[:, :, GC // 2 - 1:GC // 2].to_broadcast([P, 2 * GH, GC])
                    end = v8(B)[:, :, GC - 1:GC].to_broadcast([P, 2 * GH, GC])
                    link(nc.vector.tensor_tensor(v8(d1), v8(B), mid, ALU.subtract))
                    link(nc.vector.tensor_scalar(d1[:, :], d1[:, :], 40 * TAU, -40 * TAU, ALU.min, ALU.max))
                    link(nc.vector.tensor_tensor(v8(dl), end, v8(B), ALU.subtract))
                    dve.wait_ge(s["exps"], 5 * i + 5)
                    nc.vector.scalar_tensor_tensor(out=E[0][:, :], in0=qps, scalar=SCALE_A, in1=E[0][:, :], op0=ALU.mult, op1=ALU.mult).then_inc(s["qk"], 1)
                    nc.vector.scalar_tensor_tensor(out=E[2][:, :], in0=qps, scalar=SCALE_A, in1=E[2][:, :], op0=ALU.mult, op1=ALU.mult).then_inc(s["qk"], 1)
                    nc.vector.tensor_tensor(kp[:, :], kps, E[1][:, :], ALU.mult).then_inc(s["qk"], 1)
                    nc.vector.tensor_tensor(kpp[:, :], kps, E[3][:, :], ALU.mult).then_inc(s["qk"], 1)
                    dve.wait_ge(full[0], USES * i + 1)
                    nc.vector.tensor_tensor(attm[:, :, :], Tb[0][:, :].rearrange("p (h t) -> p h t", h=GH),
                                            causal.unsqueeze(1).to_broadcast([P, GH, P]), ALU.mult).then_inc(free[0], 1)
                    for c in range(2):
                        for h in range(GH):
                            dve.wait_ge(s["gupd"], 8 * i + 4 * c + (h | 1) + 1)
                            if c:
                                dve.wait_ge(s["state"], 8 * i + h + 1)
                            nc.vector.scalar_tensor_tensor(out=S[1 - c][:, h, :], in0=S[c][:, h, :], scalar=EL[:, 2 * h + c:2 * h + c + 1],
                                                           in1=OM[h // 2][:, (h % 2) * GV:(h % 2 + 1) * GV],
                                                           op0=ALU.mult, op1=ALU.add).then_inc(s["state"], 1)
                    dve.wait_ge(s["squares"], 4 * i + 4)
                    link = chained(dve, s["var_steps"], 2 * i)
                    link(nc.vector.tensor_scalar(gst[:, 0, :], gst[:, 0, :], 1.0 / GV, EPS, ALU.mult, ALU.add))
                    link(nc.vector.reciprocal(gst[:, 0, :], gst[:, 0, :]))
                    dve.wait_ge(s["root"], i + 1)
                    at_least(dve, s["outa"], 16 * i)
                    for h in range(GH):
                        cols = slice(h * GV, (h + 1) * GV)
                        nc.vector.scalar_tensor_tensor(out=om[:, cols], in0=big[:, h, 0:GV], scalar=gst[:, 1, h:h + 1], in1=gn[:, cols],
                                                       op0=ALU.mult, op1=ALU.mult).then_inc(s["normed"], 1)
                    dve.wait_ge(s["silu_e"], i + 1)
                    link = chained(dve, s["silu_steps"], 3 * i)
                    link(nc.vector.tensor_scalar_add(er[:, :], er[:, :], 1.0))
                    link(nc.vector.reciprocal(er[:, :], er[:, :]))
                    link(nc.vector.tensor_tensor(er[:, :], er[:, :], ra, ALU.mult))
                    dve.wait_ge(s["normed"], 4 * i + 4)
                    nc.vector.tensor_tensor(om[:, :], om[:, :], er[:, :], ALU.mult).then_inc(s["mixa"], 1)
                    for b in (0, 2, 4):
                        dve.wait_ge(full[0], USES * i + 2 + b // 2)
                        dst = qT[:, 4 * b:4 * b + 4, :] if b < 3 else kT[:, 4 * b - QH:4 * b - QH + 4, bass.ds(i * P, P)]
                        nc.vector.tensor_copy(dst, Tb[0][:, :].rearrange("p (h t) -> p h t", h=4)).then_inc(free[0], 1)

                    def row_max(h):
                        dve.wait_ge(s["scores"], 4 * i + h + 1)
                        nc.vector.reduce_max(mx[:, h:h + 1], sc_all[:, 0:NKEY], AX.X).then_inc(s["max_steps"], 1)
                        dve.wait_ge(s["max_steps"], 4 * i + h + 1)
                        nc.vector.tensor_scalar(nm[:, h:h + 1], mx[:, h:h + 1], -SCALE_B, None, ALU.mult).then_inc(s["negmax"], 1)
                    row_max(0)
                    for h in range(AH):
                        if h + 1 < AH:
                            row_max(h + 1)
                        if h < 2:
                            at_least(dve, s["pv"], 4 * i)
                        else:
                            dve.wait_ge(s["pv"], 4 * i + h - 1)
                        for b in (0, 2):
                            dve.wait_ge(full[0], USES * i + 5 + 2 * h + b // 2)
                            nc.vector.tensor_copy(PT[h % 2][:, 4 * b:4 * b + 4, :].rearrange("p j t -> p (j t)"), Tb[0][:, :]).then_inc(free[0], 1)
                        dve.wait_ge(s["exp"], 4 * i + h + 1)
                        nc.vector.reciprocal(ri[:, h:h + 1], sm[:, h:h + 1]).then_inc(s["rinv"], 1)
                        dve.wait_ge(s["rinv"], 4 * i + h + 1)
                        dve.wait_ge(s["pv"], 4 * i + h + 1)
                        if h == 0:
                            at_least(dve, s["outb"], 16 * i)
                        nc.vector.tensor_scalar(ob[:, h * HD:(h + 1) * HD], OM[h % 2][:, 0:HD], ri[:, h:h + 1], None, ALU.mult).then_inc(s["heads"], 1)
                tiles(dve, tile)


def sample_mixers(k, misc):
    nc = k.nc
    GW = GH * GV
    R = NS
    KV = 2 * AH * HD
    names = ("in", "kv", "state_in", "alr_ps", "alr", "x_ps", "x", "ln_steps", "ln", "la", "decay", "qT_ps", "qm", "ksel", "upd", "state",
             "sums", "sq", "var", "root", "silu_e", "mixa", "dve", "rope", "nsel", "qbc", "prod", "qk_done", "sT_ps", "sub", "exp", "p", "pT_ps", "pm", "pv",
             "mixb", "out", "state_out")
    s = {n: k.sem("sm_" + n) for n in names}
    kvl = [k.sem(f"sm_kv_loaded{n}") for n in range(NS)]
    stl = [k.sem(f"sm_state_loaded{n}") for n in range(NS)]
    with k.phase() as f:
        zs = f.sb("sm_z", [R, GZA])
        kv = f.sb("sm_kv", [P, NS * NG, KV])
        S = f.sb("sm_S", [P, NS * GH, GV])
        w2, ab, gn = f.sb("sm_w2", [RANK, GH * GK]), f.sb("sm_ab", [P, GH]), f.sb("sm_gn", [R, GW])
        rope = f.sb("sm_rope", [R, 2 * ROT])
        alrT, x, xa, EL = f.sb("sm_alrT", [RANK, R]), f.sb("sm_x", [P, GH, R]), f.sb("sm_xa", [P, GH, R]), f.sb("sm_EL", [P, GH, R])
        ksel = f.sb("sm_ksel", [R, 2, GH * GK])
        qT, qm = f.sb("sm_qT", [P, GH, R]), f.sb("sm_qm", [P, GH, NS, R])
        st = f.sb("sm_stats", [R, 2, GH])
        nsel = f.sb("sm_nsel", [R, NS, P])
        big = f.sb("sm_big", [R, 2048])
        er, om, ob = f.sb("sm_er", [R, GW]), f.sb("sm_om", [R, GW]), f.sb("sm_ob", [R, AH * HD])
        prod = f.sb("sm_prod", [P, 2, AH, HD])
        sc = f.sb("sm_sc", [P, NG, AH, NS])
        m2 = f.sb("sm_m2", [R, 8, 12])
        pTs, pm = f.sb("sm_pT", [P, QH, R]), f.sb("sm_pm", [P, QH, NS, R])
        misc_ps = f.ps("sm_misc_ps", [P, 512])
        up = [f.ps(f"sm_upd_ps{b}", [P, 512]) for b in range(4)]
        sp3 = f.ps("sm_s_ps", [R, 3, 512])
        ident = misc[:, C_ID:C_ID + P]
        eye8 = misc[:, C_PICK + NS * NS:C_PICK + 2 * NS * NS].rearrange("p (n m) -> p n m", m=NS)
        caches = [k.i["cache_kv_" + n][0] for n in ("w128", "w512", "w2048")]
        qk = zs[:, QB:VB].rearrange("p (h d) -> p h d", d=HD)
        vn = zs[:, VB:GZA].rearrange("p (h d) -> p h d", d=HD)
        s_ps = sp3[:, :, :].rearrange("p b n -> p (b n)").rearrange("p (h c) -> p h c", h=AH)
        with nc.Block() as block:
            @block.sync
            def _(sp):
                sp.dma_start(zs[:, :], k.z[SEQ:ROWS, 0:GZA]).then_inc(s["in"], 16)
                sp.dma_start(w2[:, :], k.i["gla_a_w2"][0]).then_inc(s["in"], 16)
                with nc.allow_non_contiguous_dma(reason="512 single values, once"):
                    sp.dma_start(ab[:, :], k.i["gla_a_b"][0].rearrange("(h p) -> p h", p=P)).then_inc(s["in"], 16)
                sp.dma_start(gn[:, :], k.i["gla_gn_g"].to_broadcast([R, GW])).then_inc(s["in"], 16)
                sp.dma_start(rope[:, :], k.c["rope"][SEQ:ROWS, :]).then_inc(s["in"], 16)
                for n in range(NS):
                    sp.dma_start(S[:, n * GH:(n + 1) * GH, :], k.i["state_gla"][0, n].rearrange("h k v -> k h v")).then_inc(stl[n], 16)
                    for g, (width, dil) in enumerate(GROUPS):
                        src = caches[g][n].rearrange("(j d) a h e -> j d (a h e)", d=dil)[:, 0, :]
                        sp.dma_start(kv[:, n * NG + g, :], src).then_inc(kvl[n], 16)
                sp.wait_ge(s["rope"], 6)
                for g, name in enumerate(("w128", "w512", "w2048")):
                    o = k.o["kv_" + name + "_sample"][0, :, GROUPS[g][0] - 1]
                    sp.dma_start(o[:, 0, :, :], qk[:, QH + g * AH:QH + (g + 1) * AH, :]).then_inc(s["out"], 16)
                    sp.dma_start(o[:, 1, :, :], vn[:, g * AH:(g + 1) * AH, :]).then_inc(s["out"], 16)
                sp.wait_ge(s["mixa"], 1)
                sp.dma_start(k.mix[SEQ:ROWS, 0:GW], om[:, :]).then_inc(s["out"], 16)
                sp.dma_start(k.o["state_sample"][0].rearrange("n h k v -> k (n h) v"), S[:, :, :]).then_inc(s["out"], 16)
                sp.wait_ge(s["mixb"], 1)
                sp.dma_start(k.mix[SEQ:ROWS, GW:GW + AH * HD], ob[:, :]).then_inc(s["out"], 16)
                sp.wait_ge(s["out"], 16 * 9)

            @block.tensor
            def _(pe):
                pe.wait_ge(s["in"], 80)
                nc.tensor.transpose(misc_ps[0:RANK, 0:R], zs[:, ALR:ALR + RANK], ident[0:R, 0:R]).then_inc(s["alr_ps"], 1)
                pe.wait_ge(s["alr"], 1)
                for h in range(GH):
                    last = nc.tensor.matmul(misc_ps[:, h * R:(h + 1) * R], w2[:, h * GK:(h + 1) * GK], alrT[:, :], start=True, stop=True)
                last.then_inc(s["x_ps"], 1)
                pe.wait_ge(s["x"], GH)
                for h in range(GH):
                    last = nc.tensor.transpose(misc_ps[:, h * R:(h + 1) * R], zs[:, QA + h * GK:QA + (h + 1) * GK], ident[0:R, 0:R])
                last.then_inc(s["qT_ps"], 1)
                for n in range(NS):
                    pe.wait_ge(s["ksel"], n + 1)
                    at_least(pe, s["state"], GH * (n - 1))
                    for h in range(GH):
                        last = nc.tensor.matmul(up[2 * (n % 2) + h // 2][:, (h % 2) * GV:(h % 2 + 1) * GV], ksel[:, n % 2, h * GK:(h + 1) * GK],
                                                zs[:, VA + h * GV:VA + (h + 1) * GV], start=True, stop=True)
                    last.then_inc(s["upd"], 1)
                pe.wait_ge(s["state"], GH * NS)
                pe.wait_ge(s["qm"], GH)
                for h in range(GH):
                    for n in range(NS):
                        last = nc.tensor.matmul(up[h // 2][0:R, (h % 2) * GV:(h % 2 + 1) * GV], qm[:, h, n, :], S[:, n * GH + h, :],
                                                start=(n == 0), stop=(n == NS - 1))
                last.then_inc(s["sums"], 1)
                pe.wait_ge(s["rope"], 6)
                pe.wait_ge(s["nsel"], 1)
                for j in range(NS * NG):
                    n, g = j // NG, j % NG
                    at_least(pe, s["prod"], j - 1)
                    nc.tensor.matmul(up[2 + j % 2][:, :], nsel[:, n, :], zs[:, QB + g * AH * HD:QB + (g + 1) * AH * HD], start=True, stop=True).then_inc(s["qbc"], 1)
                pe.wait_ge(s["qk_done"], NS * NG)
                for h in range(AH):
                    for g in range(NG):
                        last = nc.tensor.transpose(s_ps[:, h, g * P:(g + 1) * P], sc[:, g, h, :], ident)
                last.then_inc(s["sT_ps"], 1)
                pe.wait_ge(s["p"], 1)
                for g in range(NG):
                    for h in range(AH):
                        c = g * AH + h
                        last = nc.tensor.transpose(misc_ps[:, c * R:(c + 1) * R], big[:, h * 384 + g * P:h * 384 + (g + 1) * P], ident[0:R, 0:R])
                last.then_inc(s["pT_ps"], 1)
                pe.wait_ge(s["pm"], 1)
                for h in range(AH):
                    for j in range(NS * NG):
                        n, g = j // NG, j % NG
                        last = nc.tensor.matmul(up[2][0:R, h * HD:(h + 1) * HD], pm[:, g * AH + h, n, :], kv[:, j, (AH + h) * HD:(AH + h + 1) * HD],
                                                start=(j == 0), stop=(j == NS * NG - 1))
                last.then_inc(s["pv"], 1)

            @block.scalar
            def _(act):
                act.wait_ge(s["in"], 80)
                nc.scalar.activation(er[:, :], zs[:, RA:RA + GW], ACT.Exp, scale=-1.0).then_inc(s["silu_e"], 1)
                act.wait_ge(s["alr_ps"], 1)
                nc.scalar.copy(alrT[:, :], misc_ps[0:RANK, 0:R]).then_inc(s["alr"], 1)
                act.wait_ge(s["x"], GH)
                link = chained(act, s["ln_steps"])
                link(nc.scalar.activation(xa[:, :, :], x[:, :, :], ACT.Abs))
                link(nc.scalar.activation(xa[:, :, :], xa[:, :, :], ACT.Exp, scale=-1.0))
                nc.scalar.activation(xa[:, :, :], xa[:, :, :], ACT.Ln, bias=1.0).then_inc(s["ln"], 1)
                act.wait_ge(s["la"], 1)
                nc.scalar.activation(EL[:, :, :], x[:, :, :], ACT.Exp, scale=1.0 / TAU).then_inc(s["decay"], 1)
                act.wait_ge(s["sums"], 1)
                for h in range(GH):
                    nc.scalar.activation(xa_row(f, h, om), up[h // 2][0:R, (h % 2) * GV:(h % 2 + 1) * GV], ACT.Square,
                                         accum_out=st[:, 0, h:h + 1]).then_inc(s["sq"], 1)
                    act.wait_ge(s["sq"], h + 1)
                act.wait_ge(s["var"], 1)
                nc.scalar.activation(st[:, 1, :], st[:, 0, :], ACT.Sqrt).then_inc(s["root"], 1)
                act.wait_ge(s["sub"], 2)
                nc.scalar.activation(big[:, 0:1536], big[:, 0:1536], ACT.Exp, scale=SCALE_B).then_inc(s["exp"], 1)
                nc.scalar.activation(m2[:, 1, :], m2[:, 1, :], ACT.Exp, scale=SCALE_B).then_inc(s["exp"], 1)

            @block.vector
            def _(dve):
                link = chained(dve, s["dve"])

                def signal(ins, name, value):
                    ins.then_inc(s[name], 1)
                    dve.wait_ge(s[name], value)
                dve.wait_ge(s["in"], 80)
                cos = rope[:, 0:ROT].unsqueeze(1).to_broadcast([R, 2 * QH, ROT])
                sin = rope[:, ROT:2 * ROT].unsqueeze(1).to_broadcast([R, 2 * QH, ROT])
                rt = big[:, 0:4 * 2 * QH * ROT].rearrange("p (n h r) -> p n h r", n=4, h=2 * QH)
                x1, x2 = qk[:, :, 0:ROT], qk[:, :, ROT:2 * ROT]
                for n, (a, b) in enumerate(((x1, cos), (x2, sin), (x2, cos), (x1, sin))):
                    signal(nc.vector.tensor_tensor(rt[:, n], a, b, ALU.mult), "rope", n + 1)
                signal(nc.vector.tensor_tensor(x1, rt[:, 0], rt[:, 1], ALU.subtract), "rope", 5)
                signal(nc.vector.tensor_tensor(x2, rt[:, 2], rt[:, 3], ALU.add), "rope", 6)
                nc.vector.tensor_copy(nsel[:, :, :], ident[0:R, 0:NS].unsqueeze(2).to_broadcast([R, NS, P])).then_inc(s["nsel"], 1)

                def keys_of(n):
                    nc.vector.tensor_scalar(ksel[:, n % 2, :], zs[:, KA:KA + GH * GK], ident[0:R, n:n + 1], None, ALU.mult).then_inc(s["ksel"], 1)
                keys_of(0)
                keys_of(1)
                dve.wait_ge(s["x_ps"], 1)
                for h in range(GH):
                    signal(nc.vector.tensor_scalar(x[:, h, :], misc_ps[:, h * R:(h + 1) * R], ab[:, h:h + 1], None, ALU.add), "x", h + 1)
                dve.wait_ge(s["ln"], 1)
                nc.vector.scalar_tensor_tensor(out=x[:, :, :], in0=x[:, :, :], scalar=0.0, in1=xa[:, :, :], op0=ALU.min, op1=ALU.subtract).then_inc(s["la"], 1)
                dve.wait_ge(s["qT_ps"], 1)
                link(nc.vector.tensor_scalar(qT[:, :, :].rearrange("p h n -> p (h n)"), misc_ps[:, 0:GH * R], SCALE_A, None, ALU.mult))
                for h in range(GH):
                    nc.vector.tensor_tensor(qm[:, h], qT[:, h, :].unsqueeze(2).to_broadcast([P, NS, R]), eye8, ALU.mult).then_inc(s["qm"], 1)
                dve.wait_ge(s["decay"], 1)
                for n in range(NS):
                    dve.wait_ge(stl[n], 16)
                    dve.wait_ge(s["upd"], n + 1)
                    for h in range(GH):
                        j = n * GH + h
                        nc.vector.scalar_tensor_tensor(out=S[:, j, :], in0=S[:, j, :], scalar=EL[:, h, n:n + 1],
                                                       in1=up[2 * (n % 2) + h // 2][:, (h % 2) * GV:(h % 2 + 1) * GV],
                                                       op0=ALU.mult, op1=ALU.add).then_inc(s["state"], 1)
                    if n + 2 < NS:
                        keys_of(n + 2)
                dve.wait_ge(s["silu_e"], 1)
                link(nc.vector.tensor_scalar_add(er[:, :], er[:, :], 1.0))
                link(nc.vector.reciprocal(er[:, :], er[:, :]))
                link(nc.vector.tensor_tensor(er[:, :], er[:, :], zs[:, RA:RA + GW], ALU.mult))
                link(nc.vector.tensor_tensor(er[:, :], er[:, :], gn[:, :], ALU.mult))
                dve.wait_ge(s["sq"], GH)
                link(nc.vector.tensor_scalar(st[:, 0, :], st[:, 0, :], 1.0 / GV, EPS, ALU.mult, ALU.add))
                signal(nc.vector.reciprocal(st[:, 0, :], st[:, 0, :]), "var", 1)
                dve.wait_ge(s["root"], 1)
                for h in range(GH):
                    cols = slice(h * GV, (h + 1) * GV)
                    ins = nc.vector.scalar_tensor_tensor(out=om[:, cols], in0=up[h // 2][0:R, (h % 2) * GV:(h % 2 + 1) * GV], scalar=st[:, 1, h:h + 1],
                                                         in1=er[:, cols], op0=ALU.mult, op1=ALU.mult)
                    if h < GH - 1:
                        link(ins)
                ins.then_inc(s["mixa"], 1)
                for j in range(NS * NG):
                    n, g = j // NG, j % NG
                    if g == 0:
                        dve.wait_ge(kvl[n], 16 * NG)
                    dve.wait_ge(s["qbc"], j + 1)
                    pr = prod[:, j % 2]
                    nc.vector.tensor_tensor(pr, kv[:, j, 0:AH * HD].rearrange("p (h d) -> p h d", h=AH),
                                            up[2 + j % 2][:, :].rearrange("p (h d) -> p h d", h=AH), ALU.mult).then_inc(s["prod"], 1)
                    dve.wait_ge(s["prod"], j + 1)
                    nc.vector.reduce_sum(sc[:, g, :, n:n + 1], pr, AX.X).then_inc(s["qk_done"], 1)
                pn = kv_free(big)
                link(nc.vector.tensor_tensor(pn, qk[:, 0:QH, :], qk[:, QH:2 * QH, :], ALU.mult))
                link(nc.vector.reduce_sum(m2[:, 0, :].unsqueeze(2), pn, AX.X))
                dve.wait_ge(s["sT_ps"], 1)
                link(nc.vector.reduce_max(m2[:, 2, 0:AH].unsqueeze(2), s_ps, AX.X))
                link(nc.vector.reduce_max(m2[:, 3, 0:AH].unsqueeze(2), m2[:, 0, :].rearrange("p (g h) -> p h g", g=NG), AX.X))
                link(nc.vector.tensor_tensor(m2[:, 2, 0:AH], m2[:, 2, 0:AH], m2[:, 3, 0:AH], ALU.max))
                p = big[:, 0:1536].rearrange("p (h c) -> p h c", h=AH)
                signal(nc.vector.tensor_tensor(p, s_ps, m2[:, 2, 0:AH].unsqueeze(2).to_broadcast([R, AH, 384]), ALU.subtract), "sub", 1)
                gh = lambda a: a.rearrange("p (g h) -> p g h", g=NG)
                signal(nc.vector.tensor_tensor(gh(m2[:, 1, :]), gh(m2[:, 0, :]), m2[:, 2, 0:AH].unsqueeze(1).to_broadcast([R, NG, AH]), ALU.subtract), "sub", 2)
                dve.wait_ge(s["exp"], 2)
                link(nc.vector.reduce_sum(m2[:, 4, 0:AH].unsqueeze(2), p, AX.X))
                link(nc.vector.reduce_sum(m2[:, 5, 0:AH].unsqueeze(2), m2[:, 1, :].rearrange("p (g h) -> p h g", g=NG), AX.X))
                link(nc.vector.tensor_tensor(m2[:, 4, 0:AH], m2[:, 4, 0:AH], m2[:, 5, 0:AH], ALU.add))
                link(nc.vector.reciprocal(m2[:, 6, 0:AH], m2[:, 4, 0:AH]))
                link(nc.vector.tensor_tensor(gh(m2[:, 1, :]), gh(m2[:, 1, :]), m2[:, 6, 0:AH].unsqueeze(1).to_broadcast([R, NG, AH]), ALU.mult))
                signal(nc.vector.tensor_tensor(p, p, m2[:, 6, 0:AH].unsqueeze(2).to_broadcast([R, AH, 384]), ALU.mult), "p", 1)
                dve.wait_ge(s["pT_ps"], 1)
                link(nc.vector.tensor_copy(pTs[:, :, :].rearrange("p c n -> p (c n)"), misc_ps[:, 0:QH * R]))
                nc.vector.tensor_tensor(pm[:, :, :, :], pTs[:, :, :].unsqueeze(3).to_broadcast([P, QH, NS, R]),
                                        eye8.unsqueeze(1).to_broadcast([P, QH, NS, R]), ALU.mult).then_inc(s["pm"], 1)
                link(nc.vector.tensor_tensor(pn, vn, m2[:, 1, :].unsqueeze(2).to_broadcast([R, QH, HD]), ALU.mult))
                link(nc.vector.reduce_sum(ob[:, :].rearrange("p (h d) -> p h d", h=AH).unsqueeze(3), pn.rearrange("p (g h) d -> p h d g", g=NG), AX.X))
                dve.wait_ge(s["pv"], 1)
                nc.vector.tensor_tensor(ob[:, :], ob[:, :], up[2][0:R, :], ALU.add).then_inc(s["mixb"], 1)


def kv_free(big):
    return big[:, 0:QH * HD].rearrange("p (h d) -> p h d", h=QH)


def xa_row(f, h, om):
    return om[:, h * GV:(h + 1) * GV]


def merge_and_route(k, misc):
    nc = k.nc
    GW, OB = GH * GV, AH * HD
    KA_, KB_ = GW // P, OB // P
    MW = GW + OB
    names = ("wA", "wB", "wO", "wQ", "k12_l", "k12_ps", "k12_0", "k12", "gain", "m_l", "gz_l", "x_l", "sig_e", "sig_steps", "sig", "mT_ps", "mT", "br", "mg_steps", "merged", "gT_ps", "gT",
             "proj", "x1a", "x1", "sq", "var_steps", "root", "h2_steps", "h2", "hT_ps", "hT", "q_ps", "q", "qT_ps", "qT", "s_ps", "s", "top", "top_start", "top_done", "gsub", "gexp", "routed",
             "x1_out", "h2_out", "mod_l")
    s = {n: k.sem("rt_" + n) for n in names}
    with k.phase() as f:
        wA, wB = f.sb("rt_wA", [P, KA_, D]), f.sb("rt_wB", [P, KB_, D])
        wO, wQ = f.sb("rt_wO", [P, KD, D]), f.sb("rt_wQ", [P, KD, PH * DQ])
        k12 = f.sb("rt_k12", [P, 2, NK])
        mods, g2n = f.sb("rt_mods", [P, 3, D]), f.sb("rt_g", [P, D])
        m, gz, x = f.sb("rt_m", [P, MW]), f.sb("rt_gz", [P, 2 * D]), f.sb("rt_x", [P, D])
        Tm, Tg = f.sb("rt_Tm", [P, 12, P]), f.sb("rt_Tg", [P, KD, P])
        mg, h2, q2 = f.sb("rt_mg", [P, D]), f.sb("rt_h2", [P, D]), f.sb("rt_q2", [P, D])
        sc = f.sb("rt_s", [P, PH, 2, NK])
        rs = f.sb("rt_rs", [P, 2])
        work, cand, cwork = f.sb("rt_work", [P, NK]), f.sb("rt_cand", [P, TOPK, TOPK]), f.sb("rt_cwork", [P, TOPK * TOPK])
        v = f.sb("rt_v", [P, PH, 2, TOPK])
        vi = f.sb("rt_vi", [P, PH, 2, TOPK], U32)
        vif = f.sb("rt_vif", [P, PH, 2, TOPK])
        cs, ci, cj = f.sb("rt_cs", [P, PH, TOPK]), f.sb("rt_ci", [P, PH, TOPK], U32), f.sb("rt_cj", [P, PH, TOPK], U32)
        cf, cg = f.sb("rt_cf", [P, 2, PH, TOPK]), f.sb("rt_cg", [P, PH, TOPK])
        ef = f.sb("rt_ef", [P, 2, PH, TOPK])
        gs = f.sb("rt_gs", [P, 2, PH])
        G = f.ps("rt_G", [P, 4, 512])
        TP = f.ps("rt_TP", [P, 3, 512])
        kps = f.ps("rt_kps", [P, NK])
        ident = misc[:, C_ID:C_ID + P]
        Gf = G[:, :, :].rearrange("p b n -> p (b n)")
        G23 = G[:, 2:4, :].rearrange("p b n -> p (b n)").rearrange("p (c t) -> p c t", t=P)
        TPf = TP[:, :, :].rearrange("p b n -> p (b n)").rearrange("p (c t) -> p c t", t=P)

        def all_tiles(eng, tile):
            tile(0, P, P)
            with eng.Fori(1, TILES - 1) as i:
                tile(i, P, P)
            tile(TILES - 1, P, NS)
            tile(TILES, NS, 0)

        with nc.Block() as block:
            @block.sync
            def _(sp):
                sp.dma_start(k12[:, 0, 0:64], k.i["peer_k1"][0]).then_inc(s["k12_l"], 16)
                sp.dma_start(k12[:, 0, 64:128], k.i["peer_k2"][0]).then_inc(s["k12_l"], 16)
                sp.dma_start(mods[:, :, :].rearrange("p a d -> p (a d)"), k.mod[0:1, 2 * D:5 * D].to_broadcast([P, 3 * D])).then_inc(s["mod_l"], 16)
                sp.dma_start(g2n[:, :], k.i["norm2_g"].to_broadcast([P, D])).then_inc(s["mod_l"], 16)
                for t, name in ((wA, "w_branch_a"), (wB, "w_branch_b"), (wO, "w_out"), (wQ, "peer_wq")):
                    sp.dma_start(t[:, :, :], k.i[name][0].rearrange("(k p) n -> p k n", p=P)).then_inc(s[{"w_branch_a": "wA", "w_branch_b": "wB", "w_out": "wO", "peer_wq": "wQ"}[name]], 16)

                def tile(i, R, _):
                    rows = early(sp, i * P)
                    one = early(sp, i)
                    at_least(sp, s["mT_ps"], one)
                    sp.dma_start(m[0:R, :], k.mix[bass.ds(rows, R), :]).then_inc(s["m_l"], 16)
                    at_least(sp, s["merged"], one)
                    sp.dma_start(gz[0:R, :], k.z[bass.ds(rows, R), GZA:INW]).then_inc(s["gz_l"], 16)
                    at_least(sp, s["x1"], one)
                    src = k.i["x_sample"][:, 0, :] if R == NS else k.i["x_prompt"][0, bass.ds(rows, R), :]
                    sp.dma_start(x[0:R, :], src).then_inc(s["x_l"], 16)
                all_tiles(sp, tile)
                sp.wait_ge(s["h2"], TILES)
                sp.dma_start(mods[0:NS, :, :].rearrange("p a d -> p (a d)"), k.mod[1:1 + NS, 2 * D:5 * D]).then_inc(s["mod_l"], 16)

            @block.tensor
            def _(pe):
                pe.wait_ge(s["k12_l"], 32)
                nc.tensor.transpose(kps[:, :], k12[:, 0, :], ident).then_inc(s["k12_ps"], 1)

                def turn(dst, src, n, R, sem):
                    for c in range(n):
                        last = nc.tensor.transpose(dst[:, c, 0:R], src[0:R, c * P:(c + 1) * P], ident[0:R, 0:R])
                    last.then_inc(s[sem], 1)

                def product(bank, T, off, n, w, R):
                    for b in range(2):
                        for c in range(n):
                            last = nc.tensor.matmul(G[0:R, bank + b, :], T[:, off + c, 0:R], w[:, c, b * 512:(b + 1) * 512], start=(c == 0), stop=(c == n - 1))
                    return last

                def loaded(i, name):
                    if isinstance(i, int) and i == 0:
                        pe.wait_ge(s[name], 16)

                def tile(i, R, R_next):
                    if isinstance(i, int) and i == 0:
                        pe.wait_ge(s["m_l"], 16)
                        turn(TPf, m, 12, R, "mT_ps")
                    pe.wait_ge(s["mT"], i + 1)
                    at_least(pe, s["s"], i)
                    loaded(i, "wA")
                    product(2, Tm, 0, KA_, wA, R)
                    loaded(i, "wB")
                    product(0, Tm, KA_, KB_, wB, R).then_inc(s["br"], 1)
                    if R_next:
                        pe.wait_ge(s["m_l"], 16 * i + 32)
                        turn(TPf, m, 12, R_next, "mT_ps")
                    pe.wait_ge(s["merged"], i + 1)
                    turn(G23, mg, KD, R, "gT_ps")
                    pe.wait_ge(s["gT"], i + 1)
                    loaded(i, "wO")
                    product(0, Tg, 0, KD, wO, R).then_inc(s["proj"], 1)
                    pe.wait_ge(s["h2"], i + 1)
                    turn(G23, h2, KD, R, "hT_ps")
                    pe.wait_ge(s["hT"], i + 1)
                    loaded(i, "wQ")
                    product(0, Tg, 0, KD, wQ, R).then_inc(s["q_ps"], 1)
                    pe.wait_ge(s["q"], i + 1)
                    turn(G23, q2, PH, R, "qT_ps")
                    pe.wait_ge(s["qT"], i + 1)
                    if isinstance(i, int) and i == 0:
                        pe.wait_ge(s["k12"], 1)
                    for h in range(PH):
                        last = nc.tensor.matmul(G[0:R, h // 2, (h % 2) * 256:(h % 2 + 1) * 256], Tg[:, h, 0:R],
                                                k12[:, :, :].rearrange("p a n -> p (a n)"), start=True, stop=True)
                    last.then_inc(s["s_ps"], 1)
                all_tiles(pe, tile)

            @block.scalar
            def _(act):
                def copy_T(T, src, ps_sem, value, n, R, sem):
                    act.wait_ge(s[ps_sem], value)
                    nc.scalar.copy(T[:, 0:n, 0:R], src[:, 0:n, 0:R]).then_inc(s[sem], 1)

                def gate_exp(i, R):
                    act.wait_ge(s["gz_l"], 16 * i + 16)
                    nc.scalar.activation(gz[0:R, :], gz[0:R, :], ACT.Exp, scale=-1.0).then_inc(s["sig_e"], 1)

                def softmax_exp(i, R):
                    act.wait_ge(s["gsub"], i + 1)
                    nc.scalar.activation(cg[0:R], cg[0:R], ACT.Exp).then_inc(s["gexp"], 1)

                def tile(i, R, R_next):
                    first = isinstance(i, int) and i == 0
                    if first:
                        copy_T(Tm, TPf, "mT_ps", 1, 12, R, "mT")
                        gate_exp(0, R)
                    act.wait_ge(s["br"], i + 1)
                    if R_next:
                        copy_T(Tm, TPf, "mT_ps", i + 2, 12, R_next, "mT")
                    copy_T(Tg, G23, "gT_ps", i + 1, KD, R, "gT")
                    act.wait_ge(s["x1"], i + 1)
                    act.dma_start(k.x1[bass.ds(i * P, R), :], mg[0:R, :]).then_inc(s["x1_out"], 16)
                    at_least(act, s["h2_out"], 16 * i)
                    at_least(act, s["hT_ps"], i)
                    nc.scalar.activation(h2[0:R, :], mg[0:R, :], ACT.Square, accum_out=rs[0:R, 0:1]).then_inc(s["sq"], 1)
                    act.wait_ge(s["var_steps"], 2 * i + 2)
                    nc.scalar.activation(rs[0:R, 1:2], rs[0:R, 0:1], ACT.Sqrt).then_inc(s["root"], 1)
                    act.wait_ge(s["h2"], i + 1)
                    act.dma_start(k.h2[bass.ds(i * P, R), :], h2[0:R, :]).then_inc(s["h2_out"], 16)
                    copy_T(Tg, G23, "hT_ps", i + 1, KD, R, "hT")
                    if not first:
                        softmax_exp(i - 1, P)
                    if R_next:
                        gate_exp(i + 1, R_next)
                    act.wait_ge(s["q_ps"], i + 1)
                    nc.scalar.copy(q2[0:R, :], Gf[0:R, 0:2 * 512]).then_inc(s["q"], 1)
                    copy_T(Tg, G23, "qT_ps", i + 1, PH, R, "qT")
                    act.wait_ge(s["s_ps"], i + 1)
                    at_least(act, s["top_done"], i)
                    nc.scalar.copy(sc[0:R].rearrange("p h a n -> p (h a n)"), Gf[0:R, :]).then_inc(s["s"], 1)
                all_tiles(act, tile)
                softmax_exp(TILES, NS)
                act.wait_ge(s["x1_out"], 16 * (TILES + 1))
                act.wait_ge(s["h2_out"], 16 * (TILES + 1))

            @block.vector
            def _(dve):
                dve.wait_ge(s["k12_ps"], 1)
                nc.vector.memset(k12[:, :, :], 0.0).then_inc(s["k12_0"], 1)
                dve.wait_ge(s["k12_0"], 1)
                nc.vector.tensor_copy(k12[0:64, 0, :], kps[0:64, :]).then_inc(s["k12_0"], 1)
                dve.wait_ge(s["k12_0"], 2)
                nc.vector.tensor_copy(k12[64:128, 1, :], kps[64:128, :]).then_inc(s["k12"], 1)

                link = [None]

                def top_keys(i, R):
                    dve.wait_ge(s["s"], i + 1)
                    dve.sem_inc(s["top_start"], 1)
                    dve.sem_clear(s["top"])
                    link[0] = chained(dve, s["top"])
                    for h in range(PH):
                        for a in range(2):
                            vals, v0, v1 = sc[0:R, h, a, :], v[0:R, h, a, 0:8], v[0:R, h, a, 8:16]
                            link[0](nc.vector.max(v0, vals))
                            link[0](nc.vector.max_index(vi[0:R, h, a, 0:8], v0, vals))
                            link[0](nc.vector.match_replace(work[0:R, :], v0, vals, MASKED))
                            link[0](nc.vector.max(v1, work[0:R, :]))
                            link[0](nc.vector.max_index(vi[0:R, h, a, 8:16], v1, work[0:R, :]))
                    link[0](nc.vector.tensor_copy(vif[0:R].rearrange("p h a n -> p (h a n)"), vi[0:R].rearrange("p h a n -> p (h a n)")))

                def top_pairs(R):
                    for h in range(PH):
                        pair = cand[0:R].rearrange("p a b -> p (a b)")
                        link[0](nc.vector.tensor_tensor(cand[0:R], v[0:R, h, 0, :].unsqueeze(2).to_broadcast([R, TOPK, TOPK]),
                                                        v[0:R, h, 1, :].unsqueeze(1).to_broadcast([R, TOPK, TOPK]), ALU.add))
                        link[0](nc.vector.max(cs[0:R, h, 0:8], pair))
                        link[0](nc.vector.max_index(ci[0:R, h, 0:8], cs[0:R, h, 0:8], pair))
                        link[0](nc.vector.match_replace(cwork[0:R, :], cs[0:R, h, 0:8], pair, MASKED))
                        link[0](nc.vector.max(cs[0:R, h, 8:16], cwork[0:R, :]))
                        link[0](nc.vector.max_index(ci[0:R, h, 8:16], cs[0:R, h, 8:16], cwork[0:R, :]))

                def top_experts(i, R):
                    nc.vector.tensor_tensor(cg[0:R], cs[0:R], cs[0:R, :, 0:1].to_broadcast([R, PH, TOPK]), ALU.subtract).then_inc(s["gsub"], 1)
                    link[0](nc.vector.tensor_single_scalar(cj[0:R].rearrange("p h n -> p (h n)"), ci[0:R].rearrange("p h n -> p (h n)"), 4, ALU.logical_shift_right))
                    link[0](nc.vector.tensor_copy(cf[0:R, 0], cj[0:R]))
                    link[0](nc.vector.tensor_single_scalar(cj[0:R].rearrange("p h n -> p (h n)"), ci[0:R].rearrange("p h n -> p (h n)"), 15, ALU.bitwise_and))
                    link[0](nc.vector.tensor_copy(cf[0:R, 1], cj[0:R]))
                    slots = misc[0:R, C_SLOT:C_SLOT + TOPK].unsqueeze(1).to_broadcast([R, PH * TOPK, TOPK])
                    hit = sc[0:R].rearrange("p h a n -> p (h a n)")
                    for a in range(2):
                        flat = cf[0:R, a].rearrange("p h n -> p (h n)")
                        link[0](nc.vector.tensor_tensor(hit.rearrange("p (n j) -> p n j", j=TOPK), flat.unsqueeze(2).to_broadcast([R, PH * TOPK, TOPK]), slots, ALU.is_equal))
                        h4 = hit.rearrange("p (h n j) -> p h n j", h=PH, j=TOPK)
                        link[0](nc.vector.tensor_tensor(h4, h4, vif[0:R, :, a, :].unsqueeze(2).to_broadcast([R, PH, TOPK, TOPK]), ALU.mult))
                        link[0](nc.vector.reduce_sum(ef[0:R, a].rearrange("p h n -> p (h n)").unsqueeze(2), hit.rearrange("p (n j) -> p n j", j=TOPK), AX.X))
                    link[0](nc.vector.scalar_tensor_tensor(out=ef[0:R, 0], in0=ef[0:R, 0], scalar=float(NK), in1=ef[0:R, 1], op0=ALU.mult, op1=ALU.add))
                    flat = ef[0:R, 0].rearrange("p h n -> p (h n)")
                    if R == NS:
                        link[0](nc.vector.tensor_copy(k.idx_s[0:R, :], flat))
                    else:
                        link[0](nc.vector.tensor_copy(k.idx[:, bass.ds(i * P, P)], flat))
                    dve.wait_ge(s["gexp"], i + 1)
                    link[0](nc.vector.reduce_sum(gs[0:R, 0, :].unsqueeze(2), cg[0:R], AX.X))
                    link[0](nc.vector.reciprocal(gs[0:R, 1, :], gs[0:R, 0, :]))
                    dst = k.gate[:, bass.ds(i * P, P)] if R == P else k.gate_s[0:R, :]
                    nc.vector.tensor_tensor(dst.rearrange("p (h n) -> p h n", h=PH), cg[0:R],
                                            gs[0:R, 1, :].unsqueeze(2).to_broadcast([R, PH, TOPK]), ALU.mult).then_inc(s["top_done"], 1)

                def sigmoids(i, R):
                    dve.wait_ge(s["sig_e"], i + 1)
                    step = chained(dve, s["sig_steps"], 2 * i)
                    step(nc.vector.tensor_scalar_add(gz[0:R, :], gz[0:R, :], 1.0))
                    step(nc.vector.reciprocal(gz[0:R, :], gz[0:R, :]))

                def tile(i, R, R_next):
                    first = isinstance(i, int) and i == 0
                    if R == NS or first:
                        dve.wait_ge(s["mod_l"], 32 if first else 48)
                        nc.vector.scalar_tensor_tensor(out=mods[0:R, 2, :], in0=mods[0:R, 2, :], scalar=1.0, in1=g2n[0:R, :],
                                                       op0=ALU.add, op1=ALU.mult).then_inc(s["gain"], 1)
                        dve.wait_ge(s["gain"], 1 if first else 2)
                    if first:
                        sigmoids(0, R)
                    else:
                        top_keys(i - 1, P)
                    dve.wait_ge(s["br"], i + 1)
                    step = chained(dve, s["mg_steps"], 2 * i)
                    step(nc.vector.tensor_tensor(gz[0:R, 0:D], Gf[0:R, 2 * 512:4 * 512], gz[0:R, 0:D], ALU.mult))
                    step(nc.vector.tensor_tensor(gz[0:R, D:2 * D], Gf[0:R, 0:2 * 512], gz[0:R, D:2 * D], ALU.mult))
                    at_least(dve, s["x1_out"], 16 * i)
                    nc.vector.tensor_tensor(mg[0:R, :], gz[0:R, 0:D], gz[0:R, D:2 * D], ALU.add).then_inc(s["merged"], 1)
                    if not first:
                        top_pairs(P)
                    dve.wait_ge(s["proj"], i + 1)
                    dve.wait_ge(s["x_l"], 16 * i + 16)
                    nc.vector.tensor_tensor(mg[0:R, :], Gf[0:R, 0:D], mods[0:R, 0, :], ALU.mult).then_inc(s["x1a"], 1)
                    dve.wait_ge(s["x1a"], i + 1)
                    nc.vector.tensor_tensor(mg[0:R, :], mg[0:R, :], x[0:R, :], ALU.add).then_inc(s["x1"], 1)
                    dve.wait_ge(s["sq"], i + 1)
                    step = chained(dve, s["var_steps"], 2 * i)
                    step(nc.vector.tensor_scalar(rs[0:R, 0:1], rs[0:R, 0:1], 1.0 / D, EPS, ALU.mult, ALU.add))
                    step(nc.vector.reciprocal(rs[0:R, 0:1], rs[0:R, 0:1]))
                    dve.wait_ge(s["root"], i + 1)
                    step = chained(dve, s["h2_steps"], i)
                    step(nc.vector.scalar_tensor_tensor(out=h2[0:R, :], in0=mg[0:R, :], scalar=rs[0:R, 1:2], in1=mods[0:R, 2, :], op0=ALU.mult, op1=ALU.mult))
                    nc.vector.tensor_tensor(h2[0:R, :], h2[0:R, :], mods[0:R, 1, :], ALU.add).then_inc(s["h2"], 1)
                    if not first:
                        top_experts(i - 1, P)
                    if R_next:
                        sigmoids(i + 1, R_next)
                all_tiles(dve, tile)
                top_keys(TILES, NS)
                top_pairs(NS)
                top_experts(TILES, NS)


GELU_C = float(np.sqrt(2.0 / np.pi))


def gelu_steps(nc, link, a, t, u):
    link(nc.vector.tensor_tensor(t, a, a, ALU.mult))
    link(nc.vector.tensor_scalar(t, t, 0.044715, 1.0, ALU.mult, ALU.add))
    link(nc.vector.tensor_tensor(u, t, a, ALU.mult))
    return nc.vector.tensor_scalar(u, u, -50.0, None, ALU.max)


def experts(k, misc):
    nc = k.nc
    NSLOT = TOPK
    GRP = 4
    NQ = NSLOT // GRP
    names = ("in", "mod", "idxT_ps", "idxT", "bc", "bc_used", "dots", "s_u", "s_exp", "steps", "wm", "s_sum", "s_t", "x1", "sq", "var", "root", "y", "h2_l", "x1_l",
             "staged", "dotted", "g_steps", "g_u", "g_exp", "w", "diag", "vdone", "zero", "tail_t", "t_steps", "y_out", "h2s", "nsel", "tiles_done")
    s = {n: k.sem("ex_" + n) for n in names}
    us = [k.sem(f"ex_u_sample{n}") for n in range(NS)]
    vs = [k.sem(f"ex_v_sample{n}") for n in range(NS)]
    ul = [k.sem(f"ex_u_loaded{q}") for q in range(NQ)]
    vl = [k.sem(f"ex_v_loaded{q}") for q in range(NQ)]
    u_dram, v_dram = k.i["peer_u"], k.i["peer_v"]
    with k.phase() as f:
        U = [f.sb(f"ex_U{n}", [P, D]) for n in range(NSLOT)]
        V = [f.sb(f"ex_V{n}", [P, D]) for n in range(NSLOT)]
        g2m, fg = f.sb("ex_g2", [P, 2, D]), f.sb("ex_fg", [P, D])
        h2, x1, junk, y = f.sb("ex_h2", [P, D]), f.sb("ex_x1", [P, D]), f.sb("ex_junk", [P, D]), f.sb("ex_y", [P, D])
        idx = [f.sb(f"ex_idx{b}", [P, NSLOT], U32) for b in range(2)]
        idxT, gT = f.sb("ex_idxT", [P, NS], U32), f.sb("ex_gT", [P, NS])
        nsel = f.sb("ex_nsel", [NS, NS, P])
        wm = f.sb("ex_wm", [P, NS, NS])
        a, t, uu, w = (f.sb("ex_" + n, [P, NSLOT]) for n in ("a", "t", "u", "w"))
        dg = f.sb("ex_diag", [P, NSLOT, P])
        rs, sq_junk = f.sb("ex_rs", [P, 2]), f.sb("ex_sq_junk", [P, D])
        zb, zr = f.sb("ex_zero", [P, P], BF16), f.sb("ex_zero_row", [P, 512], BF16)
        acc = f.ps("ex_acc", [P, 2, 512])
        bc = [f.ps(f"ex_bc{n}", [P, 2, 512]) for n in range(2)]
        tp = f.ps("ex_tp", [P, 2 * NS])
        ident = misc[:, C_ID:C_ID + P]
        eye8 = misc[:, C_PICK + NS * NS:C_PICK + 2 * NS * NS].rearrange("p (n m) -> p n m", m=NS)
        accf = acc[:, :, :].rearrange("p b n -> p (b n)")
        SL = slice(0, NS)

        with nc.Block() as block:
            @block.sync
            def _(sp):
                sp.dma_start(g2m[:, 0, :], k.mod[0:1, 5 * D:6 * D].to_broadcast([P, D])).then_inc(s["mod"], 16)
                sp.dma_start(g2m[SL, 1, :], k.mod[1:1 + NS, 5 * D:6 * D]).then_inc(s["mod"], 16)
                sp.dma_start(fg[:, :], k.i["final_g"].to_broadcast([P, D])).then_inc(s["mod"], 16)
                sp.dma_start(h2[SL, :], k.h2[SEQ:ROWS, :]).then_inc(s["h2s"], 16)
                sp.dma_start(x1[SL, :], k.x1[SEQ:ROWS, :]).then_inc(s["mod"], 16)
                sp.wait_ge(s["y"], 1)
                sp.dma_start(k.o["y_sample"][:, 0, :], y[SL, :]).then_inc(s["y_out"], 16)
                sp.wait_ge(s["y_out"], 16)

            @block.gpsimd
            def _(pool):
                pool.wait_ge(s["idxT"], 1)
                for n in range(NS):
                    pool.indirect_dma_start(out=U[n][:, :], out_offset=None, in_=u_dram, in_offset=bass.IndirectOffsetOnAxis(ap=idxT[:, n:n + 1], axis=0)).then_inc(us[n], 16)
                    pool.indirect_dma_start(out=V[n][:, :], out_offset=None, in_=v_dram, in_offset=bass.IndirectOffsetOnAxis(ap=idxT[:, n:n + 1], axis=0)).then_inc(vs[n], 16)

            @block.tensor
            def _(pe):
                nc.tensor.transpose(tp[:, 0:NS], k.idx_s[:, :], ident[SL, SL])
                nc.tensor.transpose(tp[:, NS:2 * NS], k.gate_s[:, :], ident[SL, SL]).then_inc(s["idxT_ps"], 1)
                pe.wait_ge(s["h2s"], 16)
                pe.wait_ge(s["nsel"], 1)
                for n in range(NS):
                    at_least(pe, s["dots"], n - 1)
                    for b in range(2):
                        last = nc.tensor.matmul(bc[n % 2][:, b, :], nsel[:, n, :], h2[SL, b * 512:(b + 1) * 512], start=True, stop=True)
                    last.then_inc(s["bc"], 1)
                pe.wait_ge(s["wm"], 1)
                for n in range(NS):
                    pe.wait_ge(vs[n], 16)
                for b in range(2):
                    for n in range(NS):
                        last = nc.tensor.matmul(acc[SL, b, :], wm[:, n, :], V[n][:, b * 512:(b + 1) * 512], start=(n == 0), stop=(n == NS - 1))
                last.then_inc(s["s_sum"], 1)

            @block.scalar
            def _(act):
                act.wait_ge(s["s_u"], 1)
                nc.scalar.activation(uu[:, SL], uu[:, SL], ACT.Exp, scale=-2 * GELU_C).then_inc(s["s_exp"], 1)
                act.wait_ge(s["x1"], 1)
                nc.scalar.activation(junk[SL, :], y[SL, :], ACT.Square, accum_out=rs[SL, 0:1]).then_inc(s["sq"], 1)
                act.wait_ge(s["var"], 1)
                nc.scalar.activation(rs[SL, 1:2], rs[SL, 0:1], ACT.Sqrt).then_inc(s["root"], 1)

            @block.vector
            def _(dve):
                link = chained(dve, s["steps"])
                nc.vector.tensor_copy(nsel[:, :, :], ident[SL, SL].unsqueeze(2).to_broadcast([NS, NS, P])).then_inc(s["nsel"], 1)
                dve.wait_ge(s["idxT_ps"], 1)
                link(nc.vector.tensor_copy(gT[:, :], tp[:, NS:2 * NS]))
                nc.vector.tensor_copy(idxT[:, :], tp[:, 0:NS]).then_inc(s["idxT"], 1)
                for n in range(NS):
                    dve.wait_ge(s["bc"], n + 1)
                    dve.wait_ge(us[n], 16)
                    nc.vector.tensor_tensor_reduce(out=U[n][:, :], in0=U[n][:, :], in1=bc[n % 2][:, :, :].rearrange("p b n -> p (b n)"), scale=1.0, scalar=0.0,
                                                   op0=ALU.mult, op1=ALU.add, accum_out=a[:, n:n + 1]).then_inc(s["dots"], 1)
                dve.wait_ge(s["dots"], NS)
                gelu_steps(nc, link, a[:, SL], t[:, SL], uu[:, SL]).then_inc(s["s_u"], 1)
                dve.wait_ge(s["s_exp"], 1)
                link(nc.vector.tensor_scalar_add(uu[:, SL], uu[:, SL], 1.0))
                link(nc.vector.reciprocal(t[:, SL], uu[:, SL]))
                link(nc.vector.tensor_tensor(t[:, SL], t[:, SL], a[:, SL], ALU.mult))
                link(nc.vector.tensor_tensor(t[:, SL], t[:, SL], gT[:, :], ALU.mult))
                nc.vector.tensor_tensor(wm[:, :, :], t[:, SL].unsqueeze(2).to_broadcast([P, NS, NS]), eye8, ALU.mult).then_inc(s["wm"], 1)
                dve.wait_ge(s["mod"], 64)
                dve.wait_ge(s["s_sum"], 1)
                link(nc.vector.tensor_tensor(y[SL, :], accf[SL, :], g2m[SL, 1, :], ALU.mult))
                nc.vector.tensor_tensor(y[SL, :], y[SL, :], x1[SL, :], ALU.add).then_inc(s["x1"], 1)
                dve.wait_ge(s["sq"], 1)
                link(nc.vector.tensor_scalar(rs[SL, 0:1], rs[SL, 0:1], 1.0 / D, EPS, ALU.mult, ALU.add))
                nc.vector.reciprocal(rs[SL, 0:1], rs[SL, 0:1]).then_inc(s["var"], 1)
                dve.wait_ge(s["root"], 1)
                nc.vector.scalar_tensor_tensor(out=y[SL, :], in0=y[SL, :], scalar=rs[SL, 1:2], in1=fg[SL, :], op0=ALU.mult, op1=ALU.mult).then_inc(s["y"], 1)

        p = {n: k.sem("ep_" + n) for n in ("h2_l", "x1_l", "dotted", "g_steps", "g_u", "g_exp", "w", "diag", "vdone", "zero", "acc_t", "x2", "sq", "v_steps", "root", "y",
                                           "y_out", "summed", "staged", "dots_done")}
        with nc.Block() as block:
            @block.sync
            def _(sp):
                def tile(i):
                    rows, last_dot, t1 = early(sp, i * P), early(sp, i * (PH * NSLOT)), early(sp, i)
                    at_least(sp, p["dots_done"], last_dot)
                    sp.dma_start(h2[:, :], k.h2[bass.ds(rows, P), :]).then_inc(p["h2_l"], 16)
                    at_least(sp, p["x2"], t1)
                    sp.dma_start(x1[:, :], k.x1[bass.ds(rows, P), :]).then_inc(p["x1_l"], 16)
                first_then_loop(sp, TILES, tile)

            @block.gpsimd
            def _(pool):
                def head(i, pair, b):
                    h = pair * 2 + b
                    nc.gpsimd.tensor_copy(idx[b][:, :], k.idx[:, bass.ds(i * P + h * NSLOT, NSLOT)]).then_inc(p["staged"], 1)
                    pool.wait_ge(p["staged"], i * PH + h + 1)
                    for table, buf, used, loaded in ((u_dram, U, "dotted", ul), (v_dram, V, "vdone", vl)):
                        for n in range(NSLOT):
                            if n % GRP == 0:
                                pool.wait_ge(p[used], (i * PH + h) * NSLOT + n + GRP)
                                pool.sem_inc(p["zero"], 1)
                            pool.indirect_dma_start(out=buf[n][:, :], out_offset=None, in_=table,
                                                    in_offset=bass.IndirectOffsetOnAxis(ap=idx[b][:, n:n + 1], axis=0)).then_inc(loaded[n // GRP], 16)

                with pool.Fori(0, TILES) as i:
                    with pool.Fori(0, PH // 2) as pair:
                        for b in range(2):
                            head(i, pair, b)

            @block.tensor
            def _(pe):
                pe.sem_inc(p["vdone"], NSLOT)
                pe.wait_ge(s["tiles_done"], 2)
                with pe.Fori(0, TILES) as i:
                    pe.wait_ge(p["acc_t"], i + 1)
                    for b in range(2):
                        nc.tensor.matmul(acc[:, b, :], zb[:, :], zr[:, :], start=True, stop=False)
                    with pe.Fori(0, PH) as h:
                        for n in range(NSLOT):
                            if n % GRP == 0:
                                pe.wait_ge(vl[n // GRP], (i * PH + h) * (16 * GRP) + 16 * GRP)
                            pe.wait_ge(p["diag"], (i * PH + h) * NSLOT + n + 1)
                            for b in range(2):
                                last = nc.tensor.matmul(acc[:, b, :], dg[:, n, :], V[n][:, b * 512:(b + 1) * 512], start=False, stop=False)
                            last.then_inc(p["vdone"], 1)
                    for b in range(2):
                        last = nc.tensor.matmul(acc[:, b, :], zb[:, :], zr[:, :], start=False, stop=True)
                    last.then_inc(p["summed"], 1)

            @block.scalar
            def _(act):
                def head(i, h):
                    act.wait_ge(p["g_u"], i * PH + h + 1)
                    nc.scalar.activation(uu[:, :], uu[:, :], ACT.Exp, scale=-2 * GELU_C).then_inc(p["g_exp"], 1)
                    act.wait_ge(p["w"], i * PH + h + 1)
                    for n in range(NSLOT):
                        act.wait_ge(p["vdone"], (i * PH + h) * NSLOT + n + 1)
                        nc.scalar.activation(dg[:, n, :], ident, ACT.Copy, scale=w[:, n:n + 1]).then_inc(p["diag"], 1)

                def tail(i):
                    act.wait_ge(p["x2"], i + 1)
                    nc.scalar.activation(sq_junk[:, :], y[:, :], ACT.Square, accum_out=rs[:, 0:1]).then_inc(p["sq"], 1)
                    act.wait_ge(p["v_steps"], 2 * i + 2)
                    nc.scalar.activation(rs[:, 1:2], rs[:, 0:1], ACT.Sqrt).then_inc(p["root"], 1)
                    act.wait_ge(p["y"], i + 1)
                    act.dma_start(k.o["y_prompt"][0, bass.ds(i * P, P), :], y[:, :]).then_inc(p["y_out"], 16)

                def tile(i):
                    head(i, 0)
                    if not (isinstance(i, int) and i == 0):
                        tail(i - 1)
                    with act.Fori(1, PH) as h:
                        head(i, h)
                first_then_loop(act, TILES, tile)
                tail(TILES - 1)
                act.wait_ge(p["y_out"], 16 * TILES)

            @block.vector
            def _(dve):
                nc.vector.memset(zb[:, :], 0.0).then_inc(s["tiles_done"], 1)
                nc.vector.memset(zr[:, :], 0.0).then_inc(s["tiles_done"], 1)
                dve.sem_inc(p["dotted"], NSLOT)
                dve.sem_inc(p["acc_t"], 1)

                def head(i, h):
                    for n in range(NSLOT):
                        if n % GRP == 0:
                            dve.wait_ge(ul[n // GRP], (i * PH + h) * (16 * GRP) + 16 * GRP)
                        nc.vector.tensor_tensor_reduce(out=U[n][:, :], in0=U[n][:, :], in1=h2[:, :], scale=1.0, scalar=0.0, op0=ALU.mult, op1=ALU.add,
                                                       accum_out=a[:, n:n + 1]).then_inc(p["dotted"], 1)
                    dve.wait_ge(p["dotted"], (i * PH + h) * NSLOT + 2 * NSLOT)
                    dve.sem_inc(p["dots_done"], NSLOT)
                    link = chained(dve, p["g_steps"], (i * PH + h) * 6)
                    gelu_steps(nc, link, a[:, :], t[:, :], uu[:, :]).then_inc(p["g_u"], 1)
                    dve.wait_ge(p["g_exp"], i * PH + h + 1)
                    link(nc.vector.tensor_scalar_add(uu[:, :], uu[:, :], 1.0))
                    link(nc.vector.reciprocal(t[:, :], uu[:, :]))
                    link(nc.vector.tensor_tensor(t[:, :], t[:, :], a[:, :], ALU.mult))
                    gate = k.gate[:, bass.ds(i * P + h * NSLOT, NSLOT)]
                    at_least(dve, p["diag"], (i * PH + h) * NSLOT)
                    nc.vector.tensor_tensor(w[:, :], t[:, :], gate, ALU.mult).then_inc(p["w"], 1)

                def tail(i):
                    dve.wait_ge(p["summed"], i + 1)
                    dve.wait_ge(p["x1_l"], 16 * i + 16)
                    at_least(dve, p["y_out"], 16 * i)
                    nc.vector.tensor_tensor(y[:, :], accf, g2m[:, 0, :], ALU.mult).then_inc(p["acc_t"], 1)
                    dve.wait_ge(p["acc_t"], i + 2)
                    nc.vector.tensor_tensor(y[:, :], y[:, :], x1[:, :], ALU.add).then_inc(p["x2"], 1)
                    dve.wait_ge(p["sq"], i + 1)
                    link = chained(dve, p["v_steps"], 2 * i)
                    link(nc.vector.tensor_scalar(rs[:, 0:1], rs[:, 0:1], 1.0 / D, EPS, ALU.mult, ALU.add))
                    link(nc.vector.reciprocal(rs[:, 0:1], rs[:, 0:1]))
                    dve.wait_ge(p["root"], i + 1)
                    nc.vector.scalar_tensor_tensor(out=y[:, :], in0=y[:, :], scalar=rs[:, 1:2], in1=fg[:, :], op0=ALU.mult, op1=ALU.mult).then_inc(p["y"], 1)

                def tile(i):
                    dve.wait_ge(p["h2_l"], 16 * i + 16)
                    head(i, 0)
                    if not (isinstance(i, int) and i == 0):
                        tail(i - 1)
                    with dve.Fori(1, PH) as h:
                        head(i, h)
                first_then_loop(dve, TILES, tile)
                tail(TILES - 1)



def program(nc, ins, outs):
    with ExitStack() as stack:
        k = Ctx(nc, stack, ins, outs, {n: nc.inline_tensor(a, "table_" + n).ap() for n, a in constants().items()})
        misc = stack.enter_context(nc.sbuf_tensor("misc", [P, C_W], F32))
        modulation(k, misc)
        norm_and_project(k, misc)
        k.clear_sems()
        prompt_mixers(k, misc)
        k.clear_sems()
        sample_mixers(k, misc)
        k.clear_sems()
        k.idx = stack.enter_context(nc.sbuf_tensor("expert_idx", [P, SEQ], U32))
        k.gate = stack.enter_context(nc.sbuf_tensor("expert_gate", [P, SEQ], F32))
        k.idx_s = stack.enter_context(nc.sbuf_tensor("expert_idx_sample", [NS, P], F32))
        k.gate_s = stack.enter_context(nc.sbuf_tensor("expert_gate_sample", [NS, P], F32))
        merge_and_route(k, misc)
        k.clear_sems()
        experts(k, misc)
        k.clear_sems()
        with nc.Block() as block:
            @block.sync
            def _(sp):
                sp.wait_ge(k.cachecopy, 16 * NS * NG)


INS = ['x_prompt', 'x_sample', 'c_prompt', 'c_sample', 'state_gla', 'cache_kv_w128', 'cache_kv_w512', 'cache_kv_w2048',
       'ada_w', 'ada_b', 'norm1_g', 'w_in', 'gla_a_w2', 'gla_a_b', 'gla_gn_g', 'w_branch_a', 'w_branch_b', 'w_out',
       'norm2_g', 'peer_wq', 'peer_k1', 'peer_k2', 'peer_u', 'peer_v', 'final_g']
OUTS = [("y_prompt", (1, SEQ, D)), ("y_sample", (NS, 1, D)), ("state_prompt", (1, 1, GH, GK, GV)), ("state_sample", (1, NS, GH, GK, GV)),
        ("kv_w128_prompt", (1, 1, 128, 2, AH, HD)), ("kv_w128_sample", (1, NS, 128, 2, AH, HD)),
        ("kv_w512_prompt", (1, 1, 512, 2, AH, HD)), ("kv_w512_sample", (1, NS, 512, 2, AH, HD)),
        ("kv_w2048_prompt", (1, 1, SEQ, 2, AH, HD)), ("kv_w2048_sample", (1, NS, 2048, 2, AH, HD))]


def kernel(**inputs):
    import concourse.bacc as bacc
    from concourse.bass_utils import run_bass_kernel_spmd as run

    nc = bacc.Bacc("TRN2", target_bir_lowering=False, num_devices=1)
    arrays, ins, outs = {}, {}, {}
    for name in INS:
        a = np.ascontiguousarray(inputs[name])
        if name in ("peer_u", "peer_v"):
            a = a[0]
        if name == "final_g":
            a = a[None, :]
        arrays["in_" + name] = a
        ins[name] = nc.dram_tensor("in_" + name, a.shape, mybir.dt.from_np(a.dtype), kind="ExternalInput").ap()
    for name, shape in OUTS:
        outs[name] = nc.dram_tensor("out_" + name, shape, F32, kind="ExternalOutput").ap()
    program(nc, ins, outs)
    r = run(nc, [arrays], core_ids=[0])
    return tuple(r.results[0]["out_" + name] for name, _ in OUTS)
```

```python
from contextlib import ExitStack

import numpy as np
import concourse.bass as bass
from concourse import mybir
from concourse.alu_op_type import AluOpType as ALU

F32 = mybir.dt.float32
BF16 = mybir.dt.bfloat16
U32 = mybir.dt.uint32
ACT = mybir.ActivationFunctionType
AX = mybir.AxisListType

P = 128
D = 1024
KD = D // P
SEQ = 1024
TILES = SEQ // P
NS = 8
ROWS = SEQ + NS
PAST = 2048
GH, GK, GV = 4, 128, 256
GC = 64
RANK = 16
TAU = 16.0
GROUPS = ((128, 1), (512, 4), (2048, 16))
AH, HD = 4, 128
NG = len(GROUPS)
QH = NG * AH
ROT = HD // 4 // 2
THETA = 500000.0
PH, NK, DQ, TOPK = 8, 128, 128, 16
EPS = 1e-6
QA, KA = 0, GH * GK
VA = 2 * GH * GK
RA = VA + GH * GV
ALR = RA + GH * GV
QB = ALR + RANK
KB = QB + QH * HD
VB = KB + QH * HD
GZA = VB + QH * HD
GZB = GZA + D
INW = GZB + D
SCALE_A = GK ** -0.5
SCALE_B = HD ** -0.5
MASKED = -1e30


def at_least(eng, sem, value):
    if not isinstance(value, int) or value > 0:
        eng.wait_ge(sem, value)


def early(eng, value):
    if not isinstance(value, int):
        eng.compute_val(value)
    return value


def first_then_loop(eng, n, body):
    body(0)
    with eng.Fori(1, n) as i:
        body(i)


def chained(eng, sem, base=0):
    count = [0]

    def link(ins):
        count[0] += 1
        ins.then_inc(sem, 1)
        eng.wait_ge(sem, base + count[0])
    link.count = count
    return link


def constants():
    half = np.arange(ROT, dtype=np.float32)
    inv = np.power(np.float32(THETA), -half / np.float32(ROT)).astype(np.float32)
    pos = np.concatenate([np.arange(SEQ), np.full(NS, PAST)]).astype(np.float32)
    ang = (pos[:, None] * inv[None, :]).astype(np.float32)
    rope = np.concatenate([np.cos(ang), np.sin(ang)], axis=1).astype(np.float32)
    tq = np.arange(P)[:, None]

    def band(width, dil, ahead, n):
        dist = tq - (np.arange(n)[None, :] - ahead)
        ok = (dist >= 0) & (dist <= width) & (dist % dil == 0)
        return np.where(ok, 0.0, MASKED).astype(np.float32)

    masks = np.concatenate([band(2048, 16, 896, 1920), band(512, 4, 512, 1152), band(128, 1, 128, 384)], axis=1)
    s, t = np.arange(P)[:, None], np.arange(P)[None, :]
    causal = ((s <= t) & (s // GC == t // GC)).astype(np.float32)
    restart = np.ones((P, P), np.float32)
    restart[:, ::GC] = 0.0
    pick = np.zeros((P, P), np.float32)
    pick[:NS, :NS * NS] = (np.arange(NS)[:, None] == (np.arange(NS * NS) // NS)[None, :])
    pick[:, NS * NS:] = np.eye(NS, dtype=np.float32).reshape(1, NS * NS)
    slot = np.tile(np.arange(TOPK, dtype=np.float32)[None, :], (P, 1))
    misc = np.concatenate([np.eye(P, dtype=np.float32), causal, restart, pick, slot], axis=1)
    return {"rope": rope, "masks": masks, "misc": misc}


WIN, WIN_BUFS = 464, 3
C_ID, C_CAUSAL, C_RESTART, C_PICK, C_SLOT = 0, 128, 256, 384, 512
C_W = 528


class Ctx:

    def __init__(self, nc, stack, ins, outs, consts):
        self.nc, self.stack = nc, stack
        self.i, self.o, self.c = ins, outs, consts
        self.phase_sems = []
        self.z = nc.dram_tensor("z_scratch", (ROWS, INW), F32).ap()
        self.mod = nc.dram_tensor("mod_scratch", (1 + NS, 6 * D), F32).ap()
        self.mix = nc.dram_tensor("mix_scratch", (ROWS, GH * GV + AH * HD), F32).ap()
        self.x1 = nc.dram_tensor("x1_scratch", (ROWS, D), F32).ap()
        self.h2 = nc.dram_tensor("h2_scratch", (ROWS, D), F32).ap()

    def sem(self, name, kept=False):
        handle = self.nc.alloc_semaphore(name)
        if not kept:
            self.phase_sems.append(handle)
        return handle

    def clear_sems(self):
        self.nc.clear_and_free_semaphores(self.phase_sems)
        self.nc.all_engine_barrier()
        self.phase_sems = []

    def phase(self):
        return Phase(self)


class Phase:

    def __init__(self, k):
        self.k, self.stack = k, ExitStack()

    def __enter__(self):
        return self

    def __exit__(self, *a):
        return self.stack.__exit__(*a)

    def sb(self, name, shape, dt=F32):
        return self.stack.enter_context(self.k.nc.sbuf_tensor(name, shape, dt))

    def ps(self, name, shape, dt=F32):
        return self.stack.enter_context(self.k.nc.psum_tensor(name, shape, dt))


def modulation(k, misc):
    nc = k.nc
    NB, U, W = 12, 3, 512
    M = 1 + NS
    c_in, w_in_ = k.sem("mod_c_loaded"), [k.sem(f"mod_w_loaded{u}") for u in range(U)]
    cachecopy = k.sem("cache_rows_copied", kept=True)
    act_s, silu_s, tps, tsb = k.sem("mod_exp_done"), k.sem("mod_silu_steps"), k.sem("mod_cT_psum"), k.sem("mod_cT_ready")
    prod, summed, stored = k.sem("mod_product"), k.sem("mod_summed"), k.sem("mod_stored")
    k.cachecopy = cachecopy
    k.x_loaded, k.win_loaded = k.sem("n1_x_loaded"), [k.sem(f"win_loaded{u}") for u in range(WIN_BUFS)]
    with k.phase() as f:
        c9, e9, s9 = f.sb("c9", [M, D]), f.sb("e9", [M, D]), f.sb("s9", [M, D])
        cT = f.sb("cT", [P, KD, M])
        w = [f.sb(f"ada{u}", [P, KD, W]) for u in range(U)]
        bias, mod = f.sb("ada_bias", [M, 6 * D]), f.sb("mod_sb", [M, 6 * D])
        pT = f.ps("cT_ps", [P, KD, 16])
        pm = [f.ps(f"mod_ps{u}", [M, W]) for u in range(U)]
        wv = k.i["ada_w"][0].rearrange("(k p) n -> p k n", p=P)
        with nc.Block() as block:
            @block.sync
            def _(sp):
                sp.dma_start(c9[0:1, :], k.i["c_prompt"]).then_inc(c_in, 16)
                sp.dma_start(c9[1:M, :], k.i["c_sample"]).then_inc(c_in, 16)
                sp.dma_start(misc[:, :], k.c["misc"]).then_inc(c_in, 16)
                sp.dma_start(bias[:, :], k.i["ada_b"].to_broadcast([M, 6 * D])).then_inc(c_in, 16)

                def step(j):
                    for u in range(U):
                        at_least(sp, prod, j * U + u + 1 - U)
                        sp.dma_start(w[u][:, :, :], wv[:, :, bass.ds(j * (U * W) + u * W, W)]).then_inc(w_in_[u], 16)
                first_then_loop(sp, NB // U, step)
                sp.dma_start(k.x_rows[:, 0:TILES, :], k.i["x_prompt"][0].rearrange("(t p) d -> p t d", p=P)).then_inc(k.x_loaded, 16)
                sp.dma_start(k.x_rows[0:NS, TILES, :], k.i["x_sample"][:, 0, :]).then_inc(k.x_loaded, 16)
                for u in range(WIN_BUFS):
                    sp.dma_start(k.win[u][:, :, :], k.i["w_in"][0].rearrange("(k p) n -> p k n", p=P)[:, :, u * WIN:(u + 1) * WIN]).then_inc(k.win_loaded[u], 16)
                sp.wait_ge(summed, NB)
                sp.dma_start(k.mod, mod[:, :]).then_inc(stored, 16)
                sp.wait_ge(stored, 16)

            @block.scalar
            def _(act):
                act.wait_ge(c_in, 64)
                nc.scalar.activation(e9[:, :], c9[:, :], ACT.Exp, scale=-1.0).then_inc(act_s, 1)

            @block.vector
            def _(dve):
                dve.wait_ge(act_s, 1)
                link = chained(dve, silu_s)
                link(nc.vector.tensor_scalar_add(e9[:, :], e9[:, :], 1.0))
                link(nc.vector.reciprocal(s9[:, :], e9[:, :]))
                link(nc.vector.tensor_tensor(s9[:, :], s9[:, :], c9[:, :], ALU.mult))
                dve.wait_ge(tps, 1)
                nc.vector.tensor_copy(cT[:, :, :], pT[:, :, 0:M]).then_inc(tsb, 1)

                def step(j):
                    for u in range(U):
                        dve.wait_ge(prod, j * U + u + 1)
                        cols = bass.ds(j * (U * W) + u * W, W)
                        nc.vector.tensor_tensor(mod[:, cols], pm[u][:, :], bias[:, cols], ALU.add).then_inc(summed, 1)
                first_then_loop(dve, NB // U, step)

            @block.tensor
            def _(pe):
                pe.wait_ge(silu_s, 3)
                for c in range(KD):
                    last = nc.tensor.transpose(pT[:, c, 0:M], s9[:, c * P:(c + 1) * P], misc[0:M, C_ID:C_ID + M])
                last.then_inc(tps, 1)
                pe.wait_ge(tsb, 1)

                def step(j):
                    for u in range(U):
                        pe.wait_ge(w_in_[u], 16 * j + 16)
                        at_least(pe, summed, j * U + u + 1 - U)
                        for c in range(KD):
                            last = nc.tensor.matmul(pm[u][:, :], cT[:, c, :], w[u][:, c, :], start=(c == 0), stop=(c == KD - 1))
                        last.then_inc(prod, 1)
                first_then_loop(pe, NB // U, step)


def norm_and_project(k, misc):
    nc = k.nc
    W, U = WIN, WIN_BUFS
    STEPS = INW // W
    assert STEPS * W == INW and STEPS % U == 0
    x_in, sqs, steps, h_made, hps, hev = (k.sem("n1_" + n) for n in ("loaded", "squares", "steps", "h_made", "hT_psum", "hT_ready"))
    gm_s, root = k.sem("n1_gain_steps"), k.sem("n1_root")
    w_l = k.win_loaded
    prod, evac, used, zout = k.sem("z_product"), k.sem("z_evacuated"), k.sem("win_used"), [k.sem(f"z_stored{u}") for u in range(U)]
    with k.phase() as f:
        hT = f.sb("hT", [P, KD, ROWS])
        w = k.win
        wv = k.i["w_in"][0].rearrange("(k p) n -> p k n", p=P)
        with k.phase() as f1:
            xs = k.x_rows
            mods = f1.sb("n1_mod", [P, 2, 2, D])
            g = f1.sb("n1_g", [P, D])
            junk, h = f1.sb("n1_junk", [P, 2, D]), f1.sb("n1_h", [P, 2, D])
            ss, rs = f1.sb("n1_ss", [P, TILES + 1]), f1.sb("n1_rs", [P, TILES + 1])
            pT = [f1.ps(f"hT_ps{b}", [P, KD, P]) for b in range(2)]
            with nc.Block() as block:
                @block.sync
                def _(sp):
                    sp.dma_start(mods[:, 0, :, :].rearrange("p a d -> p (a d)"), k.mod[0:1, 0:2 * D].to_broadcast([P, 2 * D])).then_inc(x_in, 16)
                    sp.dma_start(mods[0:NS, 1, :, :].rearrange("p a d -> p (a d)"), k.mod[1:1 + NS, 0:2 * D]).then_inc(x_in, 16)
                    sp.dma_start(g[:, :], k.i["norm1_g"].to_broadcast([P, D])).then_inc(x_in, 16)

                def rows_of(i):
                    return NS if isinstance(i, int) and i == TILES else P

                def all_tiles(eng, body):
                    body(0, 0)
                    body(1, 1)
                    with eng.Fori(1, TILES // 2) as j:
                        for b in range(2):
                            body(2 * j + b, b)
                    body(TILES, 0)

                @block.scalar
                def _(act):
                    act.wait_ge(k.x_loaded, 32)
                    act.wait_ge(gm_s, 1)
                    for i in range(TILES + 1):
                        R = rows_of(i)
                        at_least(act, sqs, i - 1)
                        nc.scalar.activation(junk[0:R, i % 2, :], xs[0:R, i, :], ACT.Square, accum_out=ss[0:R, i:i + 1]).then_inc(sqs, 1)
                    act.wait_ge(steps, 2)
                    nc.scalar.activation(rs[:, :], ss[:, :], ACT.Sqrt).then_inc(root, 1)

                    def tile(i, b):
                        R = rows_of(i)
                        act.wait_ge(hps, i + 1)
                        nc.scalar.copy(hT[:, :, bass.ds(i * P, R)], pT[b][:, :, 0:R]).then_inc(hev, 1)
                    all_tiles(act, tile)

                @block.vector
                def _(dve):
                    nc.vector.memset(ss[:, :], 1.0).then_inc(gm_s, 1)
                    dve.wait_ge(x_in, 48)
                    dve.wait_ge(k.x_loaded, 32)
                    for n, R in ((0, P), (1, NS)):
                        nc.vector.scalar_tensor_tensor(out=mods[0:R, n, 1, :], in0=mods[0:R, n, 1, :], scalar=1.0, in1=g[0:R, :],
                                                       op0=ALU.add, op1=ALU.mult).then_inc(gm_s, 1)
                    dve.wait_ge(gm_s, 3)
                    dve.wait_ge(sqs, TILES + 1)
                    link = chained(dve, steps)
                    link(nc.vector.tensor_scalar(ss[:, :], ss[:, :], 1.0 / D, EPS, ALU.mult, ALU.add))
                    link(nc.vector.reciprocal(ss[:, :], ss[:, :]))
                    dve.wait_ge(root, 1)

                    def tile(i, b):
                        R = rows_of(i)
                        n = 1 if R == NS else 0
                        if not isinstance(i, int) or i > 1:
                            dve.wait_ge(hps, i - 1)
                        link = chained(dve, steps, 2 + i)
                        link(nc.vector.scalar_tensor_tensor(out=h[0:R, b, :], in0=xs[0:R, i, :] if isinstance(i, int) else xs[:, bass.ds(i, 1), :].rearrange("p a d -> p (a d)"),
                                                            scalar=rs[0:R, bass.ds(i, 1)], in1=mods[0:R, n, 1, :], op0=ALU.mult, op1=ALU.mult))
                        nc.vector.tensor_tensor(h[0:R, b, :], h[0:R, b, :], mods[0:R, n, 0, :], ALU.add).then_inc(h_made, 1)
                    all_tiles(dve, tile)

                @block.tensor
                def _(pe):
                    def tile(i, b):
                        R = rows_of(i)
                        pe.wait_ge(h_made, i + 1)
                        if not isinstance(i, int) or i > 1:
                            pe.wait_ge(hev, i - 1)
                        for c in range(KD):
                            last = nc.tensor.transpose(pT[b][:, c, 0:R], h[0:R, b, c * P:(c + 1) * P], misc[0:R, C_ID:C_ID + R])
                        last.then_inc(hps, 1)
                    all_tiles(pe, tile)

        zst = [f.sb(f"z_stage{u}", [P, TILES + 1, W]) for u in range(U)]
        NBK = 3
        pz = [f.ps(f"z_ps{b}", [P, 512]) for b in range(NBK)]
        T1 = TILES + 1
        zp = k.z[0:SEQ, :].rearrange("(t p) n -> p t n", p=P)
        with nc.Block() as block:
            @block.sync
            def _(sp):
                def shift_caches(n):
                    for name, (width, _) in zip(("w128", "w512", "w2048"), GROUPS):
                        src = k.i["cache_kv_" + name][0, bass.ds(n, 1), 1:width].rearrange("n w a h d -> n (w a h d)")
                        dst = k.o["kv_" + name + "_sample"][0, bass.ds(n, 1), 0:width - 1].rearrange("n w a h d -> n (w a h d)")
                        sp.dma_start(dst.rearrange("n (p f) -> n p f", p=16), src.rearrange("n (p f) -> n p f", p=16)).then_inc(k.cachecopy, 16)
                with sp.Fori(1, STEPS // U) as j:
                    for u in range(U):
                        sp.wait_ge(used, j * U + u + 1 - U)
                        sp.dma_start(w[u][:, :, :], wv[:, :, bass.ds(j * (U * W) + u * W, W)]).then_inc(w_l[u], 16)
                    shift_caches(j)
                shift_caches(0)
                for n in range(STEPS // U, NS):
                    shift_caches(n)

            @block.scalar
            def _(act):
                def step(j):
                    for u in range(U):
                        at_least(act, zout[u], 32 * j)
                        for t in range(T1):
                            R = NS if t == TILES else P
                            act.wait_ge(prod, j * (U * T1) + u * T1 + t + 1)
                            nc.scalar.copy(zst[u][0:R, t, :], pz[t % NBK][0:R, 0:W]).then_inc(evac, 1)
                        act.wait_ge(evac, j * (U * T1) + (u + 1) * T1)
                        cols = bass.ds(j * (U * W) + u * W, W)
                        act.dma_start(zp[:, :, cols], zst[u][:, 0:TILES, :]).then_inc(zout[u], 16)
                        act.dma_start(k.z[SEQ:ROWS, cols], zst[u][0:NS, TILES, :]).then_inc(zout[u], 16)
                first_then_loop(act, STEPS // U, step)
                for u in range(U):
                    act.wait_ge(zout[u], 32 * (STEPS // U))

            @block.tensor
            def _(pe):
                def step(j):
                    for u in range(U):
                        pe.wait_ge(w_l[u], 16 * j + 16)
                        for t in range(T1):
                            R = NS if t == TILES else P
                            at_least(pe, evac, j * (U * T1) + u * T1 + t + 1 - NBK)
                            for c in range(KD):
                                last = nc.tensor.matmul(pz[t % NBK][0:R, 0:W], hT[:, c, t * P:t * P + R], w[u][:, c, :],
                                                        start=(c == 0), stop=(c == KD - 1))
                            last.then_inc(prod, 1)
                        nc.tensor.wait_ge(prod, j * (U * T1) + (u + 1) * T1)
                        pe.sem_inc(used, 1)
                first_then_loop(pe, STEPS // U, step)


def prompt_mixers(k, misc):
    nc = k.nc
    GW = GH * GV
    KT = TILES + 5 + 2
    NKEY = KT * P
    M1, M0 = 1920, 1920 + 1152
    s = {n: k.sem("mx_" + n) for n in (
        "const", "cast", "qkT_ps", "zg", "zq", "v", "init", "tr", "alr", "x", "xb", "ln", "ln_steps", "dec_steps", "exps", "qk", "gact", "gupd", "state",
        "squares", "var", "var_steps", "root", "normed", "ra_exp", "silu_e", "silu_steps", "mixa", "rope_steps", "roped", "scores", "max_steps", "negmax", "exp",
        "pv", "rinv", "heads", "kout", "outa", "outb", "vout", "final")}
    full = [k.sem("mx_T_full0"), k.sem("mx_T_full1")]
    free = [k.sem("mx_T_free0"), k.sem("mx_T_free1")]
    USES = 12
    with k.phase() as f:
        masks = f.sb("mx_masks", [P, 3456], BF16)
        identb = f.sb("mx_ident", [P, P], BF16)
        ropes = f.sb("mx_rope", [P, TILES, 2 * ROT])
        w2, ab, gn = f.sb("mx_w2", [RANK, GH * GK]), f.sb("mx_ab", [P, GH]), f.sb("mx_gn", [P, GW])
        zg, zq = f.sb("mx_zg", [P, QB]), f.sb("mx_zq", [P, 2 * QH, HD])
        kT, V = f.sb("mx_kT", [P, QH, SEQ]), f.sb("mx_V", [P, TILES, QH * HD])
        qT = f.sb("mx_qT", [P, QH, P])
        alrT, xb, xa = f.sb("mx_alrT", [RANK, P]), f.sb("mx_xb", [P, GH * P]), f.sb("mx_xa", [P, GH * P])
        B, d1, dl = f.sb("mx_B", [P, GH * P]), f.sb("mx_d1", [P, GH * P]), f.sb("mx_dl", [P, GH * P])
        E = [f.sb("mx_E0", [P, GH * P]), d1, f.sb("mx_E2", [P, GH * P]), dl]
        EL = f.sb("mx_EL", [P, 2 * GH])
        kp, kpp = f.sb("mx_kp", [P, GH * P]), f.sb("mx_kpp", [P, GH * P])
        attm, kTok = f.sb("mx_attm", [P, GH, P]), f.sb("mx_kTok", [P, GH, P])
        S = [f.sb("mx_S0", [P, GH, GV]), f.sb("mx_S1", [P, GH, GV])]
        gst = f.sb("mx_gst", [P, 2, GH])
        er, om = f.sb("mx_er", [P, GW]), f.sb("mx_om", [P, GW])
        Pm = f.sb("mx_P", [P, NKEY])
        PT = [f.sb(f"mx_PT{n}", [P, KT, P]) for n in range(2)]
        rt = PT[1][:, :, :].rearrange("p j t -> p (j t)")[:, 0:4 * 2 * QH * ROT].rearrange("p (n h r) -> p n h r", n=4, h=2 * QH)
        mx, nm, sm, ri = (f.sb("mx_" + n, [P, AH]) for n in ("max", "negm", "sum", "rinv"))
        ob = f.sb("mx_ob", [P, AH * HD])
        big = f.ps("mx_big", [P, 4, 512])
        Tb = [f.ps("mx_T0", [P, 512]), f.ps("mx_T1", [P, 512])]
        OM = [f.ps("mx_O", [P, 512]), f.ps("mx_M", [P, 512])]
        sc_all = big[:, :, :].rearrange("p b n -> p (b n)")
        qps = big[:, 0, :]
        kps = big[:, 1, :]
        v8 = lambda t: t[:, :].rearrange("p (n c) -> p n c", c=GC)
        causal = misc[:, C_CAUSAL:C_CAUSAL + P]
        restart = misc[:, C_RESTART:C_RESTART + P]
        ident = misc[:, C_ID:C_ID + P]
        vg = zg[:, VA:VA + GW]
        ra = zg[:, RA:RA + GW]

        def tiles(eng, body):
            body(0, 0, 0, 0, 0, False)
            with eng.Fori(1, 4) as i:
                body(i, 0, 0 - i, i - 1, -1, False)
            with eng.Fori(4, TILES - 1) as i:
                body(i, i - 4, -4, i - 1, -1, True)
            body(TILES - 1, TILES - 5, -4, TILES - 2, -1, True)

        def is_last(i):
            return isinstance(i, int) and i == TILES - 1

        with nc.Block() as block:
            @block.gpsimd
            def _(pool):
                pool.dma_start(masks[:, :], k.c["masks"]).then_inc(s["cast"], 16)
                pool.dma_start(identb[:, :], k.c["misc"][:, C_ID:C_ID + P]).then_inc(s["cast"], 16)
                nc.gpsimd.memset(S[0][:, :, :], 0.0).then_inc(s["init"], 1)
                nc.gpsimd.memset(kT[:, :, :], 0.0).then_inc(s["init"], 1)

            @block.sync
            def _(sp):
                def load_gla(rows):
                    sp.dma_start(zg[:, :], k.z[bass.ds(rows, P), 0:QB]).then_inc(s["zg"], 16)

                def load_qk(rows):
                    sp.dma_start(zq[:, :, :].rearrange("p h d -> p (h d)"), k.z[bass.ds(rows, P), QB:VB]).then_inc(s["zq"], 16)
                load_gla(0)
                sp.dma_start(ropes[:, :, :], k.c["rope"][0:SEQ, :].rearrange("(t p) n -> p t n", p=P)).then_inc(s["const"], 16)
                sp.dma_start(w2[:, :], k.i["gla_a_w2"][0]).then_inc(s["const"], 16)
                with nc.allow_non_contiguous_dma(reason="512 single values, once"):
                    sp.dma_start(ab[:, :], k.i["gla_a_b"][0].rearrange("(h p) -> p h", p=P)).then_inc(s["const"], 16)
                sp.dma_start(gn[:, :], k.i["gla_gn_g"].to_broadcast([P, GW])).then_inc(s["const"], 16)
                load_qk(0)
                sp.dma_start(V[:, :, :], k.z[0:SEQ, VB:GZA].rearrange("(t p) n -> p t n", p=P)).then_inc(s["v"], 16)
                for g, name in enumerate(("w128", "w512", "w2048")):
                    o = k.o["kv_" + name + "_prompt"][0, 0]
                    W = o.shape[0]
                    sp.dma_start(o[:, 1, :, :].rearrange("t h d -> t (h d)"),
                                 k.z[SEQ - W:SEQ, VB + g * AH * HD:VB + (g + 1) * AH * HD]).then_inc(s["vout"], 16)

                def tile(i, st1, lag1, st0, lag0, late):
                    one, rows, upds, turned = (early(sp, x) for x in (i + 1, i * P, 8 * i + 8, USES * i + 4))
                    next_rows, headed, keys_out = (early(sp, x) for x in (i * P + P, 4 * i + 4, 16 * (2 * i - 2) if late else 16 * (i + 1)))
                    old = early(sp, (i - 4) * P) if late else 0
                    sp.wait_ge(s["roped"], one)
                    sp.dma_start(k.o["kv_w2048_prompt"][0, 0, bass.ds(rows, P), 0, :, :], zq[:, QH + 8:QH + 12, :]).then_inc(s["kout"], 16)
                    if late:
                        sp.dma_start(k.o["kv_w512_prompt"][0, 0, bass.ds(old, P), 0, :, :], zq[:, QH + 4:QH + 8, :]).then_inc(s["kout"], 16)
                    sp.wait_ge(s["mixa"], one)
                    sp.dma_start(k.mix[bass.ds(rows, P), 0:GW], om[:, :]).then_inc(s["outa"], 16)
                    if not is_last(i):
                        sp.wait_ge(s["gupd"], upds)
                        load_gla(next_rows)
                        sp.wait_ge(full[0], turned)
                        sp.wait_ge(full[1], turned)
                        sp.wait_ge(s["kout"], keys_out)
                        load_qk(next_rows)
                    sp.wait_ge(s["heads"], headed)
                    sp.dma_start(k.mix[bass.ds(rows, P), GW:GW + AH * HD], ob[:, :]).then_inc(s["outb"], 16)
                tiles(sp, tile)
                sp.dma_start(k.o["kv_w128_prompt"][0, 0, :, 0, :, :], zq[:, QH:QH + 4, :]).then_inc(s["kout"], 16)
                sp.wait_ge(s["state"], 8 * TILES)
                sp.dma_start(k.o["state_prompt"][0, 0].rearrange("h k v -> k h v"), S[0][:, :, :]).then_inc(s["final"], 16)
                for name, n in (("final", 1), ("vout", 3), ("kout", 8 + 4 + 1), ("outa", TILES), ("outb", TILES)):
                    sp.wait_ge(s[name], 16 * n)

            @block.tensor
            def _(pe):
                pe.wait_ge(s["const"], 64)

                def turn_alr(n):
                    pe.wait_ge(s["zg"], 16 * n + 16)
                    nc.tensor.transpose(OM[0][0:RANK, 0:P], zg[:, ALR:ALR + RANK], ident).then_inc(s["tr"], 1)

                def gate_logits(n):
                    pe.wait_ge(s["alr"], n + 1)
                    for h in range(GH):
                        last = nc.tensor.matmul(OM[0][:, h * P:(h + 1) * P], w2[:, h * GK:(h + 1) * GK], alrT[:, :], start=True, stop=True)
                    last.then_inc(s["x"], 1)

                def turn_qk(i, banks):
                    for b in banks:
                        at_least(pe, free[b % 2], USES * i + 1 + b // 2)
                        for h in range(4):
                            last = nc.tensor.transpose(Tb[b % 2][:, h * P:(h + 1) * P], zq[:, 4 * b + h, :], ident)
                        last.then_inc(full[b % 2], 1)

                turn_alr(0)
                gate_logits(0)

                def tile(i, st1, lag1, st0, lag0, late):
                    pe.wait_ge(s["zg"], 16 * i + 16)
                    at_least(pe, s["exp"], 4 * i)
                    for h in range(GH):
                        nc.tensor.transpose(qps[:, h * P:(h + 1) * P], zg[:, QA + h * GK:QA + (h + 1) * GK], ident)
                        last = nc.tensor.transpose(kps[:, h * P:(h + 1) * P], zg[:, KA + h * GK:KA + (h + 1) * GK], ident)
                    last.then_inc(s["qkT_ps"], 1)
                    pe.wait_ge(s["qk"], 4 * i + 4)
                    at_least(pe, free[0], USES * i)
                    for h in range(GH):
                        last = nc.tensor.matmul(Tb[0][:, h * P:(h + 1) * P], kp[:, h * P:(h + 1) * P], E[0][:, h * P:(h + 1) * P], start=True, stop=True)
                    last.then_inc(full[0], 1)
                    at_least(pe, free[1], USES * i)
                    for h in range(GH):
                        last = nc.tensor.transpose(Tb[1][:, h * P:(h + 1) * P], kpp[:, h * P:(h + 1) * P], ident)
                    last.then_inc(full[1], 1)
                    pe.wait_ge(free[0], USES * i + 1)
                    pe.wait_ge(free[1], USES * i + 1)
                    upd = lambda h: OM[h // 2][:, (h % 2) * GV:(h % 2 + 1) * GV]
                    at_least(pe, s["state"], 8 * i)
                    at_least(pe, s["heads"], 4 * i)
                    if isinstance(i, int) and i == 0:
                        pe.wait_ge(s["init"], 2)
                    for h in range(GH):
                        nc.tensor.matmul(big[:, h, 0:GV], attm[:, h, :], vg[:, h * GV:(h + 1) * GV], start=True, stop=False)
                        nc.tensor.matmul(big[0:GC, h, 0:GV], E[2][:, h * P:h * P + GC], S[0][:, h, :], start=False, stop=True)
                        nc.tensor.matmul(upd(h), kTok[0:GC, h, :], vg[0:GC, h * GV:(h + 1) * GV], start=True, stop=True).then_inc(s["gupd"], 1)
                    pe.wait_ge(s["roped"], i + 1)
                    turn_qk(i, (0, 1))
                    for h in range(GH):
                        pe.wait_ge(s["state"], 8 * i + (h | 1) + 1)
                        nc.tensor.matmul(big[GC:P, h, 0:GV], E[2][:, h * P + GC:(h + 1) * P], S[1][:, h, :], start=False, stop=True)
                        nc.tensor.matmul(upd(h), kTok[GC:P, h, :], vg[GC:P, h * GV:(h + 1) * GV], start=True, stop=True).then_inc(s["gupd"], 1)
                    turn_qk(i, (2, 3, 4, 5))

                    def scores(h):
                        if h == 0:
                            pe.wait_ge(free[0], USES * i + 4)
                            pe.wait_ge(free[1], USES * i + 4)
                            pe.wait_ge(s["normed"], 4 * i + 4)
                        else:
                            pe.wait_ge(s["exp"], 4 * i + h)
                        for b in range(2):
                            nc.tensor.matmul(big[:, b, :], identb[:, :], masks[:, bass.ds(896 + 512 * b - P * i, 512)], start=True, stop=False)
                            nc.tensor.matmul(big[:, b, :], qT[:, 8 + h, :], kT[:, 8 + h, b * 512:(b + 1) * 512], start=False, stop=True)
                        for c, n in ((0, 512), (512, P)):
                            dst = big[:, 2 + c // 512, 0:n]
                            nc.tensor.matmul(dst, identb[:, :], masks[:, bass.ds(M1 + 512 + c + lag1 * P, n)], start=True, stop=False)
                            nc.tensor.matmul(dst, qT[:, 4 + h, :], kT[:, 4 + h, bass.ds(st1 * P + c, n)], start=False, stop=True)
                        dst = big[:, 3, P:3 * P]
                        nc.tensor.matmul(dst, identb[:, :], masks[:, bass.ds(M0 + P + lag0 * P, 2 * P)], start=True, stop=False)
                        nc.tensor.matmul(dst, qT[:, h, :], kT[:, h, bass.ds(st0 * P, 2 * P)], start=False, stop=True).then_inc(s["scores"], 1)

                    if isinstance(i, int) and i == 0:
                        pe.wait_ge(s["cast"], 32)
                        pe.wait_ge(s["v"], 16)
                    scores(0)
                    for h in range(AH):
                        if h + 1 < AH:
                            scores(h + 1)
                        else:
                            pe.wait_ge(s["exp"], 4 * i + h + 1)
                        for b in range(4):
                            at_least(pe, free[b % 2], USES * i + 4 + 2 * h + b // 2)
                            for j in range(4 * b, min(4 * b + 4, KT)):
                                last = nc.tensor.transpose(Tb[b % 2][:, (j % 4) * P:(j % 4 + 1) * P], Pm[:, j * P:(j + 1) * P], ident)
                            last.then_inc(full[b % 2], 1)
                        pe.wait_ge(free[0], USES * i + 6 + 2 * h)
                        pe.wait_ge(free[1], USES * i + 6 + 2 * h)
                        if h < 2:
                            pe.wait_ge(s["state"], 8 * i + 8)
                        else:
                            pe.wait_ge(s["heads"], 4 * i + h - 1)
                        if h == 1 and not is_last(i):
                            pe.wait_ge(s["heads"], 4 * i + 1)
                            turn_alr(i + 1)
                        if h == 2 and not is_last(i):
                            pe.wait_ge(s["xb"], 4 * i + 8)
                        for j in range(KT):
                            g, t = (2, j) if j < 8 else (1, st1 + j - 8) if j < 13 else (0, st0 + j - 13)
                            c0 = (g * AH + h) * HD
                            vv = V[:, bass.ds(t, 1), c0:c0 + HD].rearrange("p a d -> p (a d)")
                            last = nc.tensor.matmul(OM[h % 2][:, 0:HD], PT[h % 2][:, j, :], vv, start=(j == 0), stop=(j == KT - 1))
                        last.then_inc(s["pv"], 1)
                        if h == 1 and not is_last(i):
                            gate_logits(i + 1)
                tiles(pe, tile)

            @block.scalar
            def _(act):
                act.wait_ge(s["const"], 64)

                def copy_alr(n):
                    act.wait_ge(s["tr"], n + 1)
                    nc.scalar.copy(alrT[:, :], OM[0][0:RANK, 0:P]).then_inc(s["alr"], 1)

                def log_sigmoid(n):
                    act.wait_ge(s["xb"], 4 * n + 4)
                    link = chained(act, s["ln_steps"], 2 * n)
                    link(nc.scalar.activation(xa[:, :], xb[:, :], ACT.Abs))
                    link(nc.scalar.activation(xa[:, :], xa[:, :], ACT.Exp, scale=-1.0))
                    nc.scalar.activation(xa[:, :], xa[:, :], ACT.Ln, bias=1.0).then_inc(s["ln"], 1)

                def decay_factors(n):
                    act.wait_ge(s["dec_steps"], 8 * n + 8)
                    nc.scalar.activation(E[0][:, :], d1[:, :], ACT.Exp, scale=1.0 / TAU).then_inc(s["exps"], 1)
                    nc.scalar.activation(E[2][:, :], B[:, :], ACT.Exp, scale=1.0 / TAU).then_inc(s["exps"], 1)
                    at_least(act, s["state"], 8 * n)
                    nc.scalar.activation(EL[:, :], v8(B)[:, :, GC - 1:GC].rearrange("p n c -> p (n c)"), ACT.Exp, scale=1.0 / TAU).then_inc(s["exps"], 1)
                    nc.scalar.activation(E[1][:, :], d1[:, :], ACT.Exp, scale=-1.0 / TAU).then_inc(s["exps"], 1)
                    nc.scalar.activation(E[3][:, :], dl[:, :], ACT.Exp, scale=1.0 / TAU).then_inc(s["exps"], 1)

                def copy_qk(i, b):
                    act.wait_ge(full[1], USES * i + 2 + b // 2)
                    dst = qT[:, 4 * b:4 * b + 4, :] if b < 3 else kT[:, 4 * b - QH:4 * b - QH + 4, bass.ds(i * P, P)]
                    nc.scalar.copy(dst, Tb[1][:, :].rearrange("p (h t) -> p h t", h=4)).then_inc(free[1], 1)

                copy_alr(0)
                log_sigmoid(0)
                decay_factors(0)

                def tile(i, st1, lag1, st0, lag0, late):
                    act.wait_ge(s["zg"], 16 * i + 16)
                    at_least(act, s["mixa"], i)
                    nc.scalar.activation(er[:, :], ra, ACT.Exp, scale=-1.0).then_inc(s["ra_exp"], 1)
                    act.wait_ge(s["ra_exp"], i + 1)
                    nc.scalar.activation(er[:, :], er[:, :], ACT.Copy, bias=1.0).then_inc(s["silu_e"], 1)
                    act.wait_ge(full[1], USES * i + 1)
                    nc.scalar.copy(kTok[:, :, :].rearrange("p h d -> p (h d)"), Tb[1][:, :]).then_inc(free[1], 1)
                    copy_qk(i, 1)
                    act.wait_ge(s["gupd"], 8 * i + 8)
                    for h in range(GH):
                        nc.scalar.activation((xa, kpp)[h // 2][:, (h % 2) * GV:(h % 2 + 1) * GV], big[:, h, 0:GV], ACT.Square,
                                             accum_out=gst[:, 0, h:h + 1]).then_inc(s["squares"], 1)
                    copy_qk(i, 3)
                    act.wait_ge(s["var_steps"], 2 * i + 2)
                    nc.scalar.activation(gst[:, 1, :], gst[:, 0, :], ACT.Sqrt).then_inc(s["root"], 1)
                    copy_qk(i, 5)
                    for h in range(AH):
                        act.wait_ge(s["negmax"], 4 * i + h + 1)
                        if h:
                            act.wait_ge(full[0], USES * i + 4 + 2 * h)
                            act.wait_ge(full[1], USES * i + 4 + 2 * h)
                        nc.scalar.activation(Pm[:, :], sc_all[:, 0:NKEY], ACT.Exp, bias=nm[:, h:h + 1], scale=SCALE_B,
                                             accum_out=sm[:, h:h + 1]).then_inc(s["exp"], 1)
                        if h < 2:
                            at_least(act, s["pv"], 4 * i)
                        else:
                            act.wait_ge(s["pv"], 4 * i + h - 1)
                        for b in (1, 3):
                            n = min(4, KT - 4 * b)
                            act.wait_ge(full[1], USES * i + 5 + 2 * h + b // 2)
                            nc.scalar.copy(PT[h % 2][:, 4 * b:4 * b + n, :].rearrange("p j t -> p (j t)"), Tb[1][:, 0:n * P]).then_inc(free[1], 1)
                        if not is_last(i):
                            if h == 1:
                                copy_alr(i + 1)
                            elif h == 2:
                                log_sigmoid(i + 1)
                            elif h == 3:
                                decay_factors(i + 1)
                tiles(act, tile)

            @block.vector
            def _(dve):
                dve.wait_ge(s["const"], 64)

                def biased_logits(n):
                    dve.wait_ge(s["x"], n + 1)
                    for h in range(GH):
                        nc.vector.tensor_scalar(xb[:, h * P:(h + 1) * P], OM[0][:, h * P:(h + 1) * P], ab[:, h:h + 1], None, ALU.add).then_inc(s["xb"], 1)

                def log_decays(n):
                    dve.wait_ge(s["ln"], n + 1)
                    link = chained(dve, s["dec_steps"], 8 * n)
                    link(nc.vector.scalar_tensor_tensor(out=xb[:, :], in0=xb[:, :], scalar=0.0, in1=xa[:, :], op0=ALU.min, op1=ALU.subtract))
                    for h in range(GH):
                        link(nc.vector.tensor_tensor_scan(B[:, h * P:(h + 1) * P], restart, xb[:, h * P:(h + 1) * P], 0.0, ALU.mult, ALU.add))
                    return link

                def decay_arguments(link):
                    mid = v8(B)[:, :, GC // 2 - 1:GC // 2].to_broadcast([P, 2 * GH, GC])
                    end = v8(B)[:, :, GC - 1:GC].to_broadcast([P, 2 * GH, GC])
                    link(nc.vector.tensor_tensor(v8(d1), v8(B), mid, ALU.subtract))
                    link(nc.vector.tensor_scalar(d1[:, :], d1[:, :], 40 * TAU, -40 * TAU, ALU.min, ALU.max))
                    link(nc.vector.tensor_tensor(v8(dl), end, v8(B), ALU.subtract))

                def copy_qk(i, b):
                    dve.wait_ge(full[0], USES * i + 2 + b // 2)
                    dst = qT[:, 4 * b:4 * b + 4, :] if b < 3 else kT[:, 4 * b - QH:4 * b - QH + 4, bass.ds(i * P, P)]
                    nc.vector.tensor_copy(dst, Tb[0][:, :].rearrange("p (h t) -> p h t", h=4)).then_inc(free[0], 1)

                biased_logits(0)
                decay_arguments(log_decays(0))

                def tile(i, st1, lag1, st0, lag0, late):
                    dve.wait_ge(s["qkT_ps"], i + 1)
                    dve.wait_ge(s["exps"], 5 * i + 5)
                    nc.vector.scalar_tensor_tensor(out=E[0][:, :], in0=qps, scalar=SCALE_A, in1=E[0][:, :], op0=ALU.mult, op1=ALU.mult).then_inc(s["qk"], 1)
                    nc.vector.scalar_tensor_tensor(out=E[2][:, :], in0=qps, scalar=SCALE_A, in1=E[2][:, :], op0=ALU.mult, op1=ALU.mult).then_inc(s["qk"], 1)
                    nc.vector.tensor_tensor(kp[:, :], kps, E[1][:, :], ALU.mult).then_inc(s["qk"], 1)
                    nc.vector.tensor_tensor(kpp[:, :], kps, E[3][:, :], ALU.mult).then_inc(s["qk"], 1)
                    dve.wait_ge(full[0], USES * i + 1)
                    nc.vector.tensor_tensor(attm[:, :, :], Tb[0][:, :].rearrange("p (h t) -> p h t", h=GH),
                                            causal.unsqueeze(1).to_broadcast([P, GH, P]), ALU.mult).then_inc(free[0], 1)
                    dve.wait_ge(s["zq"], 16 * i + 16)
                    cos = ropes[:, bass.ds(i, 1), 0:ROT].to_broadcast([P, 2 * QH, ROT])
                    sin = ropes[:, bass.ds(i, 1), ROT:2 * ROT].to_broadcast([P, 2 * QH, ROT])
                    x1, x2 = zq[:, :, 0:ROT], zq[:, :, ROT:2 * ROT]
                    for n, (a, b) in enumerate(((x1, cos), (x2, sin), (x2, cos), (x1, sin))):
                        nc.vector.tensor_tensor(rt[:, n], a, b, ALU.mult).then_inc(s["rope_steps"], 1)
                    dve.wait_ge(s["rope_steps"], 5 * i + 4)
                    nc.vector.tensor_tensor(x1, rt[:, 0], rt[:, 1], ALU.subtract).then_inc(s["rope_steps"], 1)
                    nc.vector.tensor_tensor(x2, rt[:, 2], rt[:, 3], ALU.add).then_inc(s["roped"], 1)
                    dve.wait_ge(s["rope_steps"], 5 * i + 5)
                    dve.wait_ge(s["roped"], i + 1)
                    for c in range(2):
                        for h in range(GH):
                            dve.wait_ge(s["gupd"], 8 * i + 4 * c + (h | 1) + 1)
                            if c:
                                dve.wait_ge(s["state"], 8 * i + h + 1)
                            nc.vector.scalar_tensor_tensor(out=S[1 - c][:, h, :], in0=S[c][:, h, :], scalar=EL[:, 2 * h + c:2 * h + c + 1],
                                                           in1=OM[h // 2][:, (h % 2) * GV:(h % 2 + 1) * GV],
                                                           op0=ALU.mult, op1=ALU.add).then_inc(s["state"], 1)
                        copy_qk(i, 2 * c)
                    dve.wait_ge(s["silu_e"], i + 1)
                    link = chained(dve, s["silu_steps"], 2 * i)
                    link(nc.vector.reciprocal(er[:, :], er[:, :]))
                    link(nc.vector.tensor_tensor(er[:, :], er[:, :], ra, ALU.mult))
                    dve.wait_ge(s["squares"], 4 * i + 4)
                    link = chained(dve, s["var_steps"], 2 * i)
                    link(nc.vector.tensor_scalar(gst[:, 0, :], gst[:, 0, :], 1.0 / GV, EPS, ALU.mult, ALU.add))
                    link(nc.vector.reciprocal(gst[:, 0, :], gst[:, 0, :]))
                    dve.wait_ge(s["root"], i + 1)
                    at_least(dve, s["outa"], 16 * i)
                    for h in range(GH):
                        cols = slice(h * GV, (h + 1) * GV)
                        nc.vector.scalar_tensor_tensor(out=om[:, cols], in0=big[:, h, 0:GV], scalar=gst[:, 1, h:h + 1], in1=gn[:, cols],
                                                       op0=ALU.mult, op1=ALU.mult).then_inc(s["normed"], 1)
                    copy_qk(i, 4)
                    dve.wait_ge(s["normed"], 4 * i + 4)
                    nc.vector.tensor_tensor(om[:, :], om[:, :], er[:, :], ALU.mult).then_inc(s["mixa"], 1)

                    def row_max(h):
                        dve.wait_ge(s["scores"], 4 * i + h + 1)
                        nc.vector.reduce_max(mx[:, h:h + 1], sc_all[:, 0:NKEY], AX.X).then_inc(s["max_steps"], 1)
                        dve.wait_ge(s["max_steps"], 4 * i + h + 1)
                        nc.vector.tensor_scalar(nm[:, h:h + 1], mx[:, h:h + 1], -SCALE_B, None, ALU.mult).then_inc(s["negmax"], 1)
                    row_max(0)
                    for h in range(AH):
                        if h + 1 < AH:
                            row_max(h + 1)
                        if h < 2:
                            at_least(dve, s["pv"], 4 * i)
                        else:
                            dve.wait_ge(s["pv"], 4 * i + h - 1)
                        for b in (0, 2):
                            dve.wait_ge(full[0], USES * i + 5 + 2 * h + b // 2)
                            nc.vector.tensor_copy(PT[h % 2][:, 4 * b:4 * b + 4, :].rearrange("p j t -> p (j t)"), Tb[0][:, :]).then_inc(free[0], 1)
                        if h == 3 and not is_last(i):
                            link = log_decays(i + 1)
                        dve.wait_ge(s["exp"], 4 * i + h + 1)
                        nc.vector.reciprocal(ri[:, h:h + 1], sm[:, h:h + 1]).then_inc(s["rinv"], 1)
                        dve.wait_ge(s["rinv"], 4 * i + h + 1)
                        dve.wait_ge(s["pv"], 4 * i + h + 1)
                        if h == 0:
                            at_least(dve, s["outb"], 16 * i)
                        nc.vector.tensor_scalar(ob[:, h * HD:(h + 1) * HD], OM[h % 2][:, 0:HD], ri[:, h:h + 1], None, ALU.mult).then_inc(s["heads"], 1)
                        if h == 1 and not is_last(i):
                            biased_logits(i + 1)
                        if h == 3 and not is_last(i):
                            decay_arguments(link)
                tiles(dve, tile)


def sample_mixers(k, misc):
    nc = k.nc
    GW = GH * GV
    R = NS
    KV = 2 * AH * HD
    names = ("in", "kv", "state_in", "alr_ps", "alr", "x_ps", "x", "ln_steps", "ln", "la", "decay", "qT_ps", "qm", "ksel", "upd", "state",
             "sums", "sq", "var", "root", "silu_e", "mixa", "dve", "rope", "nsel", "qbc", "prod", "qk_done", "sT_ps", "sub", "exp", "p", "pT_ps", "pm", "pv",
             "mixb", "out", "state_out")
    s = {n: k.sem("sm_" + n) for n in names}
    kvl = [k.sem(f"sm_kv_loaded{n}") for n in range(NS)]
    stl = [k.sem(f"sm_state_loaded{n}") for n in range(NS)]
    with k.phase() as f:
        zs = f.sb("sm_z", [R, GZA])
        kv = f.sb("sm_kv", [P, NS * NG, KV])
        S = f.sb("sm_S", [P, NS * GH, GV])
        w2, ab, gn = f.sb("sm_w2", [RANK, GH * GK]), f.sb("sm_ab", [P, GH]), f.sb("sm_gn", [R, GW])
        rope = f.sb("sm_rope", [R, 2 * ROT])
        alrT, x, xa, EL = f.sb("sm_alrT", [RANK, R]), f.sb("sm_x", [P, GH, R]), f.sb("sm_xa", [P, GH, R]), f.sb("sm_EL", [P, GH, R])
        ksel = f.sb("sm_ksel", [R, 2, GH * GK])
        qT, qm = f.sb("sm_qT", [P, GH, R]), f.sb("sm_qm", [P, GH, NS, R])
        st = f.sb("sm_stats", [R, 2, GH])
        nsel = f.sb("sm_nsel", [R, NS, P])
        big = f.sb("sm_big", [R, 2048])
        er, om, ob = f.sb("sm_er", [R, GW]), f.sb("sm_om", [R, GW]), f.sb("sm_ob", [R, AH * HD])
        prod = f.sb("sm_prod", [P, 2, AH, HD])
        sc = f.sb("sm_sc", [P, NG, AH, NS])
        m2 = f.sb("sm_m2", [R, 8, 12])
        pTs, pm = f.sb("sm_pT", [P, QH, R]), f.sb("sm_pm", [P, QH, NS, R])
        misc_ps = f.ps("sm_misc_ps", [P, 512])
        up = [f.ps(f"sm_upd_ps{b}", [P, 512]) for b in range(4)]
        sp3 = f.ps("sm_s_ps", [R, 3, 512])
        ident = misc[:, C_ID:C_ID + P]
        eye8 = misc[:, C_PICK + NS * NS:C_PICK + 2 * NS * NS].rearrange("p (n m) -> p n m", m=NS)
        caches = [k.i["cache_kv_" + n][0] for n in ("w128", "w512", "w2048")]
        qk = zs[:, QB:VB].rearrange("p (h d) -> p h d", d=HD)
        vn = zs[:, VB:GZA].rearrange("p (h d) -> p h d", d=HD)
        s_ps = sp3[:, :, :].rearrange("p b n -> p (b n)").rearrange("p (h c) -> p h c", h=AH)
        with nc.Block() as block:
            @block.sync
            def _(sp):
                sp.dma_start(zs[:, :], k.z[SEQ:ROWS, 0:GZA]).then_inc(s["in"], 16)
                sp.dma_start(w2[:, :], k.i["gla_a_w2"][0]).then_inc(s["in"], 16)
                with nc.allow_non_contiguous_dma(reason="512 single values, once"):
                    sp.dma_start(ab[:, :], k.i["gla_a_b"][0].rearrange("(h p) -> p h", p=P)).then_inc(s["in"], 16)
                sp.dma_start(gn[:, :], k.i["gla_gn_g"].to_broadcast([R, GW])).then_inc(s["in"], 16)
                sp.dma_start(rope[:, :], k.c["rope"][SEQ:ROWS, :]).then_inc(s["in"], 16)
                for n in range(NS):
                    sp.dma_start(S[:, n * GH:(n + 1) * GH, :], k.i["state_gla"][0, n].rearrange("h k v -> k h v")).then_inc(stl[n], 16)
                    for g, (width, dil) in enumerate(GROUPS):
                        src = caches[g][n].rearrange("(j d) a h e -> j d (a h e)", d=dil)[:, 0, :]
                        sp.dma_start(kv[:, n * NG + g, :], src).then_inc(kvl[n], 16)
                sp.wait_ge(s["rope"], 6)
                for g, name in enumerate(("w128", "w512", "w2048")):
                    o = k.o["kv_" + name + "_sample"][0, :, GROUPS[g][0] - 1]
                    sp.dma_start(o[:, 0, :, :], qk[:, QH + g * AH:QH + (g + 1) * AH, :]).then_inc(s["out"], 16)
                    sp.dma_start(o[:, 1, :, :], vn[:, g * AH:(g + 1) * AH, :]).then_inc(s["out"], 16)
                sp.wait_ge(s["mixa"], 1)
                sp.dma_start(k.mix[SEQ:ROWS, 0:GW], om[:, :]).then_inc(s["out"], 16)
                sp.dma_start(k.o["state_sample"][0].rearrange("n h k v -> k (n h) v"), S[:, :, :]).then_inc(s["out"], 16)
                sp.wait_ge(s["mixb"], 1)
                sp.dma_start(k.mix[SEQ:ROWS, GW:GW + AH * HD], ob[:, :]).then_inc(s["out"], 16)
                sp.wait_ge(s["out"], 16 * 9)

            @block.tensor
            def _(pe):
                pe.wait_ge(s["in"], 80)
                nc.tensor.transpose(misc_ps[0:RANK, 0:R], zs[:, ALR:ALR + RANK], ident[0:R, 0:R]).then_inc(s["alr_ps"], 1)
                pe.wait_ge(s["alr"], 1)
                for h in range(GH):
                    last = nc.tensor.matmul(misc_ps[:, h * R:(h + 1) * R], w2[:, h * GK:(h + 1) * GK], alrT[:, :], start=True, stop=True)
                last.then_inc(s["x_ps"], 1)
                pe.wait_ge(s["x"], GH)
                for h in range(GH):
                    last = nc.tensor.transpose(misc_ps[:, h * R:(h + 1) * R], zs[:, QA + h * GK:QA + (h + 1) * GK], ident[0:R, 0:R])
                last.then_inc(s["qT_ps"], 1)
                for n in range(NS):
                    pe.wait_ge(s["ksel"], n + 1)
                    at_least(pe, s["state"], GH * (n - 1))
                    for h in range(GH):
                        last = nc.tensor.matmul(up[2 * (n % 2) + h // 2][:, (h % 2) * GV:(h % 2 + 1) * GV], ksel[:, n % 2, h * GK:(h + 1) * GK],
                                                zs[:, VA + h * GV:VA + (h + 1) * GV], start=True, stop=True)
                    last.then_inc(s["upd"], 1)
                pe.wait_ge(s["state"], GH * NS)
                pe.wait_ge(s["qm"], GH)
                for h in range(GH):
                    for n in range(NS):
                        last = nc.tensor.matmul(up[h // 2][0:R, (h % 2) * GV:(h % 2 + 1) * GV], qm[:, h, n, :], S[:, n * GH + h, :],
                                                start=(n == 0), stop=(n == NS - 1))
                last.then_inc(s["sums"], 1)
                pe.wait_ge(s["rope"], 6)
                pe.wait_ge(s["nsel"], 1)
                for j in range(NS * NG):
                    n, g = j // NG, j % NG
                    at_least(pe, s["prod"], j - 1)
                    nc.tensor.matmul(up[2 + j % 2][:, :], nsel[:, n, :], zs[:, QB + g * AH * HD:QB + (g + 1) * AH * HD], start=True, stop=True).then_inc(s["qbc"], 1)
                pe.wait_ge(s["qk_done"], NS * NG)
                for h in range(AH):
                    for g in range(NG):
                        last = nc.tensor.transpose(s_ps[:, h, g * P:(g + 1) * P], sc[:, g, h, :], ident)
                last.then_inc(s["sT_ps"], 1)
                pe.wait_ge(s["p"], 1)
                for g in range(NG):
                    for h in range(AH):
                        c = g * AH + h
                        last = nc.tensor.transpose(misc_ps[:, c * R:(c + 1) * R], big[:, h * 384 + g * P:h * 384 + (g + 1) * P], ident[0:R, 0:R])
                last.then_inc(s["pT_ps"], 1)
                pe.wait_ge(s["pm"], 1)
                for h in range(AH):
                    for j in range(NS * NG):
                        n, g = j // NG, j % NG
                        last = nc.tensor.matmul(up[2][0:R, h * HD:(h + 1) * HD], pm[:, g * AH + h, n, :], kv[:, j, (AH + h) * HD:(AH + h + 1) * HD],
                                                start=(j == 0), stop=(j == NS * NG - 1))
                last.then_inc(s["pv"], 1)

            @block.scalar
            def _(act):
                act.wait_ge(s["in"], 80)
                nc.scalar.activation(er[:, :], zs[:, RA:RA + GW], ACT.Exp, scale=-1.0).then_inc(s["silu_e"], 1)
                act.wait_ge(s["alr_ps"], 1)
                nc.scalar.copy(alrT[:, :], misc_ps[0:RANK, 0:R]).then_inc(s["alr"], 1)
                act.wait_ge(s["x"], GH)
                link = chained(act, s["ln_steps"])
                link(nc.scalar.activation(xa[:, :, :], x[:, :, :], ACT.Abs))
                link(nc.scalar.activation(xa[:, :, :], xa[:, :, :], ACT.Exp, scale=-1.0))
                nc.scalar.activation(xa[:, :, :], xa[:, :, :], ACT.Ln, bias=1.0).then_inc(s["ln"], 1)
                act.wait_ge(s["la"], 1)
                nc.scalar.activation(EL[:, :, :], x[:, :, :], ACT.Exp, scale=1.0 / TAU).then_inc(s["decay"], 1)
                act.wait_ge(s["sums"], 1)
                for h in range(GH):
                    nc.scalar.activation(xa_row(f, h, om), up[h // 2][0:R, (h % 2) * GV:(h % 2 + 1) * GV], ACT.Square,
                                         accum_out=st[:, 0, h:h + 1]).then_inc(s["sq"], 1)
                    act.wait_ge(s["sq"], h + 1)
                act.wait_ge(s["var"], 1)
                nc.scalar.activation(st[:, 1, :], st[:, 0, :], ACT.Sqrt).then_inc(s["root"], 1)
                act.wait_ge(s["sub"], 2)
                nc.scalar.activation(big[:, 0:1536], big[:, 0:1536], ACT.Exp, scale=SCALE_B).then_inc(s["exp"], 1)
                nc.scalar.activation(m2[:, 1, :], m2[:, 1, :], ACT.Exp, scale=SCALE_B).then_inc(s["exp"], 1)

            @block.vector
            def _(dve):
                link = chained(dve, s["dve"])

                def signal(ins, name, value):
                    ins.then_inc(s[name], 1)
                    dve.wait_ge(s[name], value)
                dve.wait_ge(s["in"], 80)
                cos = rope[:, 0:ROT].unsqueeze(1).to_broadcast([R, 2 * QH, ROT])
                sin = rope[:, ROT:2 * ROT].unsqueeze(1).to_broadcast([R, 2 * QH, ROT])
                rt = big[:, 0:4 * 2 * QH * ROT].rearrange("p (n h r) -> p n h r", n=4, h=2 * QH)
                x1, x2 = qk[:, :, 0:ROT], qk[:, :, ROT:2 * ROT]
                for n, (a, b) in enumerate(((x1, cos), (x2, sin), (x2, cos), (x1, sin))):
                    signal(nc.vector.tensor_tensor(rt[:, n], a, b, ALU.mult), "rope", n + 1)
                signal(nc.vector.tensor_tensor(x1, rt[:, 0], rt[:, 1], ALU.subtract), "rope", 5)
                signal(nc.vector.tensor_tensor(x2, rt[:, 2], rt[:, 3], ALU.add), "rope", 6)
                nc.vector.tensor_copy(nsel[:, :, :], ident[0:R, 0:NS].unsqueeze(2).to_broadcast([R, NS, P])).then_inc(s["nsel"], 1)

                def keys_of(n):
                    nc.vector.tensor_scalar(ksel[:, n % 2, :], zs[:, KA:KA + GH * GK], ident[0:R, n:n + 1], None, ALU.mult).then_inc(s["ksel"], 1)
                keys_of(0)
                keys_of(1)
                dve.wait_ge(s["x_ps"], 1)
                for h in range(GH):
                    signal(nc.vector.tensor_scalar(x[:, h, :], misc_ps[:, h * R:(h + 1) * R], ab[:, h:h + 1], None, ALU.add), "x", h + 1)
                dve.wait_ge(s["ln"], 1)
                nc.vector.scalar_tensor_tensor(out=x[:, :, :], in0=x[:, :, :], scalar=0.0, in1=xa[:, :, :], op0=ALU.min, op1=ALU.subtract).then_inc(s["la"], 1)
                dve.wait_ge(s["qT_ps"], 1)
                link(nc.vector.tensor_scalar(qT[:, :, :].rearrange("p h n -> p (h n)"), misc_ps[:, 0:GH * R], SCALE_A, None, ALU.mult))
                for h in range(GH):
                    nc.vector.tensor_tensor(qm[:, h], qT[:, h, :].unsqueeze(2).to_broadcast([P, NS, R]), eye8, ALU.mult).then_inc(s["qm"], 1)
                dve.wait_ge(s["decay"], 1)
                for n in range(NS):
                    dve.wait_ge(stl[n], 16)
                    dve.wait_ge(s["upd"], n + 1)
                    for h in range(GH):
                        j = n * GH + h
                        nc.vector.scalar_tensor_tensor(out=S[:, j, :], in0=S[:, j, :], scalar=EL[:, h, n:n + 1],
                                                       in1=up[2 * (n % 2) + h // 2][:, (h % 2) * GV:(h % 2 + 1) * GV],
                                                       op0=ALU.mult, op1=ALU.add).then_inc(s["state"], 1)
                    if n + 2 < NS:
                        keys_of(n + 2)
                dve.wait_ge(s["silu_e"], 1)
                link(nc.vector.tensor_scalar_add(er[:, :], er[:, :], 1.0))
                link(nc.vector.reciprocal(er[:, :], er[:, :]))
                link(nc.vector.tensor_tensor(er[:, :], er[:, :], zs[:, RA:RA + GW], ALU.mult))
                link(nc.vector.tensor_tensor(er[:, :], er[:, :], gn[:, :], ALU.mult))
                dve.wait_ge(s["sq"], GH)
                link(nc.vector.tensor_scalar(st[:, 0, :], st[:, 0, :], 1.0 / GV, EPS, ALU.mult, ALU.add))
                signal(nc.vector.reciprocal(st[:, 0, :], st[:, 0, :]), "var", 1)
                dve.wait_ge(s["root"], 1)
                for h in range(GH):
                    cols = slice(h * GV, (h + 1) * GV)
                    ins = nc.vector.scalar_tensor_tensor(out=om[:, cols], in0=up[h // 2][0:R, (h % 2) * GV:(h % 2 + 1) * GV], scalar=st[:, 1, h:h + 1],
                                                         in1=er[:, cols], op0=ALU.mult, op1=ALU.mult)
                    if h < GH - 1:
                        link(ins)
                ins.then_inc(s["mixa"], 1)
                for j in range(NS * NG):
                    n, g = j // NG, j % NG
                    if g == 0:
                        dve.wait_ge(kvl[n], 16 * NG)
                    dve.wait_ge(s["qbc"], j + 1)
                    pr = prod[:, j % 2]
                    nc.vector.tensor_tensor(pr, kv[:, j, 0:AH * HD].rearrange("p (h d) -> p h d", h=AH),
                                            up[2 + j % 2][:, :].rearrange("p (h d) -> p h d", h=AH), ALU.mult).then_inc(s["prod"], 1)
                    dve.wait_ge(s["prod"], j + 1)
                    nc.vector.reduce_sum(sc[:, g, :, n:n + 1], pr, AX.X).then_inc(s["qk_done"], 1)
                pn = kv_free(big)
                link(nc.vector.tensor_tensor(pn, qk[:, 0:QH, :], qk[:, QH:2 * QH, :], ALU.mult))
                link(nc.vector.reduce_sum(m2[:, 0, :].unsqueeze(2), pn, AX.X))
                dve.wait_ge(s["sT_ps"], 1)
                link(nc.vector.reduce_max(m2[:, 2, 0:AH].unsqueeze(2), s_ps, AX.X))
                link(nc.vector.reduce_max(m2[:, 3, 0:AH].unsqueeze(2), m2[:, 0, :].rearrange("p (g h) -> p h g", g=NG), AX.X))
                link(nc.vector.tensor_tensor(m2[:, 2, 0:AH], m2[:, 2, 0:AH], m2[:, 3, 0:AH], ALU.max))
                p = big[:, 0:1536].rearrange("p (h c) -> p h c", h=AH)
                signal(nc.vector.tensor_tensor(p, s_ps, m2[:, 2, 0:AH].unsqueeze(2).to_broadcast([R, AH, 384]), ALU.subtract), "sub", 1)
                gh = lambda a: a.rearrange("p (g h) -> p g h", g=NG)
                signal(nc.vector.tensor_tensor(gh(m2[:, 1, :]), gh(m2[:, 0, :]), m2[:, 2, 0:AH].unsqueeze(1).to_broadcast([R, NG, AH]), ALU.subtract), "sub", 2)
                dve.wait_ge(s["exp"], 2)
                link(nc.vector.reduce_sum(m2[:, 4, 0:AH].unsqueeze(2), p, AX.X))
                link(nc.vector.reduce_sum(m2[:, 5, 0:AH].unsqueeze(2), m2[:, 1, :].rearrange("p (g h) -> p h g", g=NG), AX.X))
                link(nc.vector.tensor_tensor(m2[:, 4, 0:AH], m2[:, 4, 0:AH], m2[:, 5, 0:AH], ALU.add))
                link(nc.vector.reciprocal(m2[:, 6, 0:AH], m2[:, 4, 0:AH]))
                link(nc.vector.tensor_tensor(gh(m2[:, 1, :]), gh(m2[:, 1, :]), m2[:, 6, 0:AH].unsqueeze(1).to_broadcast([R, NG, AH]), ALU.mult))
                signal(nc.vector.tensor_tensor(p, p, m2[:, 6, 0:AH].unsqueeze(2).to_broadcast([R, AH, 384]), ALU.mult), "p", 1)
                dve.wait_ge(s["pT_ps"], 1)
                link(nc.vector.tensor_copy(pTs[:, :, :].rearrange("p c n -> p (c n)"), misc_ps[:, 0:QH * R]))
                nc.vector.tensor_tensor(pm[:, :, :, :], pTs[:, :, :].unsqueeze(3).to_broadcast([P, QH, NS, R]),
                                        eye8.unsqueeze(1).to_broadcast([P, QH, NS, R]), ALU.mult).then_inc(s["pm"], 1)
                link(nc.vector.tensor_tensor(pn, vn, m2[:, 1, :].unsqueeze(2).to_broadcast([R, QH, HD]), ALU.mult))
                link(nc.vector.reduce_sum(ob[:, :].rearrange("p (h d) -> p h d", h=AH).unsqueeze(3), pn.rearrange("p (g h) d -> p h d g", g=NG), AX.X))
                dve.wait_ge(s["pv"], 1)
                nc.vector.tensor_tensor(ob[:, :], ob[:, :], up[2][0:R, :], ALU.add).then_inc(s["mixb"], 1)


def kv_free(big):
    return big[:, 0:QH * HD].rearrange("p (h d) -> p h d", h=QH)


def xa_row(f, h, om):
    return om[:, h * GV:(h + 1) * GV]


class Together:

    def __init__(self, eng, sem):
        self.eng, self.sem, self.count = eng, sem, 0

    def mark(self, ins):
        self.count += 1
        ins.then_inc(self.sem, 1)

    def wait_all(self):
        self.eng.wait_ge(self.sem, self.count)


def merge_and_route(k, misc):
    nc = k.nc
    GW, OB = GH * GV, AH * HD
    KA_, KB_ = GW // P, OB // P
    MW = GW + OB
    names = ("wA", "wB", "wO", "wQ", "k12_l", "k12_ps", "k12_0", "k12", "gain", "m_l", "gz_l", "x_l", "gz_exp", "sig_e", "sig_steps", "mT_ps", "mT", "br", "mg_steps", "merged", "gT_ps", "gT",
             "proj", "x1a", "x1", "sq", "var_steps", "root", "h2_steps", "h2", "hT_ps", "hT", "q_ps", "q", "qT_ps", "qT", "s_ps", "s", "top", "top_start", "top_done", "keys_done", "gsub", "gexp",
             "x1_out", "h2_out", "mod_l")
    s = {n: k.sem("rt_" + n) for n in names}
    with k.phase() as f:
        wA, wB = f.sb("rt_wA", [P, KA_, D]), f.sb("rt_wB", [P, KB_, D])
        wO, wQ = f.sb("rt_wO", [P, KD, D]), f.sb("rt_wQ", [P, KD, PH * DQ])
        k12 = f.sb("rt_k12", [P, 2, NK])
        mods = f.sb("rt_mods", [P, 3, D])
        m, gz, x = f.sb("rt_m", [P, MW]), f.sb("rt_gz", [P, 2 * D]), f.sb("rt_x", [P, D])
        Tm, Tg = f.sb("rt_Tm", [P, 12, P]), f.sb("rt_Tg", [P, KD, P])
        mg, h2, q2 = f.sb("rt_mg", [P, D]), f.sb("rt_h2", [P, D]), f.sb("rt_q2", [P, D])
        sc = f.sb("rt_s", [P, PH, 2, NK])
        g2n = q2
        rs = f.sb("rt_rs", [P, 2])
        work, cand = f.sb("rt_work", [P, PH, 2 * NK]), f.sb("rt_cand", [P, PH, TOPK, TOPK])
        v = f.sb("rt_v", [P, PH, 2, TOPK])
        vi = f.sb("rt_vi", [P, PH, 2, TOPK], U32)
        vif = f.sb("rt_vif", [P, PH, 2, TOPK])
        cs, ci, cj = f.sb("rt_cs", [P, PH, TOPK]), f.sb("rt_ci", [P, PH, TOPK], U32), f.sb("rt_cj", [P, 2, PH, TOPK], U32)
        cf, cg = f.sb("rt_cf", [P, 2, PH, TOPK]), f.sb("rt_cg", [P, PH, TOPK])
        gs = f.sb("rt_gs", [P, 2, PH])
        G = f.ps("rt_G", [P, 4, 512])
        TP = f.ps("rt_TP", [P, 3, 512])
        kps = f.ps("rt_kps", [P, NK])
        cand_flat = cand[:, :, :, :].rearrange("p h a b -> p h (a b)")
        ident = misc[:, C_ID:C_ID + P]
        Gf = G[:, :, :].rearrange("p b n -> p (b n)")
        TPf = TP[:, :, :].rearrange("p b n -> p (b n)").rearrange("p (c t) -> p c t", t=P)

        def all_tiles(eng, tile):
            tile(0, P, P)
            with eng.Fori(1, TILES - 1) as i:
                tile(i, P, P)
            tile(TILES - 1, P, NS)
            tile(TILES, NS, 0)

        with nc.Block() as block:
            @block.sync
            def _(sp):
                sp.dma_start(k12[:, 0, 0:64], k.i["peer_k1"][0]).then_inc(s["k12_l"], 16)
                sp.dma_start(k12[:, 0, 64:128], k.i["peer_k2"][0]).then_inc(s["k12_l"], 16)
                def load_m(rows, R):
                    sp.dma_start(m[0:R, :], k.mix[bass.ds(rows, R), :]).then_inc(s["m_l"], 16)

                def load_gz(rows, R):
                    sp.dma_start(gz[0:R, :], k.z[bass.ds(rows, R), GZA:INW]).then_inc(s["gz_l"], 16)

                def load_x(rows, R):
                    src = k.i["x_sample"][:, 0, :] if R == NS else k.i["x_prompt"][0, bass.ds(rows, R), :]
                    sp.dma_start(x[0:R, :], src).then_inc(s["x_l"], 16)

                def load_w(t, name, sem):
                    sp.dma_start(t[:, :, :], k.i[name][0].rearrange("(k p) n -> p k n", p=P)).then_inc(s[sem], 16)

                load_m(0, P)
                load_w(wA, "w_branch_a", "wA")
                load_gz(0, P)
                load_w(wB, "w_branch_b", "wB")
                load_w(wO, "w_out", "wO")
                load_x(0, P)
                sp.dma_start(mods[:, :, :].rearrange("p a d -> p (a d)"), k.mod[0:1, 2 * D:5 * D].to_broadcast([P, 3 * D])).then_inc(s["mod_l"], 16)
                sp.dma_start(g2n[:, :], k.i["norm2_g"].to_broadcast([P, D])).then_inc(s["mod_l"], 16)
                load_w(wQ, "peer_wq", "wQ")

                def tile(i, R, _):
                    if isinstance(i, int) and i == 0:
                        return
                    rows = early(sp, i * P)
                    one = early(sp, i)
                    sp.wait_ge(s["mT_ps"], one)
                    load_m(rows, R)
                    sp.wait_ge(s["merged"], one)
                    load_gz(rows, R)
                    sp.wait_ge(s["x1"], one)
                    load_x(rows, R)
                all_tiles(sp, tile)
                sp.wait_ge(s["h2"], TILES)
                sp.dma_start(mods[0:NS, :, :].rearrange("p a d -> p (a d)"), k.mod[1:1 + NS, 2 * D:5 * D]).then_inc(s["mod_l"], 16)
                sp.wait_ge(s["qT_ps"], TILES)
                sp.dma_start(g2n[0:NS, :], k.i["norm2_g"].to_broadcast([NS, D])).then_inc(s["mod_l"], 16)

            @block.tensor
            def _(pe):
                pe.wait_ge(s["k12_l"], 32)
                nc.tensor.transpose(kps[:, :], k12[:, 0, :], ident).then_inc(s["k12_ps"], 1)

                def turn(dst, src, n, R, sem):
                    for c in range(n):
                        last = nc.tensor.transpose(dst[:, c, 0:R], src[0:R, c * P:(c + 1) * P], ident[0:R, 0:R])
                    last.then_inc(s[sem], 1)

                def product(bank, T, off, n, w, R):
                    for b in range(2):
                        for c in range(n):
                            last = nc.tensor.matmul(G[0:R, bank + b, :], T[:, off + c, 0:R], w[:, c, b * 512:(b + 1) * 512], start=(c == 0), stop=(c == n - 1))
                    return last

                def loaded(i, name):
                    if isinstance(i, int) and i == 0:
                        pe.wait_ge(s[name], 16)

                def branch_a(i, R):
                    pe.wait_ge(s["mT"], i + 1)
                    loaded(i, "wA")
                    product(2, Tm, 0, KA_, wA, R)

                pe.wait_ge(s["m_l"], 16)
                turn(TPf, m, 12, P, "mT_ps")
                branch_a(0, P)

                def tile(i, R, R_next):
                    at_least(pe, s["s"], 2 * i)
                    loaded(i, "wB")
                    product(0, Tm, KA_, KB_, wB, R).then_inc(s["br"], 1)
                    if R_next:
                        pe.wait_ge(s["m_l"], 16 * i + 32)
                        turn(TPf, m, 12, R_next, "mT_ps")
                        pe.wait_ge(s["mT"], i + 2)
                    pe.wait_ge(s["merged"], i + 1)
                    turn(TPf, mg, KD, R, "gT_ps")
                    pe.wait_ge(s["gT"], i + 1)
                    loaded(i, "wO")
                    product(0, Tg, 0, KD, wO, R).then_inc(s["proj"], 1)
                    if R_next:
                        branch_a(i + 1, R_next)
                    pe.wait_ge(s["h2"], i + 1)
                    turn(TPf, h2, KD, R, "hT_ps")
                    pe.wait_ge(s["hT"], i + 1)
                    loaded(i, "wQ")
                    product(0, Tg, 0, KD, wQ, R).then_inc(s["q_ps"], 1)
                    pe.wait_ge(s["q"], i + 1)
                    turn(TPf, q2, PH, R, "qT_ps")
                    pe.wait_ge(s["qT"], i + 1)
                    if isinstance(i, int) and i == 0:
                        pe.wait_ge(s["k12"], 1)
                    for h in range(PH):
                        bank = G[0:R, h // 2] if h < 4 else TP[0:R, h // 2 - 2]
                        last = nc.tensor.matmul(bank[:, (h % 2) * 256:(h % 2 + 1) * 256], Tg[:, h, 0:R],
                                                k12[:, :, :].rearrange("p a n -> p (a n)"), start=True, stop=True)
                    last.then_inc(s["s_ps"], 1)
                all_tiles(pe, tile)

            @block.scalar
            def _(act):
                def copy_T(T, src, ps_sem, value, n, R, sem):
                    act.wait_ge(s[ps_sem], value)
                    nc.scalar.copy(T[:, 0:n, 0:R], src[:, 0:n, 0:R]).then_inc(s[sem], 1)

                def gate_exp(i, R):
                    act.wait_ge(s["gz_l"], 16 * i + 16)
                    nc.scalar.activation(gz[0:R, :], gz[0:R, :], ACT.Exp, scale=-1.0).then_inc(s["gz_exp"], 1)
                    act.wait_ge(s["gz_exp"], i + 1)
                    nc.scalar.activation(gz[0:R, :], gz[0:R, :], ACT.Copy, bias=1.0).then_inc(s["sig_e"], 1)

                def softmax_exp(i, R):
                    act.wait_ge(s["gsub"], i + 1)
                    nc.scalar.activation(cg[0:R], cg[0:R], ACT.Exp).then_inc(s["gexp"], 1)

                def tile(i, R, R_next):
                    first = isinstance(i, int) and i == 0
                    if first:
                        copy_T(Tm, TPf, "mT_ps", 1, 12, R, "mT")
                        gate_exp(0, R)
                    act.wait_ge(s["br"], i + 1)
                    if R_next:
                        copy_T(Tm, TPf, "mT_ps", i + 2, 12, R_next, "mT")
                    copy_T(Tg, TPf, "gT_ps", i + 1, KD, R, "gT")
                    act.wait_ge(s["x1"], i + 1)
                    act.dma_start(k.x1[bass.ds(i * P, R), :], mg[0:R, :]).then_inc(s["x1_out"], 16)
                    at_least(act, s["h2_out"], 16 * i)
                    at_least(act, s["hT_ps"], i)
                    nc.scalar.activation(h2[0:R, :], mg[0:R, :], ACT.Square, accum_out=rs[0:R, 0:1]).then_inc(s["sq"], 1)
                    act.wait_ge(s["var_steps"], 2 * i + 2)
                    nc.scalar.activation(rs[0:R, 1:2], rs[0:R, 0:1], ACT.Sqrt).then_inc(s["root"], 1)
                    act.wait_ge(s["h2"], i + 1)
                    act.dma_start(k.h2[bass.ds(i * P, R), :], h2[0:R, :]).then_inc(s["h2_out"], 16)
                    copy_T(Tg, TPf, "hT_ps", i + 1, KD, R, "hT")
                    if R_next:
                        gate_exp(i + 1, R_next)
                    act.wait_ge(s["q_ps"], i + 1)
                    if R == NS or first:
                        act.wait_ge(s["gain"], 1 if first else 2)
                    nc.scalar.copy(q2[0:R, :], Gf[0:R, 0:2 * 512]).then_inc(s["q"], 1)
                    copy_T(Tg, TPf, "qT_ps", i + 1, PH, R, "qT")
                    if not first:
                        softmax_exp(i - 1, P)
                    act.wait_ge(s["s_ps"], i + 1)
                    at_least(act, s["keys_done"], i)
                    for half, src in enumerate((G, TP)):
                        nc.scalar.copy(sc[0:R, 4 * half:4 * half + 4].rearrange("p h a n -> p (h a n)"),
                                       src[0:R, 0:2, :].rearrange("p b n -> p (b n)")).then_inc(s["s"], 1)
                all_tiles(act, tile)
                softmax_exp(TILES, NS)
                act.wait_ge(s["x1_out"], 16 * (TILES + 1))
                act.wait_ge(s["h2_out"], 16 * (TILES + 1))

            @block.vector
            def _(dve):
                dve.wait_ge(s["k12_ps"], 1)
                nc.vector.memset(k12[:, :, :], 0.0).then_inc(s["k12_0"], 1)
                dve.wait_ge(s["k12_0"], 1)
                nc.vector.tensor_copy(k12[0:64, 0, :], kps[0:64, :]).then_inc(s["k12_0"], 1)
                dve.wait_ge(s["k12_0"], 2)
                nc.vector.tensor_copy(k12[64:128, 1, :], kps[64:128, :]).then_inc(s["k12"], 1)

                steps = [None]

                def top_keys(i, R):
                    dve.wait_ge(s["s"], 2 * i + 2)
                    dve.sem_inc(s["top_start"], 1)
                    dve.sem_clear(s["top"])
                    steps[0] = Together(dve, s["top"])
                    lists = [(sc[0:R, h, a, :], work[0:R, h, a * NK:(a + 1) * NK], v[0:R, h, a, :], vi[0:R, h, a, :]) for h in range(PH) for a in range(2)]
                    top16(lists)
                    dve.sem_inc(s["keys_done"], 1)
                    steps[0].mark(nc.vector.tensor_copy(vif[0:R].rearrange("p h a n -> p (h a n)"), vi[0:R].rearrange("p h a n -> p (h a n)")))
                    steps[0].wait_all()

                def top16(lists):
                    for vals, _, best, _ in lists:
                        steps[0].mark(nc.vector.max(best[:, 0:8], vals))
                    steps[0].wait_all()
                    for vals, rest, best, place in lists:
                        steps[0].mark(nc.vector.match_replace(rest, best[:, 0:8], vals, MASKED))
                        steps[0].mark(nc.vector.max_index(place[:, 0:8], best[:, 0:8], vals))
                    steps[0].wait_all()
                    for _, rest, best, _ in lists:
                        steps[0].mark(nc.vector.max(best[:, 8:16], rest))
                    steps[0].wait_all()
                    for _, rest, best, place in lists:
                        steps[0].mark(nc.vector.max_index(place[:, 8:16], best[:, 8:16], rest))
                    steps[0].wait_all()

                def top_pairs(R):
                    for h in range(PH):
                        steps[0].mark(nc.vector.tensor_tensor(cand[0:R, h], v[0:R, h, 0, :].unsqueeze(2).to_broadcast([R, TOPK, TOPK]),
                                                              v[0:R, h, 1, :].unsqueeze(1).to_broadcast([R, TOPK, TOPK]), ALU.add))
                    steps[0].wait_all()
                    top16([(cand[0:R, h].rearrange("p a b -> p (a b)"), work[0:R, h, :], cs[0:R, h, :], ci[0:R, h, :]) for h in range(PH)])

                def top_experts(i, R):
                    nc.vector.tensor_tensor(cg[0:R], cs[0:R], cs[0:R, :, 0:1].to_broadcast([R, PH, TOPK]), ALU.subtract).then_inc(s["gsub"], 1)
                    mark, wait_all = steps[0].mark, steps[0].wait_all
                    mark(nc.vector.tensor_single_scalar(cj[0:R, 0], ci[0:R], 4, ALU.logical_shift_right))
                    mark(nc.vector.tensor_single_scalar(cj[0:R, 1], ci[0:R], 15, ALU.bitwise_and))
                    wait_all()
                    mark(nc.vector.tensor_copy(cf[0:R], cj[0:R]))
                    wait_all()
                    slots = misc[0:R, C_SLOT:C_SLOT + TOPK].unsqueeze(1).to_broadcast([R, PH * TOPK, TOPK])
                    hits = [room[0:R].rearrange("p h n -> p (h n)") for room in (work, cand_flat)]
                    for a in range(2):
                        flat = cf[0:R, a].rearrange("p h n -> p (h n)")
                        mark(nc.vector.tensor_tensor(hits[a].rearrange("p (n j) -> p n j", j=TOPK), flat.unsqueeze(2).to_broadcast([R, PH * TOPK, TOPK]), slots, ALU.is_equal))
                    wait_all()
                    for a in range(2):
                        h4 = hits[a].rearrange("p (h n j) -> p h n j", h=PH, j=TOPK)
                        mark(nc.vector.tensor_tensor(h4, h4, vif[0:R, :, a, :].unsqueeze(2).to_broadcast([R, PH, TOPK, TOPK]), ALU.mult))
                    wait_all()
                    for a in range(2):
                        mark(nc.vector.reduce_sum(cf[0:R, a].rearrange("p h n -> p (h n)").unsqueeze(2), hits[a].rearrange("p (n j) -> p n j", j=TOPK), AX.X))
                    wait_all()
                    dst = k.idx_s[0:R, :] if R == NS else k.idx[:, bass.ds(i * P, P)]
                    mark(nc.vector.scalar_tensor_tensor(out=dst, in0=cf[0:R, 0].rearrange("p h n -> p (h n)"), scalar=float(NK),
                                                        in1=cf[0:R, 1].rearrange("p h n -> p (h n)"), op0=ALU.mult, op1=ALU.add))
                    dve.wait_ge(s["gexp"], i + 1)
                    mark(nc.vector.reduce_sum(gs[0:R, 0, :].unsqueeze(2), cg[0:R], AX.X))
                    wait_all()
                    mark(nc.vector.reciprocal(gs[0:R, 1, :], gs[0:R, 0, :]))
                    wait_all()
                    dst = k.gate[:, bass.ds(i * P, P)] if R == P else k.gate_s[0:R, :]
                    nc.vector.tensor_tensor(dst.rearrange("p (h n) -> p h n", h=PH), cg[0:R],
                                            gs[0:R, 1, :].unsqueeze(2).to_broadcast([R, PH, TOPK]), ALU.mult).then_inc(s["top_done"], 1)

                def sigmoids(i, R):
                    dve.wait_ge(s["sig_e"], i + 1)
                    step = chained(dve, s["sig_steps"], i)
                    step(nc.vector.reciprocal(gz[0:R, :], gz[0:R, :]))

                def tile(i, R, R_next):
                    first = isinstance(i, int) and i == 0
                    if first:
                        sigmoids(0, R)
                    dve.wait_ge(s["br"], i + 1)
                    step = chained(dve, s["mg_steps"], 2 * i)
                    step(nc.vector.tensor_tensor(gz[0:R, 0:D], Gf[0:R, 2 * 512:4 * 512], gz[0:R, 0:D], ALU.mult))
                    step(nc.vector.tensor_tensor(gz[0:R, D:2 * D], Gf[0:R, 0:2 * 512], gz[0:R, D:2 * D], ALU.mult))
                    at_least(dve, s["x1_out"], 16 * i)
                    nc.vector.tensor_tensor(mg[0:R, :], gz[0:R, 0:D], gz[0:R, D:2 * D], ALU.add).then_inc(s["merged"], 1)
                    if not first:
                        top_keys(i - 1, P)
                    if R == NS or first:
                        dve.wait_ge(s["mod_l"], 32 if first else 64)
                        nc.vector.scalar_tensor_tensor(out=mods[0:R, 2, :], in0=mods[0:R, 2, :], scalar=1.0, in1=g2n[0:R, :],
                                                       op0=ALU.add, op1=ALU.mult).then_inc(s["gain"], 1)
                        dve.wait_ge(s["gain"], 1 if first else 2)
                    dve.wait_ge(s["proj"], i + 1)
                    dve.wait_ge(s["x_l"], 16 * i + 16)
                    nc.vector.tensor_tensor(mg[0:R, :], Gf[0:R, 0:D], mods[0:R, 0, :], ALU.mult).then_inc(s["x1a"], 1)
                    dve.wait_ge(s["x1a"], i + 1)
                    nc.vector.tensor_tensor(mg[0:R, :], mg[0:R, :], x[0:R, :], ALU.add).then_inc(s["x1"], 1)
                    dve.wait_ge(s["sq"], i + 1)
                    step = chained(dve, s["var_steps"], 2 * i)
                    step(nc.vector.tensor_scalar(rs[0:R, 0:1], rs[0:R, 0:1], 1.0 / D, EPS, ALU.mult, ALU.add))
                    step(nc.vector.reciprocal(rs[0:R, 0:1], rs[0:R, 0:1]))
                    dve.wait_ge(s["root"], i + 1)
                    step = chained(dve, s["h2_steps"], i)
                    step(nc.vector.scalar_tensor_tensor(out=h2[0:R, :], in0=mg[0:R, :], scalar=rs[0:R, 1:2], in1=mods[0:R, 2, :], op0=ALU.mult, op1=ALU.mult))
                    nc.vector.tensor_tensor(h2[0:R, :], h2[0:R, :], mods[0:R, 1, :], ALU.add).then_inc(s["h2"], 1)
                    if not first:
                        top_pairs(P)
                        top_experts(i - 1, P)
                    if R_next:
                        sigmoids(i + 1, R_next)
                all_tiles(dve, tile)
                top_keys(TILES, NS)
                top_pairs(NS)
                top_experts(TILES, NS)


GELU_C = float(np.sqrt(2.0 / np.pi))


def gelu_steps(nc, link, a, t, u):
    link(nc.vector.tensor_tensor(t, a, a, ALU.mult))
    link(nc.vector.tensor_scalar(t, t, 0.044715, 1.0, ALU.mult, ALU.add))
    link(nc.vector.tensor_tensor(u, t, a, ALU.mult))
    return nc.vector.tensor_scalar(u, u, -50.0, None, ALU.max)


def experts(k, misc):
    nc = k.nc
    NSLOT = TOPK
    GRP = 4
    NQ = NSLOT // GRP
    HALF = NSLOT - NS
    names = ("in", "mod", "idxT_ps", "idxT", "bc", "bc_used", "dots", "s_u", "s_exp", "steps", "wm", "s_sum", "s_t", "x1", "sq", "var", "root", "y", "h2_l", "x1_l",
             "staged", "dotted", "g_steps", "g_u", "g_exp", "w", "diag", "vdone", "zero", "tail_t", "t_steps", "y_out", "h2s", "nsel", "tiles_done")
    s = {n: k.sem("ex_" + n) for n in names}
    us = [k.sem(f"ex_u_sample{n}") for n in range(NS)]
    vs = [k.sem(f"ex_v_sample{n}") for n in range(NS)]
    ul = [k.sem(f"ex_u_loaded{q}") for q in range(NQ)]
    vl = [k.sem(f"ex_v_loaded{q}") for q in range(NQ)]
    u_dram, v_dram = k.i["peer_u"], k.i["peer_v"]
    with k.phase() as f:
        U = [f.sb(f"ex_U{n}", [P, D]) for n in range(NSLOT)]
        V = [f.sb(f"ex_V{n}", [P, D]) for n in range(NSLOT)]
        g2m, fg = f.sb("ex_g2", [P, 2, D]), f.sb("ex_fg", [P, D])
        h2, x1, junk, y = f.sb("ex_h2", [P, D]), f.sb("ex_x1", [P, D]), f.sb("ex_junk", [P, D]), f.sb("ex_y", [P, D])
        idx = [f.sb(f"ex_idx{b}", [P, NSLOT], U32) for b in range(2)]
        idxT, gT = f.sb("ex_idxT", [P, NS], U32), f.sb("ex_gT", [P, NS])
        nsel = f.sb("ex_nsel", [NS, NS, P])
        wm = f.sb("ex_wm", [P, NS, NS])
        a, t, uu, w = (f.sb("ex_" + n, [P, NSLOT]) for n in ("a", "t", "u", "w"))
        dg = f.sb("ex_diag", [P, NSLOT, P])
        rs, sq_junk = f.sb("ex_rs", [P, 2]), f.sb("ex_sq_junk", [P, D])
        zb, zr = f.sb("ex_zero", [P, P], BF16), f.sb("ex_zero_row", [P, 512], BF16)
        acc = f.ps("ex_acc", [P, 2, 512])
        bc = [f.ps(f"ex_bc{n}", [P, 2, 512]) for n in range(2)]
        tp = f.ps("ex_tp", [P, 2 * NS])
        ident = misc[:, C_ID:C_ID + P]
        eye8 = misc[:, C_PICK + NS * NS:C_PICK + 2 * NS * NS].rearrange("p (n m) -> p n m", m=NS)
        accf = acc[:, :, :].rearrange("p b n -> p (b n)")
        SL = slice(0, NS)

        p = {n: k.sem("ep_" + n) for n in ("h2_l", "x1_l", "dotted", "g_steps", "g_u", "g_exp", "w", "diag", "vdone", "zero", "acc_t", "x2", "sq", "v_steps", "root", "y",
                                           "y_out", "summed", "staged", "dots_done")}
        with nc.Block() as block:
            @block.sync
            def _(sp):
                sp.dma_start(g2m[:, 0, :], k.mod[0:1, 5 * D:6 * D].to_broadcast([P, D])).then_inc(s["mod"], 16)
                sp.dma_start(g2m[SL, 1, :], k.mod[1:1 + NS, 5 * D:6 * D]).then_inc(s["mod"], 16)
                sp.dma_start(fg[:, :], k.i["final_g"].to_broadcast([P, D])).then_inc(s["mod"], 16)
                sp.dma_start(h2[SL, :], k.h2[SEQ:ROWS, :]).then_inc(s["h2s"], 16)
                sp.dma_start(x1[SL, :], k.x1[SEQ:ROWS, :]).then_inc(s["mod"], 16)

                def tile(i):
                    first = isinstance(i, int) and i == 0
                    rows, last_dot, t1 = early(sp, i * P), early(sp, i * (PH * NSLOT)), early(sp, i)
                    if first:
                        sp.wait_ge(s["bc"], NS)
                    at_least(sp, p["dots_done"], last_dot)
                    sp.dma_start(h2[:, :], k.h2[bass.ds(rows, P), :]).then_inc(p["h2_l"], 16)
                    if first:
                        sp.wait_ge(s["x1"], 1)
                    at_least(sp, p["x2"], t1)
                    sp.dma_start(x1[:, :], k.x1[bass.ds(rows, P), :]).then_inc(p["x1_l"], 16)
                    if first:
                        sp.wait_ge(s["y"], 1)
                        sp.dma_start(k.o["y_sample"][:, 0, :], y[SL, :]).then_inc(s["y_out"], 16)
                first_then_loop(sp, TILES, tile)
                sp.wait_ge(s["y_out"], 16)

            @block.gpsimd
            def _(pool):
                pool.wait_ge(s["idxT"], 1)
                for n in range(NS):
                    pool.indirect_dma_start(out=U[HALF + n][:, :], out_offset=None, in_=u_dram, in_offset=bass.IndirectOffsetOnAxis(ap=idxT[:, n:n + 1], axis=0)).then_inc(us[n], 16)
                    pool.indirect_dma_start(out=V[HALF + n][:, :], out_offset=None, in_=v_dram, in_offset=bass.IndirectOffsetOnAxis(ap=idxT[:, n:n + 1], axis=0)).then_inc(vs[n], 16)

                def head(i, pair, b):
                    h = pair * 2 + b
                    nc.gpsimd.tensor_copy(idx[b][:, :], k.idx[:, bass.ds(i * P + h * NSLOT, NSLOT)]).then_inc(p["staged"], 1)
                    pool.wait_ge(p["staged"], i * PH + h + 1)
                    for table, buf, used, loaded in ((u_dram, U, "dotted", ul), (v_dram, V, "vdone", vl)):
                        for n in range(NSLOT):
                            if n % GRP == 0:
                                pool.wait_ge(p[used], (i * PH + h) * NSLOT + n + GRP)
                                pool.sem_inc(p["zero"], 1)
                            pool.indirect_dma_start(out=buf[n][:, :], out_offset=None, in_=table,
                                                    in_offset=bass.IndirectOffsetOnAxis(ap=idx[b][:, n:n + 1], axis=0)).then_inc(loaded[n // GRP], 16)

                with pool.Fori(0, TILES) as i:
                    with pool.Fori(0, PH // 2) as pair:
                        for b in range(2):
                            head(i, pair, b)

            @block.tensor
            def _(pe):
                pe.sem_inc(p["vdone"], HALF)
                nc.tensor.transpose(tp[:, 0:NS], k.idx_s[:, :], ident[SL, SL])
                nc.tensor.transpose(tp[:, NS:2 * NS], k.gate_s[:, :], ident[SL, SL]).then_inc(s["idxT_ps"], 1)
                pe.wait_ge(s["h2s"], 16)
                pe.wait_ge(s["nsel"], 1)
                for n in range(NS):
                    at_least(pe, s["dots"], n - 1)
                    for b in range(2):
                        last = nc.tensor.matmul(bc[n % 2][:, b, :], nsel[:, n, :], h2[SL, b * 512:(b + 1) * 512], start=True, stop=True)
                    last.then_inc(s["bc"], 1)
                pe.wait_ge(s["wm"], 1)
                for n in range(NS):
                    pe.wait_ge(vs[n], 16)
                for b in range(2):
                    for n in range(NS):
                        last = nc.tensor.matmul(acc[SL, b, :], wm[:, n, :], V[HALF + n][:, b * 512:(b + 1) * 512], start=(n == 0), stop=(n == NS - 1))
                last.then_inc(s["s_sum"], 1)

                pe.wait_ge(s["s_sum"], 1)
                pe.sem_inc(p["vdone"], NSLOT - HALF)
                pe.wait_ge(s["tiles_done"], 2)
                with pe.Fori(0, TILES) as i:
                    pe.wait_ge(p["acc_t"], i + 1)
                    for b in range(2):
                        nc.tensor.matmul(acc[:, b, :], zb[:, :], zr[:, :], start=True, stop=False)
                    with pe.Fori(0, PH) as h:
                        for n in range(NSLOT):
                            if n % GRP == 0:
                                pe.wait_ge(vl[n // GRP], (i * PH + h) * (16 * GRP) + 16 * GRP)
                            pe.wait_ge(p["diag"], (i * PH + h) * NSLOT + n + 1)
                            for b in range(2):
                                last = nc.tensor.matmul(acc[:, b, :], dg[:, n, :], V[n][:, b * 512:(b + 1) * 512], start=False, stop=False)
                            last.then_inc(p["vdone"], 1)
                    for b in range(2):
                        last = nc.tensor.matmul(acc[:, b, :], zb[:, :], zr[:, :], start=False, stop=True)
                    last.then_inc(p["summed"], 1)

            @block.scalar
            def _(act):
                act.wait_ge(s["s_u"], 1)
                nc.scalar.activation(uu[:, SL], uu[:, SL], ACT.Exp, scale=-2 * GELU_C).then_inc(s["s_exp"], 1)
                act.wait_ge(s["x1"], 1)
                nc.scalar.activation(junk[SL, :], y[SL, :], ACT.Square, accum_out=rs[SL, 0:1]).then_inc(s["sq"], 1)
                act.wait_ge(s["var"], 1)
                nc.scalar.activation(rs[SL, 1:2], rs[SL, 0:1], ACT.Sqrt).then_inc(s["root"], 1)

                def head(i, h):
                    act.wait_ge(p["g_u"], i * PH + h + 1)
                    nc.scalar.activation(uu[:, :], uu[:, :], ACT.Exp, scale=-2 * GELU_C).then_inc(p["g_exp"], 1)
                    act.wait_ge(p["w"], i * PH + h + 1)
                    for n in range(NSLOT):
                        act.wait_ge(p["vdone"], (i * PH + h) * NSLOT + n + 1)
                        nc.scalar.activation(dg[:, n, :], ident, ACT.Copy, scale=w[:, n:n + 1]).then_inc(p["diag"], 1)

                def tail(i):
                    act.wait_ge(p["x2"], i + 1)
                    nc.scalar.activation(sq_junk[:, :], y[:, :], ACT.Square, accum_out=rs[:, 0:1]).then_inc(p["sq"], 1)
                    act.wait_ge(p["v_steps"], 2 * i + 2)
                    nc.scalar.activation(rs[:, 1:2], rs[:, 0:1], ACT.Sqrt).then_inc(p["root"], 1)
                    act.wait_ge(p["y"], i + 1)
                    act.dma_start(k.o["y_prompt"][0, bass.ds(i * P, P), :], y[:, :]).then_inc(p["y_out"], 16)

                def tile(i):
                    head(i, 0)
                    if not (isinstance(i, int) and i == 0):
                        tail(i - 1)
                    with act.Fori(1, PH) as h:
                        head(i, h)
                first_then_loop(act, TILES, tile)
                tail(TILES - 1)
                act.wait_ge(p["y_out"], 16 * TILES)

            @block.vector
            def _(dve):
                dve.sem_inc(p["dotted"], HALF)
                nc.vector.memset(zb[:, :], 0.0).then_inc(s["tiles_done"], 1)
                nc.vector.memset(zr[:, :], 0.0).then_inc(s["tiles_done"], 1)
                link = chained(dve, s["steps"])
                nc.vector.tensor_copy(nsel[:, :, :], ident[SL, SL].unsqueeze(2).to_broadcast([NS, NS, P])).then_inc(s["nsel"], 1)
                dve.wait_ge(s["idxT_ps"], 1)
                link(nc.vector.tensor_copy(gT[:, :], tp[:, NS:2 * NS]))
                nc.vector.tensor_copy(idxT[:, :], tp[:, 0:NS]).then_inc(s["idxT"], 1)
                for n in range(NS):
                    dve.wait_ge(s["bc"], n + 1)
                    dve.wait_ge(us[n], 16)
                    nc.vector.tensor_tensor_reduce(out=U[HALF + n][:, :], in0=U[HALF + n][:, :], in1=bc[n % 2][:, :, :].rearrange("p b n -> p (b n)"), scale=1.0, scalar=0.0,
                                                   op0=ALU.mult, op1=ALU.add, accum_out=a[:, n:n + 1]).then_inc(s["dots"], 1)
                dve.wait_ge(s["dots"], NS)
                dve.sem_inc(p["dotted"], NSLOT - HALF)
                gelu_steps(nc, link, a[:, SL], t[:, SL], uu[:, SL]).then_inc(s["s_u"], 1)
                dve.wait_ge(s["s_exp"], 1)
                link(nc.vector.tensor_scalar_add(uu[:, SL], uu[:, SL], 1.0))
                link(nc.vector.reciprocal(t[:, SL], uu[:, SL]))
                link(nc.vector.tensor_tensor(t[:, SL], t[:, SL], a[:, SL], ALU.mult))
                link(nc.vector.tensor_tensor(t[:, SL], t[:, SL], gT[:, :], ALU.mult))
                nc.vector.tensor_tensor(wm[:, :, :], t[:, SL].unsqueeze(2).to_broadcast([P, NS, NS]), eye8, ALU.mult).then_inc(s["wm"], 1)
                dve.wait_ge(s["mod"], 64)
                dve.wait_ge(s["s_sum"], 1)
                link(nc.vector.tensor_tensor(y[SL, :], accf[SL, :], g2m[SL, 1, :], ALU.mult))
                nc.vector.tensor_tensor(y[SL, :], y[SL, :], x1[SL, :], ALU.add).then_inc(s["x1"], 1)
                dve.wait_ge(s["sq"], 1)
                link(nc.vector.tensor_scalar(rs[SL, 0:1], rs[SL, 0:1], 1.0 / D, EPS, ALU.mult, ALU.add))
                nc.vector.reciprocal(rs[SL, 0:1], rs[SL, 0:1]).then_inc(s["var"], 1)
                dve.wait_ge(s["root"], 1)
                nc.vector.scalar_tensor_tensor(out=y[SL, :], in0=y[SL, :], scalar=rs[SL, 1:2], in1=fg[SL, :], op0=ALU.mult, op1=ALU.mult).then_inc(s["y"], 1)

                dve.sem_inc(p["acc_t"], 1)

                def head(i, h):
                    for n in range(NSLOT):
                        if n % GRP == 0:
                            dve.wait_ge(ul[n // GRP], (i * PH + h) * (16 * GRP) + 16 * GRP)
                        nc.vector.tensor_tensor_reduce(out=U[n][:, :], in0=U[n][:, :], in1=h2[:, :], scale=1.0, scalar=0.0, op0=ALU.mult, op1=ALU.add,
                                                       accum_out=a[:, n:n + 1]).then_inc(p["dotted"], 1)
                    dve.wait_ge(p["dotted"], (i * PH + h) * NSLOT + 2 * NSLOT)
                    dve.sem_inc(p["dots_done"], NSLOT)
                    link = chained(dve, p["g_steps"], (i * PH + h) * 6)
                    gelu_steps(nc, link, a[:, :], t[:, :], uu[:, :]).then_inc(p["g_u"], 1)
                    dve.wait_ge(p["g_exp"], i * PH + h + 1)
                    link(nc.vector.tensor_scalar_add(uu[:, :], uu[:, :], 1.0))
                    link(nc.vector.reciprocal(t[:, :], uu[:, :]))
                    link(nc.vector.tensor_tensor(t[:, :], t[:, :], a[:, :], ALU.mult))
                    gate = k.gate[:, bass.ds(i * P + h * NSLOT, NSLOT)]
                    at_least(dve, p["diag"], (i * PH + h) * NSLOT)
                    nc.vector.tensor_tensor(w[:, :], t[:, :], gate, ALU.mult).then_inc(p["w"], 1)

                def tail(i):
                    dve.wait_ge(p["summed"], i + 1)
                    dve.wait_ge(p["x1_l"], 16 * i + 16)
                    if isinstance(i, int) and i == 0:
                        dve.wait_ge(s["y_out"], 16)
                    at_least(dve, p["y_out"], 16 * i)
                    nc.vector.tensor_tensor(y[:, :], accf, g2m[:, 0, :], ALU.mult).then_inc(p["acc_t"], 1)
                    dve.wait_ge(p["acc_t"], i + 2)
                    nc.vector.tensor_tensor(y[:, :], y[:, :], x1[:, :], ALU.add).then_inc(p["x2"], 1)
                    dve.wait_ge(p["sq"], i + 1)
                    link = chained(dve, p["v_steps"], 2 * i)
                    link(nc.vector.tensor_scalar(rs[:, 0:1], rs[:, 0:1], 1.0 / D, EPS, ALU.mult, ALU.add))
                    link(nc.vector.reciprocal(rs[:, 0:1], rs[:, 0:1]))
                    dve.wait_ge(p["root"], i + 1)
                    nc.vector.scalar_tensor_tensor(out=y[:, :], in0=y[:, :], scalar=rs[:, 1:2], in1=fg[:, :], op0=ALU.mult, op1=ALU.mult).then_inc(p["y"], 1)

                def tile(i):
                    dve.wait_ge(p["h2_l"], 16 * i + 16)
                    head(i, 0)
                    if not (isinstance(i, int) and i == 0):
                        tail(i - 1)
                    with dve.Fori(1, PH) as h:
                        head(i, h)
                first_then_loop(dve, TILES, tile)
                tail(TILES - 1)


def program(nc, ins, outs):
    with ExitStack() as stack:
        k = Ctx(nc, stack, ins, outs, {n: nc.inline_tensor(a, "table_" + n).ap() for n, a in constants().items()})
        misc = stack.enter_context(nc.sbuf_tensor("misc", [P, C_W], F32))
        with k.phase() as f:
            k.x_rows = f.sb("x_rows", [P, TILES + 1, D])
            k.win = [f.sb(f"win{u}", [P, KD, WIN]) for u in range(WIN_BUFS)]
            modulation(k, misc)
            norm_and_project(k, misc)
        k.clear_sems()
        prompt_mixers(k, misc)
        k.clear_sems()
        sample_mixers(k, misc)
        k.clear_sems()
        k.idx = stack.enter_context(nc.sbuf_tensor("expert_idx", [P, SEQ], U32))
        k.gate = stack.enter_context(nc.sbuf_tensor("expert_gate", [P, SEQ], F32))
        k.idx_s = stack.enter_context(nc.sbuf_tensor("expert_idx_sample", [NS, P], F32))
        k.gate_s = stack.enter_context(nc.sbuf_tensor("expert_gate_sample", [NS, P], F32))
        merge_and_route(k, misc)
        k.clear_sems()
        experts(k, misc)
        k.clear_sems()
        with nc.Block() as block:
            @block.sync
            def _(sp):
                sp.wait_ge(k.cachecopy, 16 * NS * NG)


INS = ['x_prompt', 'x_sample', 'c_prompt', 'c_sample', 'state_gla', 'cache_kv_w128', 'cache_kv_w512', 'cache_kv_w2048',
       'ada_w', 'ada_b', 'norm1_g', 'w_in', 'gla_a_w2', 'gla_a_b', 'gla_gn_g', 'w_branch_a', 'w_branch_b', 'w_out',
       'norm2_g', 'peer_wq', 'peer_k1', 'peer_k2', 'peer_u', 'peer_v', 'final_g']
OUTS = [("y_prompt", (1, SEQ, D)), ("y_sample", (NS, 1, D)), ("state_prompt", (1, 1, GH, GK, GV)), ("state_sample", (1, NS, GH, GK, GV)),
        ("kv_w128_prompt", (1, 1, 128, 2, AH, HD)), ("kv_w128_sample", (1, NS, 128, 2, AH, HD)),
        ("kv_w512_prompt", (1, 1, 512, 2, AH, HD)), ("kv_w512_sample", (1, NS, 512, 2, AH, HD)),
        ("kv_w2048_prompt", (1, 1, SEQ, 2, AH, HD)), ("kv_w2048_sample", (1, NS, 2048, 2, AH, HD))]


def kernel(**inputs):
    import concourse.bacc as bacc
    from concourse.bass_utils import run_bass_kernel_spmd as run

    nc = bacc.Bacc("TRN2", target_bir_lowering=False, num_devices=1)
    arrays, ins, outs = {}, {}, {}
    for name in INS:
        a = np.ascontiguousarray(inputs[name])
        if name in ("peer_u", "peer_v"):
            a = a[0]
        if name == "final_g":
            a = a[None, :]
        arrays["in_" + name] = a
        ins[name] = nc.dram_tensor("in_" + name, a.shape, mybir.dt.from_np(a.dtype), kind="ExternalInput").ap()
    for name, shape in OUTS:
        outs[name] = nc.dram_tensor("out_" + name, shape, F32, kind="ExternalOutput").ap()
    program(nc, ins, outs)
    r = run(nc, [arrays], core_ids=[0])
    return tuple(r.results[0]["out_" + name] for name, _ in OUTS)
```
